# Optimizing a Trainium2 kernel written in Bass

```python
import numpy as np
import jax
import jax.numpy as jnp
from jax import lax
import math
import jax, jax.numpy as jnp

D_MODEL = 1024
BATCH = 1
SEQ = 512
DEPTH = 1

HEAD_DIM = 64
NSA_HEADS = D_MODEL // (2 * HEAD_DIM)
NSA_KV_GROUPS = max(1, NSA_HEADS // 4)
NSA_HPG = NSA_HEADS // NSA_KV_GROUPS
NSA_CMP_LEN = 32
NSA_CMP_STRIDE = 16
NSA_CMP_HID = 128
NSA_SEL_BLOCK = 64
NSA_SEL_TOP = 16
NSA_WINDOW = 512
NSA_Q_CHUNK = 64
MOBA_HEADS = D_MODEL // (2 * HEAD_DIM)
MOBA_BLOCK = 256
MOBA_TOP = 3
MOBA_Q_CHUNK = 32
N_EXPERTS = 32
TOP_K = 4
D_FF = 1024
SWIGLU_LIMIT = 7.0
SWIGLU_ALPHA = 1.702
MOE_BLOCK = 128
EPS = 1e-6
NEG = -1e30
FORCE_SCORE = 1e4

NSA_W = NSA_HEADS * HEAD_DIM
NSA_KV_W = NSA_KV_GROUPS * HEAD_DIM
MOBA_W = MOBA_HEADS * HEAD_DIM
MIX_W = NSA_W + MOBA_W
IN_WIDTHS = (NSA_W, NSA_KV_W, NSA_KV_W, NSA_KV_W, NSA_KV_W, NSA_KV_W, NSA_KV_W,
             3 * NSA_HEADS, MOBA_W, MOBA_W, MOBA_W)
IN_W = sum(IN_WIDTHS)


def rms_norm(x, g):
    xf = x.astype(jnp.float32)
    y = xf * lax.rsqrt(jnp.mean(xf * xf, axis=-1, keepdims=True) + EPS)
    return (y * g.astype(jnp.float32)).astype(x.dtype)

def alibi_slopes(n):
    return jnp.asarray(2.0 ** (-8.0 * np.arange(1, n + 1) / n), dtype=jnp.float32)

def masked_softmax(s, mask):
    s = jnp.where(mask, s.astype(jnp.float32), NEG)
    p = jax.nn.softmax(s, axis=-1)
    return jnp.where(mask, p, 0.0)

def _heads(t, n_heads):
    b, s, _ = t.shape
    return t.reshape(b, s, n_heads, HEAD_DIM).transpose(0, 2, 1, 3)

_gather_blocks = jax.vmap(jax.vmap(lambda blocks, idx: blocks[idx]))

def _compress(kv, pos, w1, w2):
    s = kv.shape[2]
    n_cmp = (s - NSA_CMP_LEN) // NSA_CMP_STRIDE + 1
    idx = NSA_CMP_STRIDE * np.arange(n_cmp)[:, None] + np.arange(NSA_CMP_LEN)[None, :]
    blocks = kv[:, :, idx] + pos
    flat = blocks.reshape(kv.shape[0], kv.shape[1], n_cmp, NSA_CMP_LEN * HEAD_DIM)
    return jax.nn.gelu(flat @ w1) @ w2

def nsa_mixer(q, k_cmp, v_cmp, k_slc, v_slc, k_win, v_win, gates, k_gain, cmp_pos, cmp_w1, cmp_w2):
    B, G, Hg, S, dh = q.shape
    scale = dh ** -0.5
    sl = alibi_slopes(G * Hg).reshape(1, G, Hg, 1, 1)
    kc = rms_norm(_compress(k_cmp, cmp_pos[0], cmp_w1[0], cmp_w2[0]), k_gain)
    vc = _compress(v_cmp, cmp_pos[1], cmp_w1[1], cmp_w2[1])
    n_cmp = kc.shape[2]
    cmp_start = NSA_CMP_STRIDE * np.arange(n_cmp)
    cmp_end = jnp.asarray(cmp_start + NSA_CMP_LEN - 1, dtype=jnp.int32)
    cmp_center = jnp.asarray(cmp_start + 0.5 * (NSA_CMP_LEN - 1), dtype=jnp.float32)
    n_sel = S // NSA_SEL_BLOCK
    sel_start = NSA_SEL_BLOCK * np.arange(n_sel)
    incid = jnp.asarray((cmp_start[:, None] <= sel_start[None, :] + NSA_SEL_BLOCK - 1)
                        & (cmp_start[:, None] + NSA_CMP_LEN - 1 >= sel_start[None, :]), dtype=jnp.float32)
    n_top = min(NSA_SEL_TOP, n_sel)
    ks = rms_norm(k_slc, k_gain).reshape(B, G, n_sel, NSA_SEL_BLOCK, dh)
    vs = v_slc.reshape(B, G, n_sel, NSA_SEL_BLOCK, dh)
    pad = ((0, 0), (0, 0), (NSA_WINDOW, 0), (0, 0))
    kw = jnp.pad(rms_norm(k_win, k_gain), pad)
    vw = jnp.pad(v_win, pad)
    blk_ids = jnp.arange(n_sel)[None, :]
    in_blk = jnp.arange(NSA_SEL_BLOCK)
    win_off = jnp.arange(NSA_WINDOW + NSA_Q_CHUNK)
    C = NSA_Q_CHUNK
    m_sel = n_top * NSA_SEL_BLOCK

    def chunk(q0):
        qc = lax.dynamic_slice_in_dim(q, q0, C, axis=3)
        gc = lax.dynamic_slice_in_dim(gates, q0, C, axis=3)
        t = q0 + jnp.arange(C)
        tf = t.astype(jnp.float32)
        s = jnp.einsum('bghcd,bgnd->bghcn', qc, kc, preferred_element_type=jnp.float32) * scale
        s = s - sl * (tf[:, None] - cmp_center[None, :])
        p_cmp = masked_softmax(s, cmp_end[None, :] <= t[:, None])
        o_cmp = jnp.einsum('bghcn,bgnd->bghcd', p_cmp.astype(vc.dtype), vc)
        imp = jnp.einsum('bghcn,nj->bgcj', p_cmp, incid)
        cur = (t // NSA_SEL_BLOCK)[:, None]
        forced = (blk_ids == 0) | (blk_ids == cur) | (blk_ids == cur - 1)
        imp = jnp.where(forced, FORCE_SCORE, imp)
        imp = jnp.where(blk_ids <= cur, imp, NEG)
        _, sel = lax.top_k(imp, n_top)
        ksel = _gather_blocks(ks, sel).reshape(B, G, C, m_sel, dh)
        vsel = _gather_blocks(vs, sel).reshape(B, G, C, m_sel, dh)
        pos = (sel[..., None] * NSA_SEL_BLOCK + in_blk).reshape(B, G, C, m_sel)
        dist = (t[None, None, :, None] - pos)[:, :, None]
        s = jnp.einsum('bghcd,bgcmd->bghcm', qc, ksel, preferred_element_type=jnp.float32) * scale
        s = s - sl * dist.astype(jnp.float32)
        p = masked_softmax(s, dist >= 0)
        o_sel = jnp.einsum('bghcm,bgcmd->bghcd', p.astype(vsel.dtype), vsel)
        kwc = lax.dynamic_slice_in_dim(kw, q0, NSA_WINDOW + C, axis=2)
        vwc = lax.dynamic_slice_in_dim(vw, q0, NSA_WINDOW + C, axis=2)
        pos_w = q0 - NSA_WINDOW + win_off
        dist_w = t[:, None] - pos_w[None, :]
        mask_w = (dist_w >= 0) & (dist_w < NSA_WINDOW) & (pos_w >= 0)[None, :]
        s = jnp.einsum('bghcd,bgkd->bghck', qc, kwc, preferred_element_type=jnp.float32) * scale
        s = s - sl * dist_w.astype(jnp.float32)
        p = masked_softmax(s, mask_w)
        o_win = jnp.einsum('bghck,bgkd->bghcd', p.astype(vwc.dtype), vwc)
        return gc[..., 0:1] * o_cmp + gc[..., 1:2] * o_sel + gc[..., 2:3] * o_win

    out = lax.map(chunk, jnp.arange(0, S, C))
    return out.transpose(1, 0, 4, 2, 3, 5).reshape(B, S, G * Hg * dh)

def moba_mixer(q, k, v):
    B, H, S, dh = q.shape
    scale = dh ** -0.5
    sl = alibi_slopes(H).reshape(1, H, 1, 1)
    n_blk = -(-S // MOBA_BLOCK)
    pad = ((0, 0), (0, 0), (0, n_blk * MOBA_BLOCK - S), (0, 0))
    kp = jnp.pad(k, pad)
    vp = jnp.pad(v, pad)
    kb = kp.reshape(B, H, n_blk, MOBA_BLOCK, dh)
    vb = vp.reshape(B, H, n_blk, MOBA_BLOCK, dh)
    kmean = jnp.mean(kb.astype(jnp.float32), axis=3)
    n_top = min(MOBA_TOP, n_blk - 1)
    in_blk = jnp.arange(MOBA_BLOCK)
    blk_ids = jnp.arange(n_blk)
    C = MOBA_Q_CHUNK
    m_g = n_top * MOBA_BLOCK

    def chunk(q0):
        qc = lax.dynamic_slice_in_dim(q, q0, C, axis=2)
        t = q0 + jnp.arange(C)
        cb = q0 // MOBA_BLOCK
        kcur = lax.dynamic_slice_in_dim(kp, cb * MOBA_BLOCK, MOBA_BLOCK, axis=2)
        vcur = lax.dynamic_slice_in_dim(vp, cb * MOBA_BLOCK, MOBA_BLOCK, axis=2)
        dist_c = t[:, None] - (cb * MOBA_BLOCK + in_blk)[None, :]
        s_c = jnp.einsum('bhcd,bhkd->bhck', qc, kcur, preferred_element_type=jnp.float32) * scale
        s_c = s_c - sl * dist_c.astype(jnp.float32)
        mask_c = jnp.broadcast_to(dist_c >= 0, s_c.shape)
        if n_top > 0:
            gate = jnp.einsum('bhcd,bhnd->bhcn', qc, kmean, preferred_element_type=jnp.float32)
            gate = jnp.where(blk_ids < cb, gate, NEG)
            _, sel = lax.top_k(gate, n_top)
            kg = _gather_blocks(kb, sel).reshape(B, H, C, m_g, dh)
            vg = _gather_blocks(vb, sel).reshape(B, H, C, m_g, dh)
            pos_g = (sel[..., None] * MOBA_BLOCK + in_blk).reshape(B, H, C, m_g)
            dist_g = t[None, None, :, None] - pos_g
            s_g = jnp.einsum('bhcd,bhcmd->bhcm', qc, kg, preferred_element_type=jnp.float32) * scale
            s_g = s_g - sl * dist_g.astype(jnp.float32)
            mask_g = jnp.repeat(sel < cb, MOBA_BLOCK, axis=-1)
            p = masked_softmax(jnp.concatenate([s_g, s_c], axis=-1),
                               jnp.concatenate([mask_g, mask_c], axis=-1))
            o = (jnp.einsum('bhcm,bhcmd->bhcd', p[..., :m_g].astype(vg.dtype), vg)
                 + jnp.einsum('bhck,bhkd->bhcd', p[..., m_g:].astype(vcur.dtype), vcur))
        else:
            p = masked_softmax(s_c, mask_c)
            o = jnp.einsum('bhck,bhkd->bhcd', p.astype(vcur.dtype), vcur)
        return o

    out = lax.map(chunk, jnp.arange(0, S, C))
    return out.transpose(1, 0, 3, 2, 4).reshape(B, S, H * dh)

def hybrid_mixer(h, w_in, w_out, nsa_q_gain, nsa_k_gain, cmp_pos, cmp_w1, cmp_w2, moba_q_gain, moba_k_gain):
    B, S, _ = h.shape
    z = h @ w_in
    points = [int(v) for v in np.cumsum(IN_WIDTHS)[:-1]]
    q_n, kc, vc, ks, vs, kw, vw, g_n, q_m, k_m, v_m = jnp.split(z, points, axis=-1)
    qn = rms_norm(_heads(q_n, NSA_HEADS), nsa_q_gain).reshape(B, NSA_KV_GROUPS, NSA_HPG, S, HEAD_DIM)
    gates = jax.nn.sigmoid(g_n.reshape(B, S, NSA_KV_GROUPS, NSA_HPG, 3)).transpose(0, 2, 3, 1, 4)
    o_nsa = nsa_mixer(qn, _heads(kc, NSA_KV_GROUPS), _heads(vc, NSA_KV_GROUPS),
                      _heads(ks, NSA_KV_GROUPS), _heads(vs, NSA_KV_GROUPS),
                      _heads(kw, NSA_KV_GROUPS), _heads(vw, NSA_KV_GROUPS),
                      gates, nsa_k_gain, cmp_pos, cmp_w1, cmp_w2)
    o_moba = moba_mixer(rms_norm(_heads(q_m, MOBA_HEADS), moba_q_gain),
                        rms_norm(_heads(k_m, MOBA_HEADS), moba_k_gain),
                        _heads(v_m, MOBA_HEADS))
    return jnp.concatenate([o_nsa, o_moba], axis=-1) @ w_out

def sparse_moe(h, router_w, router_b, w1, b1, w2, b2):
    B, S, D = h.shape
    T = B * S
    hf = h.reshape(T, D)
    logits = (hf @ router_w + router_b).astype(jnp.float32)
    top_val, top_idx = lax.top_k(logits, TOP_K)
    gate = jax.nn.softmax(top_val, axis=-1)
    A = T * TOP_K
    e_flat = top_idx.reshape(A)
    tok_flat = jnp.arange(A, dtype=jnp.int32) // TOP_K
    w_flat = gate.reshape(A).astype(h.dtype)
    order = jnp.argsort(e_flat)
    e_s, tok_s, w_s = e_flat[order], tok_flat[order], w_flat[order]
    counts = jnp.bincount(e_flat, length=N_EXPERTS)
    padded = (counts + MOE_BLOCK - 1) // MOE_BLOCK * MOE_BLOCK
    start = jnp.cumsum(counts) - counts
    pend = jnp.cumsum(padded)
    pstart = pend - padded
    dest = pstart[e_s] + jnp.arange(A) - start[e_s]
    R = A + N_EXPERTS * MOE_BLOCK
    n_blocks = R // MOE_BLOCK
    row_tok = jnp.zeros((R,), jnp.int32).at[dest].set(tok_s)
    row_w = jnp.zeros((R,), h.dtype).at[dest].set(w_s)
    blk_e = jnp.minimum(jnp.searchsorted(pend, jnp.arange(n_blocks) * MOE_BLOCK, side='right'), N_EXPERTS - 1)

    def expert_block(args):
        e, toks, wts = args
        u = hf[toks] @ w1[e] + b1[e]
        g_, lin = u[:, :D_FF], u[:, D_FF:]
        g_ = jnp.minimum(g_, SWIGLU_LIMIT)
        lin = jnp.clip(lin, -SWIGLU_LIMIT, SWIGLU_LIMIT)
        y = ((lin + 1.0) * g_ * jax.nn.sigmoid(SWIGLU_ALPHA * g_)) @ w2[e] + b2[e]
        return y * wts[:, None]

    y = lax.map(expert_block, (blk_e, row_tok.reshape(n_blocks, MOE_BLOCK), row_w.reshape(n_blocks, MOE_BLOCK)))
    out = jax.ops.segment_sum(y.reshape(R, D), row_tok, num_segments=T)
    return out.reshape(B, S, D)

def first_inputs(seed: int = 0) -> dict:
    key = jax.random.key(seed)
    ks = jax.random.split(key, 21)
    n = jax.random.normal
    f32 = jnp.float32
    D = D_MODEL
    return {
        'x': n(ks[0], (BATCH, SEQ, D), f32),
        'c': n(ks[1], (BATCH, D), f32),
        'ada_w': n(ks[2], (DEPTH, D, 6 * D), f32) * (0.5 * D ** -0.5),
        'ada_b': n(ks[3], (DEPTH, 6 * D), f32) * 0.01,
        'ln1_g': 1.0 + 0.01 * n(ks[4], (DEPTH, D), f32),
        'ln2_g': 1.0 + 0.01 * n(ks[5], (DEPTH, D), f32),
        'w_in': n(ks[6], (DEPTH, D, IN_W), f32) * D ** -0.5,
        'nsa_q_gain': 1.0 + 0.01 * n(ks[7], (DEPTH, HEAD_DIM), f32),
        'nsa_k_gain': 1.0 + 0.01 * n(ks[8], (DEPTH, HEAD_DIM), f32),
        'nsa_cmp_pos': 0.1 * n(ks[9], (DEPTH, 2, NSA_CMP_LEN, HEAD_DIM), f32),
        'nsa_cmp_w1': n(ks[10], (DEPTH, 2, NSA_CMP_LEN * HEAD_DIM, NSA_CMP_HID), f32) * (NSA_CMP_LEN * HEAD_DIM) ** -0.5,
        'nsa_cmp_w2': n(ks[11], (DEPTH, 2, NSA_CMP_HID, HEAD_DIM), f32) * NSA_CMP_HID ** -0.5,
        'moba_q_gain': 1.0 + 0.01 * n(ks[12], (DEPTH, HEAD_DIM), f32),
        'moba_k_gain': 1.0 + 0.01 * n(ks[13], (DEPTH, HEAD_DIM), f32),
        'w_out': n(ks[14], (DEPTH, MIX_W, D), f32) * MIX_W ** -0.5,
        'router_w': n(ks[15], (DEPTH, D, N_EXPERTS), f32) * D ** -0.5,
        'router_b': 0.01 * n(ks[16], (DEPTH, N_EXPERTS), f32),
        'exp_w1': n(ks[17], (DEPTH, N_EXPERTS, D, 2 * D_FF), f32) * D ** -0.5,
        'exp_b1': 0.01 * n(ks[18], (DEPTH, N_EXPERTS, 2 * D_FF), f32),
        'exp_w2': n(ks[19], (DEPTH, N_EXPERTS, D_FF, D), f32) * D_FF ** -0.5,
        'exp_b2': 0.01 * n(ks[20], (DEPTH, N_EXPERTS, D), f32),
    }

def first_block(x, c, ada_w, ada_b, ln1_g, ln2_g, w_in, nsa_q_gain, nsa_k_gain, nsa_cmp_pos, nsa_cmp_w1,
              nsa_cmp_w2, moba_q_gain, moba_k_gain, w_out, router_w, router_b, exp_w1, exp_b1, exp_w2, exp_b2):
    cond = jax.nn.silu(c)
    for l in range(DEPTH):
        mod = (cond @ ada_w[l] + ada_b[l])[:, None, :]
        sh1, sc1, g1, sh2, sc2, g2 = jnp.split(mod, 6, axis=-1)
        h = rms_norm(x, ln1_g[l]) * (1.0 + sc1) + sh1
        x = x + g1 * hybrid_mixer(h, w_in[l], w_out[l], nsa_q_gain[l], nsa_k_gain[l], nsa_cmp_pos[l],
                                  nsa_cmp_w1[l], nsa_cmp_w2[l], moba_q_gain[l], moba_k_gain[l])
        h = rms_norm(x, ln2_g[l]) * (1.0 + sc2) + sh2
        x = x + g2 * sparse_moe(h, router_w[l], router_b[l], exp_w1[l], exp_b1[l], exp_w2[l], exp_b2[l])
    return x


MIX_WIDTH = D_MODEL
DA_HEADS = 4
DA_QK_DIM = 64
DA_V_DIM = 2 * DA_QK_DIM
DA_WIDTH = DA_HEADS * DA_V_DIM
RET_HEADS = 4
RET_QK_DIM = 64
RET_V_DIM = 2 * RET_QK_DIM
RET_WIDTH = RET_HEADS * RET_V_DIM
Q_BLOCK = 128
RET_CHUNK = 128

DA_Q_COLS = DA_HEADS * 2 * DA_QK_DIM
DA_K_COLS = DA_HEADS * 2 * DA_QK_DIM
DA_V_COLS = DA_WIDTH
DA_G_COLS = DA_WIDTH
RET_Q_COLS = RET_HEADS * RET_QK_DIM
RET_K_COLS = RET_HEADS * RET_QK_DIM
RET_V_COLS = RET_WIDTH
RET_G_COLS = RET_WIDTH
IN_WIDTH = DA_Q_COLS + DA_K_COLS + DA_V_COLS + DA_G_COLS + RET_Q_COLS + RET_K_COLS + RET_V_COLS + RET_G_COLS


def _rms(x, w=None):
    xf = x.astype(jnp.float32)
    y = xf * lax.rsqrt(jnp.mean(xf * xf, axis=-1, keepdims=True) + EPS)
    if w is not None:
        y = y * w.astype(jnp.float32)
    return y.astype(x.dtype)

def _alibi_slopes(n_heads):
    return jnp.asarray([2.0 ** (-8.0 * (i + 1) / n_heads) for i in range(n_heads)], dtype=jnp.float32)

def _diff_attention(q, k, v, lam, slopes):
    b, s = q.shape[0], q.shape[1]
    q = jnp.transpose(q, (0, 2, 3, 1, 4))
    k = jnp.transpose(k, (0, 2, 3, 1, 4))
    v = jnp.transpose(v, (0, 2, 1, 3))
    scale = DA_QK_DIM ** -0.5
    key_pos = jnp.arange(s)

    def block(i):
        start = i * Q_BLOCK
        qb = lax.dynamic_slice_in_dim(q, start, Q_BLOCK, axis=3)
        sc = jnp.einsum('bhmqd,bhmkd->bhmqk', qb, k).astype(jnp.float32) * scale
        qpos = start + jnp.arange(Q_BLOCK)
        dist = jnp.abs(qpos[:, None] - key_pos[None, :]).astype(jnp.float32)
        sc = sc - (slopes[:, None, None] * dist)[None, :, None]
        p = jax.nn.softmax(sc, axis=-1)
        w = p[:, :, 0] - lam * p[:, :, 1]
        return jnp.einsum('bhqk,bhkd->bhqd', w.astype(v.dtype), v)

    out = lax.map(block, jnp.arange(s // Q_BLOCK))
    return jnp.transpose(out, (1, 0, 3, 2, 4)).reshape(b, s, DA_HEADS, DA_V_DIM)

def _retention_dir(q, k, v, log_g, inclusive):
    b, h, s, dk = q.shape
    dv = v.shape[-1]
    nc = s // RET_CHUNK

    def chunks(t):
        return jnp.moveaxis(t.reshape(b, h, nc, RET_CHUNK, t.shape[-1]), 2, 0)

    n = jnp.arange(RET_CHUNK)
    diff = n[:, None] - n[None, :]
    mask = diff >= 0 if inclusive else diff > 0
    dmat = jnp.where(mask[None], jnp.exp(log_g[:, None, None] * jnp.maximum(diff, 0).astype(jnp.float32)), 0.0)
    xi = jnp.exp(log_g[:, None] * (n + 1).astype(jnp.float32))
    zeta = jnp.exp(log_g[:, None] * (RET_CHUNK - 1 - n).astype(jnp.float32))
    chunk_decay = jnp.exp(log_g * RET_CHUNK)

    def step(state, qkv):
        qc, kc, vc = qkv
        inner = jnp.einsum('bhqk,bhkv->bhqv', jnp.einsum('bhqd,bhkd->bhqk', qc, kc) * dmat, vc)
        cross = jnp.einsum('bhqd,bhdv->bhqv', qc * xi[..., None], state)
        new_state = chunk_decay[:, None, None] * state + jnp.einsum('bhkd,bhkv->bhdv', kc * zeta[..., None], vc)
        return new_state, inner + cross

    state0 = jnp.zeros((b, h, dk, dv), jnp.float32)
    _, out = lax.scan(step, state0, (chunks(q), chunks(k), chunks(v)))
    return jnp.moveaxis(out, 0, 2).reshape(b, h, s, dv)

def _bidirectional_retention(q, k, v, decay_fwd, decay_bwd):
    qf = jnp.transpose(q, (0, 2, 1, 3)).astype(jnp.float32)
    kf = jnp.transpose(k, (0, 2, 1, 3)).astype(jnp.float32) * (RET_QK_DIM ** -0.5)
    vf = jnp.transpose(v, (0, 2, 1, 3)).astype(jnp.float32)
    lg_f = jax.nn.log_sigmoid(decay_fwd.astype(jnp.float32))
    lg_b = jax.nn.log_sigmoid(decay_bwd.astype(jnp.float32))
    fwd = _retention_dir(qf, kf, vf, lg_f, True)
    flip = lambda t: jnp.flip(t, axis=2)
    bwd = flip(_retention_dir(flip(qf), flip(kf), flip(vf), lg_b, False))
    out = _rms(fwd + bwd)
    return jnp.transpose(out, (0, 2, 1, 3)).astype(q.dtype)

def second_inputs(seed: int = 0) -> dict:
    key = jax.random.key(seed)
    ks = jax.random.split(key, 14)
    x = jax.random.normal(ks[0], (BATCH, SEQ, D_MODEL), jnp.float32)
    norm_w = 1.0 + 0.02 * jax.random.normal(ks[1], (DEPTH, D_MODEL), jnp.float32)
    w_in = jax.random.normal(ks[2], (DEPTH, D_MODEL, IN_WIDTH), jnp.float32) * D_MODEL ** -0.5
    q_norm_w = 1.0 + 0.02 * jax.random.normal(ks[3], (DEPTH, DA_QK_DIM), jnp.float32)
    k_norm_w = 1.0 + 0.02 * jax.random.normal(ks[4], (DEPTH, DA_QK_DIM), jnp.float32)
    lambda_q1 = 0.1 * jax.random.normal(ks[5], (DEPTH, DA_QK_DIM), jnp.float32)
    lambda_k1 = 0.1 * jax.random.normal(ks[6], (DEPTH, DA_QK_DIM), jnp.float32)
    lambda_q2 = 0.1 * jax.random.normal(ks[7], (DEPTH, DA_QK_DIM), jnp.float32)
    lambda_k2 = 0.1 * jax.random.normal(ks[8], (DEPTH, DA_QK_DIM), jnp.float32)
    subln_w = 1.0 + 0.02 * jax.random.normal(ks[9], (DEPTH, DA_V_DIM), jnp.float32)
    gamma = 1.0 - 2.0 ** (-5.0 - jnp.arange(RET_HEADS, dtype=jnp.float32))
    base_logit = jnp.log(gamma) - jnp.log1p(-gamma)
    ret_decay_fwd = base_logit[None] + 0.1 * jax.random.normal(ks[10], (DEPTH, RET_HEADS), jnp.float32)
    ret_decay_bwd = base_logit[None] + 0.1 * jax.random.normal(ks[11], (DEPTH, RET_HEADS), jnp.float32)
    w_out = jax.random.normal(ks[12], (DEPTH, MIX_WIDTH, D_MODEL), jnp.float32) * (MIX_WIDTH ** -0.5) / math.sqrt(2.0 * DEPTH)
    return {"x": x, "norm_w": norm_w, "w_in": w_in, "q_norm_w": q_norm_w, "k_norm_w": k_norm_w,
            "lambda_q1": lambda_q1, "lambda_k1": lambda_k1, "lambda_q2": lambda_q2, "lambda_k2": lambda_k2,
            "subln_w": subln_w, "ret_decay_fwd": ret_decay_fwd, "ret_decay_bwd": ret_decay_bwd, "w_out": w_out}

def second_block(x, norm_w, w_in, q_norm_w, k_norm_w, lambda_q1, lambda_k1, lambda_q2, lambda_k2,
              subln_w, ret_decay_fwd, ret_decay_bwd, w_out):
    b, s, _ = x.shape
    slopes = _alibi_slopes(DA_HEADS)
    sizes = [DA_Q_COLS, DA_K_COLS, DA_V_COLS, DA_G_COLS, RET_Q_COLS, RET_K_COLS, RET_V_COLS, RET_G_COLS]
    offsets = [int(o) for o in np.cumsum(sizes)[:-1]]
    for l in range(DEPTH):
        xn = _rms(x, norm_w[l])
        h = jnp.einsum('bsd,de->bse', xn, w_in[l])
        qa, ka, va, ga, qr, kr, vr, gr = jnp.split(h, offsets, axis=-1)

        lambda_init = 0.8 - 0.6 * math.exp(-0.3 * l)
        lam = (jnp.exp(jnp.sum(lambda_q1[l].astype(jnp.float32) * lambda_k1[l].astype(jnp.float32)))
               - jnp.exp(jnp.sum(lambda_q2[l].astype(jnp.float32) * lambda_k2[l].astype(jnp.float32)))
               + lambda_init)
        qa = _rms(qa.reshape(b, s, DA_HEADS, 2, DA_QK_DIM), q_norm_w[l])
        ka = _rms(ka.reshape(b, s, DA_HEADS, 2, DA_QK_DIM), k_norm_w[l])
        va = va.reshape(b, s, DA_HEADS, DA_V_DIM)
        oa = _diff_attention(qa, ka, va, lam, slopes)
        oa = (_rms(oa, subln_w[l]) * (1.0 - lambda_init)).reshape(b, s, DA_WIDTH)

        qr = qr.reshape(b, s, RET_HEADS, RET_QK_DIM)
        kr = kr.reshape(b, s, RET_HEADS, RET_QK_DIM)
        vr = vr.reshape(b, s, RET_HEADS, RET_V_DIM)
        orr = _bidirectional_retention(qr, kr, vr, ret_decay_fwd[l], ret_decay_bwd[l]).reshape(b, s, RET_WIDTH)

        mixed = jnp.concatenate([oa * jax.nn.silu(ga), orr * jax.nn.silu(gr)], axis=-1)
        x = x + jnp.einsum('bse,ed->bsd', mixed, w_out[l])
    return x


def setup_inputs(seed=0):
    out = dict(first_inputs(seed))
    for name, value in second_inputs(seed + 1).items():
        if name != "x":
            out[name + "_2"] = value
    return out


def reference(
    x, c, ada_w, ada_b, ln1_g, ln2_g, w_in, nsa_q_gain, nsa_k_gain, nsa_cmp_pos, nsa_cmp_w1,
    nsa_cmp_w2, moba_q_gain, moba_k_gain, w_out, router_w, router_b, exp_w1, exp_b1, exp_w2,
    exp_b2, norm_w_2, w_in_2, q_norm_w_2, k_norm_w_2, lambda_q1_2, lambda_k1_2, lambda_q2_2,
    lambda_k2_2, subln_w_2, ret_decay_fwd_2, ret_decay_bwd_2, w_out_2,
):
    x = first_block(
        x, c, ada_w, ada_b, ln1_g, ln2_g, w_in, nsa_q_gain, nsa_k_gain, nsa_cmp_pos, nsa_cmp_w1,
        nsa_cmp_w2, moba_q_gain, moba_k_gain, w_out, router_w, router_b, exp_w1, exp_b1, exp_w2,
        exp_b2,
    )
    return second_block(
        x, norm_w_2, w_in_2, q_norm_w_2, k_norm_w_2, lambda_q1_2, lambda_k1_2, lambda_q2_2,
        lambda_k2_2, subln_w_2, ret_decay_fwd_2, ret_decay_bwd_2, w_out_2,
    )


_drawn_inputs = setup_inputs


def setup_inputs(seed=0):
    import zlib

    import numpy as np

    out = dict(_drawn_inputs(seed))
    spreads = {}
    factors = {'ada_b': 3.011,
     'ln1_g': 8.0,
     'ln2_g': 4.075,
     'nsa_q_gain': 8.0,
     'nsa_k_gain': 8.0,
     'nsa_cmp_pos': 3.671,
     'moba_q_gain': 8.0,
     'moba_k_gain': 8.0,
     'router_b': 4.09,
     'exp_b1': 8.0,
     'exp_b2': 8.0,
     'norm_w_2': 3.894,
     'q_norm_w_2': 8.0,
     'k_norm_w_2': 8.0,
     'lambda_q1_2': 8.0,
     'lambda_k1_2': 8.0,
     'lambda_q2_2': 5.86,
     'lambda_k2_2': 4.655,
     'subln_w_2': 8.0}
    for name, (base, spread) in spreads.items():
        noise = np.random.default_rng([zlib.crc32(name.encode()), seed]).standard_normal(out[name].shape)
        drawn = base * np.exp(spread * noise) if base else spread * noise
        out[name] = jnp.asarray(drawn.astype(out[name].dtype))
    for name, factor in factors.items():
        out[name] = (out[name] * factor).astype(out[name].dtype)
    return out
```

```python
from contextlib import ExitStack

import concourse.bass as bass
from concourse import mybir

F32 = mybir.dt.float32
I32 = mybir.dt.int32
U32 = mybir.dt.uint32
ALU = mybir.AluOpType
ACT = mybir.ActivationFunctionType
X = mybir.AxisListType.X

P = 128
S = 512
D = 1024
NT = S // P
ND = D // P
EPS = 1e-6
NEG = 1e30
HD = 64
HEADS = 8
CMP_N = 32
CMP_L, CMP_STRIDE = 32, 16
NEXP, TOPK, FF = 32, 4, 1024
CAP = 128
SLOTS = 12
SW = 256
FIRST_SLOT = 5
JUNK = S * TOPK
ALPHA, LIMIT = 1.702, 7.0
LAMBDA_INIT = 0.2


def chunk_plan():
    plan = [("ada", i, 1) for i in range(8)]
    plan += [("q_nsa", 0, 1), ("q_nsa", 1, 1), ("kv_cmp", 0, 1), ("kv_slc", 0, 1), ("kv_win", 0, 1)]
    plan += [("cmp_w1", 0, 2), ("cmp_w1", 1, 2)]
    plan += [("q_moba", i, 1) for i in range(2)] + [("k_moba", i, 1) for i in range(2)]
    plan += [("v_moba", i, 1) for i in range(2)]
    plan += [("ada", i, 1) for i in range(8, 24)]
    plan += [("w_out", i, 1) for i in range(4)]
    at, before = FIRST_SLOT, {}
    for name, part, n in plan:
        before[name, part] = at
        at += n
    moe = at
    assert moe % SLOTS == 0
    after = [("w_in_2", i, 1) for i in range(14)] + [("w_out_2", i, 1) for i in range(4)]
    at = moe + SLOTS * NEXP
    for name, part, n in after:
        before[name, part] = at
        at += n
    return plan, after, before, moe


def two_block_layer(nc, x, c, ada_w, ada_b, ln1_g, ln2_g, w_in, nsa_q_gain, nsa_k_gain, nsa_cmp_pos,
                 nsa_cmp_w1, nsa_cmp_w2, moba_q_gain, moba_k_gain, w_out, router_w, router_b,
                 exp_w1, exp_b1, exp_w2, exp_b2, norm_w_2, w_in_2, q_norm_w_2, k_norm_w_2,
                 lambda_q1_2, lambda_k1_2, lambda_q2_2, lambda_k2_2, subln_w_2,
                 ret_decay_fwd_2, ret_decay_bwd_2, w_out_2, out):
    PLAN, AFTER, PLACE, MOE0 = chunk_plan()

    h2_dram = nc.dram_tensor("h2_rows", (S, D), F32, kind="Internal").ap()
    y_dram = nc.dram_tensor("expert_rows", (JUNK + CAP, D), F32, kind="Internal").ap()

    with ExitStack() as ctx:
        def sb(name, shape, dt=F32):
            return ctx.enter_context(nc.sbuf_tensor(name, shape, dt))

        def sem(name):
            return ctx.enter_context(nc.semaphore(name))

        bank = [ctx.enter_context(nc.psum_tensor(f"bank{i}", [P, 512], F32)) for i in range(8)]

        ring = sb("ring", [P, SLOTS, 8, SW])
        ringf = ring[:, :, :, :].rearrange("p s k c -> p (s k c)")
        resT = sb("resT", [P, ND, S])
        hT = sb("hT", [P, ND, S])
        ident = sb("ident", [P, P])
        ones = sb("ones", [P, P])
        head_mean = sb("head_mean", [P, P])
        before_tok = sb("before_tok", [P, P])
        iota_c = sb("iota_c", [P, P])
        vecs = sb("vecs", [P, 96])
        mod = sb("mod", [P, 48])
        small = sb("small", [P, 64])
        ARENA = 18432
        arena = sb("arena", [P, ARENA])

        def room(at, shape, parts=P):
            n = 1
            for s in shape:
                n *= s
            assert at + n <= ARENA, (at, shape)
            ap = arena[0:parts, at:at + n]
            if len(shape) == 1:
                return ap
            if len(shape) == 2:
                return ap.rearrange("p (a b) -> p a b", b=shape[1])
            return ap.rearrange("p (a b c) -> p a b c", b=shape[1], c=shape[2])

        qkT = room(0, [8, S])
        vtok = room(4096, [NT, S])
        gtok = room(6144, [NT, S])
        OM = 8192
        omix = room(OM, [NT, D])
        x_rows = omix
        rows_out = omix
        BI = OM + 4096
        bias8 = room(BI, [HEADS, S])
        bias4 = room(BI, [4, 896])
        decay = room(BI, [4, 896])
        WK = BI + 4096
        work = room(WK, [4, S])
        biased = [work[:, 0, :], work[:, 1, :]]
        probT = [work[:, 2, :], work[:, 3, :]]
        sq = [work[:, 0, :], work[:, 1, :]]
        rr = [work[:, 2, :], work[:, 3, :]]
        cmp_in = [room(6144, [CMP_L, CMP_N]), room(7168, [CMP_L, CMP_N])]
        cmp_bias = room(6144 + 0, [NT, HEADS, CMP_N])
        cmp_s = room(7168, [HEADS, CMP_N])
        cmp_pT = room(7168 + 256, [2, P])
        vc_diag = room(7168 + 512, [2, 256])
        hid = room(WK, [4, CMP_N])
        hid4 = room(WK + 128, [2, 4, CMP_N])
        hid_t = room(WK + 384, [4, CMP_N])
        posT = sb("posT", [P, 2, CMP_L])
        cw2 = sb("cw2", [P, 2, HD])
        kcT = room(WK + 512, [CMP_N])
        kc_n = room(WK + 640, [P], CMP_N)
        gate_w = room(6144, [8, 24])
        nsa_gate = sb("nsa_gate", [P, NT, 24])
        xg = room(0, [D])
        xgT = room(1024, [ND, CAP])
        actT = room(2048, [ND, CAP])
        ybuf = room(3072, [D])
        onehot = room(4096, [NT, CAP])
        route = room(4608, [NT, NEXP, 4])
        b1T = room(5120, [NEXP, 16])
        g_t = room(5632, [2, CAP])
        s_t = room(5888, [2, CAP])
        l_t = room(6144, [2, CAP])
        sel = room(6400, [NT, NEXP])
        posm = room(6528, [NT, NEXP])
        gates = room(6656, [NT, NEXP])
        lg = room(6784, [NT, NEXP])
        lt = room(6912, [NT, NEXP])
        cnt = room(7040, [4, NEXP])
        gatesT = room(7168, [S], NEXP)
        b1_rows = room(OM + 1024, [2 * FF], NEXP)
        y_rows = [room(0, [TOPK, D]), room(BI, [TOPK, D])]
        rw = room(OM + 3072, [ND, NEXP])
        rb_row = sb("rb_row", [1, NEXP])
        b2_keep = room(OM, [D], NEXP)
        h2_rows = room(BI, [NT, D])
        vec_rows = room(WK + 512, [P], 86)
        pos_rows = room(WK + 1024, [2 * P], CMP_L)
        ret_s = [work, qkT[:, 4:8, :]]
        ret_dist = omix[:, 2:4, 512:960]
        ret_tmp = omix[:, 0:2, 512:960]
        m8 = sb("m8", [P, NT, 8])
        b1c = sb("b1c", [P, 16])
        meta = sb("meta", [P, 4])
        meta_c = sb("meta_c", [P, 4])
        iota_b = room(7680, [CAP])
        src_i = sb("src_i", [P, 1], U32)
        dst_i = sb("dst_i", [P, 1], U32)
        dst_n = sb("dst_n", [P, 1])
        extra_i = sb("extra_i", [1, 1], I32)
        exp_i = sb("exp_i", [1, 1], I32)
        mn = sb("mn", [P, 4])
        ls = sb("ls", [P, 4])
        cf = sb("cf", [P, 4])
        cs = sb("cs", [P, 5, HEADS])
        lam_rows = sb("lam_rows", [P, 4, HD])
        subln = sb("subln", [P, P])
        lgam = sb("lgam", [P, 8, 8])
        ms = sb("ms", [P, 4])

        eps_c, tok_c, junk_c, valid_c = 0, 1, 5, 6
        a1_c, g_c, a2_c, lam_c, o_c = 10, 18, 24, 32, 40
        tok_id = small[:, tok_c:tok_c + NT]
        junk = small[:, junk_c:junk_c + 1]
        row_ok = small[:, valid_c:valid_c + NT]
        a1, a2 = small[:, a1_c:a1_c + 8], small[:, a2_c:a2_c + 8]
        gain = small[:, g_c:g_c + 6]
        lam = small[:, lam_c:lam_c + 6]
        o_cell = small[:, o_c:o_c + 4]
        neg_junk = small[:, 44:45]
        eps = small[:, eps_c:eps_c + 1]

        landed = [sem(f"landed{s}") for s in range(SLOTS)]
        slot_used = sem("slot_used")
        vec_in, x_in, gate_in, small_in = sem("vec_in"), sem("x_in"), sem("gate_in"), sem("small_in")
        q_in = sem("q_in")
        rt_in, lam_in, b_in = sem("rt_in"), sem("lam_in"), sem("b_in")
        pool_c = sem("pool_c")
        consts = sem("consts")
        dv = sem("dv")
        ac = sem("ac")
        vec_t, vec_ok = sem("vec_t"), sem("vec_ok")
        xt_t, xt_ok = sem("xt_t"), sem("xt_ok")
        silu_e, silu_ok = sem("silu_e"), sem("silu_ok")
        mod_a, mod_ok = sem("mod_a"), sem("mod_ok")
        sq_ok, sum_ok, rstd_ok, hs_ok, h_ok = sem("sq_ok"), sem("sum_ok"), sem("rstd_ok"), sem("hs_ok"), sem("h_ok")
        z_done, z_sq, z_mean, z_r, z_free = sem("z_done"), sem("z_sq"), sem("z_mean"), sem("z_r"), sem("z_free")
        dist_ok, scaled_ok, bias_ok = sem("dist_ok"), sem("scaled_ok"), sem("bias_ok")
        s_done, s_bias, s_exp, t_done, t_ok, o_done, o_acc = (
            sem(n) for n in ("s_done", "s_bias", "s_exp", "t_done", "t_ok", "o_done", "o_acc"))
        c_in, c_pe, c_dv, c_ac = sem("c_in"), sem("c_pe"), sem("c_dv"), sem("c_ac")
        mixT_t, mixT_ok, out_t, res_ok = sem("mixT_t"), sem("mixT_ok"), sem("out_t"), sem("res_ok")
        r_pe, r_dv, r_ac, h2_t, h2_ok, h2_out = (
            sem(n) for n in ("r_pe", "r_dv", "r_ac", "h2_t", "h2_ok", "h2_out"))

        class BlockSignals:
            def __init__(self, n):
                self.hot, self.idx, self.idx_ok, self.got, self.xt, self.xt_ok = (
                    sem(n + w) for w in ("hot", "idx", "idx_ok", "got", "xt", "xt_ok"))
                self.u, self.g, self.sig, self.act, self.y, self.y_ok, self.put = (
                    sem(n + w) for w in ("u", "g", "sig", "act", "y", "y_ok", "put"))
                self.free, self.dst, self.l = sem(n + "free"), sem(n + "dst"), sem(n + "l")
        main, over = BlockSignals("m_"), BlockSignals("o_")
        waited_sp, waited_pe, waited_dve, waited_pool = (sem("waited_" + n) for n in ("sp", "pe", "dve", "pool"))
        exp_ok, over_done, over_in, over_used = sem("exp_ok"), sem("over_done"), sem("over_in"), sem("over_used")
        y_in = [sem("y_in0"), sem("y_in1")]
        y_sum, y_t, y_used = sem("y_sum"), sem("y_t"), sem("y_used")
        f_t, f_ok, f_out = sem("f_t"), sem("f_ok"), sem("f_out")
        g_pe, g_dv, g_ac = sem("g_pe"), sem("g_dv"), sem("g_ac")
        rt_s, rt_d, rt_o, rt_f = sem("rt_s"), sem("rt_d"), sem("rt_o"), sem("rt_f")
        rt_pv, rt_rd, rt_m = sem("rt_pv"), sem("rt_rd"), sem("rt_m")
        lg_ok, sel_ok, gT_ok = sem("lg_ok"), sem("sel_ok"), sem("gT_ok")
        CP0, CD0 = 3, 12

        def slot(n):
            return n % SLOTS

        def fill_of(n):
            return (n - slot(n)) // SLOTS + (0 if slot(n) < FIRST_SLOT else 1)

        def arrived(eng, name, part=0, slots=1):
            n = PLACE[name, part]
            for m in range(n, n + slots):
                eng.wait_ge(landed[slot(m)], 16 * fill_of(m))

        def chunk(name, part=0):
            return ring[:, slot(PLACE[name, part]), :, :]

        def t_job(name, part, col, dst, g=None, scale=None):
            return dict(kind="T", name=name, part=part, col=col, dst=dst,
                        how="norm" if g is not None else "plain", g=g, scale=scale)

        def v_job(name, part, col, width, i0, dst, how="plain"):
            return dict(kind="V", name=name, part=part, col=col, width=width, i0=i0, dst=dst, how=how,
                        g=None, scale=None)

        nsa_jobs = [t_job("q_nsa", t // 2, P * (t % 2), qkT[:, t, :], 0) for t in range(4)]
        nsa_jobs += [t_job("kv_cmp", 0, 0, qkT[:, 6, :]), t_job("kv_cmp", 0, P, qkT[:, 7, :])]
        nsa_jobs += [t_job("kv_slc", 0, 0, qkT[:, 4, :], 1),
                     v_job("kv_slc", 0, P, P, 0, vtok[:, :, 0:P])]
        nsa_jobs += [t_job("kv_win", 0, 0, qkT[:, 5, :], 1),
                     v_job("kv_win", 0, P, P, 0, vtok[:, :, P:2 * P])]
        nsa_jobs += [dict(kind="G", how="sigmoid", dst=nsa_gate[:, :, :], name=None, g=None, scale=None)]
        moba_jobs = [t_job("q_moba", t // 2, P * (t % 2), qkT[:, t, :], 2) for t in range(4)]
        moba_jobs += [t_job("k_moba", t // 2, P * (t % 2), qkT[:, 4 + t, :], 3) for t in range(4)]
        moba_jobs += [v_job("v_moba", c, 0, SW, 2 * i, vtok[:, 2 * i:2 * i + 2, SW * c:SW * c + SW])
                      for c in range(2) for i in range(2)]
        da_jobs = [t_job("w_in_2", t // 2, P * (t % 2), qkT[:, t, :], 4) for t in range(4)]
        da_jobs += [t_job("w_in_2", 2 + t // 2, P * (t % 2), qkT[:, 4 + t, :], 5) for t in range(4)]
        da_jobs += [v_job("w_in_2", 4 + c, 0, SW, 2 * i, vtok[:, 2 * i:2 * i + 2, SW * c:SW * c + SW])
                    for c in range(2) for i in range(2)]
        da_jobs += [v_job("w_in_2", 6 + c, 0, SW, 2 * i, gtok[:, 2 * i:2 * i + 2, SW * c:SW * c + SW], "silu")
                    for c in range(2) for i in range(2)]
        ret_jobs = [t_job("w_in_2", 8, P * t, qkT[:, t, :], scale=HD ** -0.5) for t in range(2)]
        ret_jobs += [t_job("w_in_2", 9, P * t, qkT[:, 2 + t, :]) for t in range(2)]
        ret_jobs += [v_job("w_in_2", 10 + c, 0, SW, 2 * i, vtok[:, 2 * i:2 * i + 2, SW * c:SW * c + SW])
                     for c in range(2) for i in range(2)]
        ret_jobs += [v_job("w_in_2", 12 + c, 0, SW, 2 * i, gtok[:, 2 * i:2 * i + 2, SW * c:SW * c + SW], "silu")
                     for c in range(2) for i in range(2)]
        at = norms = rs = 0
        for jobs in (nsa_jobs, moba_jobs, da_jobs, ret_jobs):
            for n, j in enumerate(jobs):
                j.update(at=at, norm_at=norms, r_at=rs)
                j["last_of_chunk"] = j["name"] is not None and (
                    n + 1 == len(jobs) or (jobs[n + 1]["name"], jobs[n + 1].get("part")) != (j["name"], j.get("part")))
                at += 1
                norms += j["how"] == "norm"
                rs += j["how"] != "plain"

        def z_bank(j):
            return bank[j["at"] % 3]

        def mean_bank(j):
            return bank[3 + j["norm_at"] % 2]

        def pe_project(pe, jobs):
            def mean(j):
                pe.wait_ge(z_sq, j["norm_at"] + 1)
                pe.matmul(mean_bank(j)[:, :], head_mean[:, :], sq[j["norm_at"] % 2], start=True, stop=True)\
                  .then_inc(z_mean, 1)
            waiting = None
            for j in jobs:
                if j["at"] >= 3:
                    pe.wait_ge(z_free, j["at"] - 2)
                if j["name"]:
                    arrived(pe, j["name"], j["part"])
                if j["name"] == "q_nsa":
                    pe.wait_ge(q_in, 16 * 6)
                z = z_bank(j)
                if j["kind"] == "T":
                    for k in range(ND):
                        w = chunk(j["name"], j["part"])[:, k, j["col"]:j["col"] + P]
                        mm = pe.matmul(z[:, :], w, hT[:, k, :], start=(k == 0), stop=(k == ND - 1))
                elif j["kind"] == "V":
                    wd = j["width"]
                    for n in range(S // wd):
                        for k in range(ND):
                            i = j["i0"] + n
                            mm = pe.matmul(z[:, n * wd:(n + 1) * wd], hT[:, k, i * P:(i + 1) * P],
                                           chunk(j["name"], j["part"])[:, k, j["col"]:j["col"] + wd],
                                           start=(k == 0), stop=(k == ND - 1))
                else:
                    pe.wait_ge(gate_in, 16)
                    for i in range(NT):
                        for k in range(ND):
                            mm = pe.matmul(z[:, 24 * i:24 * i + 24], hT[:, k, i * P:(i + 1) * P],
                                           gate_w[:, k, :], start=(k == 0), stop=(k == ND - 1))
                mm.then_inc(z_done, 1)
                if j["last_of_chunk"]:
                    slots_read(pe)
                if waiting is not None:
                    mean(waiting)
                    waiting = None
                if j["how"] == "norm":
                    waiting = j
            if waiting is not None:
                mean(waiting)

        def slots_read(pe, n=1):
            pe.matmul(bank[7][0:32, 510:512], ident[:, 0:32], ident[:, 0:2], start=True, stop=True,
                      skip_group_check=True).then_inc(slot_used, n)

        def job_z(j):
            z = z_bank(j)
            if j["kind"] == "T":
                return z[:, :]
            if j["kind"] == "V":
                return z[:, :].rearrange("p (n w) -> p n w", w=j["width"])
            return z[:, 0:96].rearrange("p (n w) -> p n w", w=24)

        def job_r(j):
            r = rr[j["r_at"] % 2]
            if j["kind"] == "T":
                return r
            if j["kind"] == "V":
                return r.rearrange("p (n w) -> p n w", w=j["width"])
            return r[:, 0:96].rearrange("p (n w) -> p n w", w=24)

        def r_done_before(jobs_all, n):
            for j in jobs_all:
                if j["how"] != "plain" and j["r_at"] == n:
                    return j["at"] + 1

        ALL_JOBS = nsa_jobs + moba_jobs + da_jobs + ret_jobs

        def act_project(act, link, jobs):
            for j in jobs:
                if j["how"] == "plain":
                    continue
                act.wait_ge(z_done, j["at"] + 1)
                if j["r_at"] >= 2:
                    act.wait_ge(z_free, r_done_before(ALL_JOBS, j["r_at"] - 2))
                if j["how"] == "norm":
                    if j["norm_at"] >= 2:
                        act.wait_ge(z_mean, j["norm_at"] - 1)
                    act.activation(sq[j["norm_at"] % 2], z_bank(j)[:, :], ACT.Square).then_inc(z_sq, 1)
                    act.wait_ge(z_mean, j["norm_at"] + 1)
                    link(act.activation(job_r(j), mean_bank(j)[:, :], ACT.Ln, bias=eps))
                    act.activation(job_r(j), job_r(j), ACT.Exp, scale=-0.5).then_inc(z_r, 1)
                else:
                    act.activation(job_r(j), job_z(j), ACT.Sigmoid).then_inc(z_r, 1)

        def dve_project(dve, jobs):
            for j in jobs:
                if j["how"] == "plain":
                    dve.wait_ge(z_done, j["at"] + 1)
                    if j["scale"] is not None:
                        ins = dve.tensor_scalar(j["dst"], job_z(j), j["scale"], None, ALU.mult)
                    else:
                        ins = dve.tensor_copy(j["dst"], job_z(j))
                else:
                    dve.wait_ge(z_r, j["r_at"] + 1)
                    if j["how"] == "norm":
                        g = gain[:, j["g"]:j["g"] + 1]
                        ins = dve.scalar_tensor_tensor(out=j["dst"], in0=job_z(j), scalar=g, in1=job_r(j),
                                                       op0=ALU.mult, op1=ALU.mult)
                    elif j["how"] == "silu":
                        ins = dve.tensor_tensor(j["dst"], job_z(j), job_r(j), ALU.mult)
                    else:
                        ins = dve.tensor_copy(j["dst"], job_r(j))
                ins.then_inc(z_free, 1)

        nsa_steps, moba_steps, da_steps = [], [], []
        for br in range(2):
            for h in [0, 4, 1, 5, 2, 6, 3, 7]:
                half = HD * (h // 4)
                for i in range(NT):
                    nsa_steps.append(dict(
                        q=qkT[half:half + HD, h % 4, i * P:(i + 1) * P], k=qkT[half:half + HD, 4 + br, 0:P * (i + 1)],
                        v=lambda kt, br=br, half=half: vtok[:, kt, P * br + half:P * br + half + HD], vw=HD,
                        bias=bias8[:, h, S - P * (i + 1):S], blocks=i + 1,
                        over=nsa_gate[:, i, 3 * h + br + 1:3 * h + br + 2], dst=omix[:, i, HD * h:HD * h + HD], add=True))
        for h in range(HEADS):
            half = HD * (h % 2)
            for i in range(NT):
                moba_steps.append(dict(
                    q=qkT[half:half + HD, h // 2, i * P:(i + 1) * P], k=qkT[half:half + HD, 4 + h // 2, 0:P * (i + 1)],
                    v=lambda kt, h=h: vtok[:, kt, HD * h:HD * h + HD], vw=HD,
                    bias=bias8[:, h, S - P * (i + 1):S], blocks=i + 1,
                    over=None, dst=omix[:, i, 512 + HD * h:512 + HD * h + HD], add=False))
        for h in range(4):
            for m in range(2):
                for i in range(NT):
                    da_steps.append(dict(
                        q=qkT[HD * m:HD * m + HD, h, i * P:(i + 1) * P], k=qkT[HD * m:HD * m + HD, 4 + h, :],
                        v=lambda kt, h=h: vtok[:, kt, P * h:P * h + P], vw=P,
                        bias=bias4[:, h, 384 - P * i:384 - P * i + S], blocks=NT,
                        over=None if m == 0 else lam[:, 5:6], dst=omix[:, i, P * h:P * h + P], add=(m == 1)))
        at = 0
        for steps in (nsa_steps, moba_steps, da_steps):
            for st in steps:
                st["at"] = at
                at += 1
        O_NSA, O_MOBA, O_DA = len(nsa_steps), len(nsa_steps) + len(moba_steps), at

        def pe_attend(pe, steps):
            def scores(st):
                n = st["at"]
                if n >= 3:
                    pe.wait_ge(s_bias, n - 2)
                pe.matmul(bank[n % 3][:, 0:P * st["blocks"]], st["q"], st["k"], start=True, stop=True)\
                  .then_inc(s_done, 1)

            def turn(st):
                n = st["at"]
                pe.wait_ge(s_exp, n + 1)
                if n >= 3:
                    pe.wait_ge(t_ok, n - 2)
                for b in range(st["blocks"]):
                    mm = pe.transpose(bank[3 + n % 3][:, b * P:(b + 1) * P], biased[n % 2][:, b * P:(b + 1) * P],
                                      ident[:, :])
                mm.then_inc(t_done, 1)

            def values(st):
                n = st["at"]
                pe.wait_ge(t_ok, n + 1)
                if n >= 2:
                    pe.wait_ge(o_acc, n - 1)
                for b in range(st["blocks"]):
                    mm = pe.matmul(bank[6 + n % 2][:, 0:st["vw"]], probT[n % 2][:, b * P:(b + 1) * P], st["v"](b),
                                   start=(b == 0), stop=(b == st["blocks"] - 1))
                mm.then_inc(o_done, 1)
            for n in range(len(steps) + 2):
                if n < len(steps):
                    scores(steps[n])
                if 1 <= n <= len(steps):
                    turn(steps[n - 1])
                if n >= 2:
                    values(steps[n - 2])

        def act_attend(act, steps):
            def copy(st):
                n = st["at"]
                act.wait_ge(t_done, n + 1)
                if n >= 2:
                    act.wait_ge(o_done, n - 1)
                w = P * st["blocks"]
                act.activation(probT[n % 2][:, 0:w], bank[3 + n % 3][:, 0:w], ACT.Copy).then_inc(t_ok, 1)
            for m, st in enumerate(steps):
                n, w = st["at"], P * st["blocks"]
                act.wait_ge(s_bias, n + 1)
                if n >= 4:
                    act.wait_ge(o_acc, n - 3)
                act.activation(biased[n % 2][:, 0:w], biased[n % 2][:, 0:w], ACT.Exp, scale=-1.0,
                               bias=mn[:, n % 4:n % 4 + 1], accum_out=ls[:, n % 4:n % 4 + 1]).then_inc(s_exp, 1)
                if m >= 1:
                    copy(steps[m - 1])
            copy(steps[-1])

        def dve_attend(dve, link, steps):
            def accumulate(st):
                n = st["at"]
                c = cf[:, n % 4:n % 4 + 1]
                dve.wait_ge(s_exp, n + 1)
                link(dve.reciprocal(c, ls[:, n % 4:n % 4 + 1]))
                if st["over"] is not None:
                    link(dve.tensor_tensor(c, st["over"], c, ALU.mult))
                dve.wait_ge(o_done, n + 1)
                if n >= 1:
                    dve.wait_ge(o_acc, n)
                if st["add"]:
                    ins = dve.scalar_tensor_tensor(out=st["dst"], in0=bank[6 + n % 2][:, 0:st["vw"]], scalar=c,
                                                   in1=st["dst"], op0=ALU.mult, op1=ALU.add)
                else:
                    ins = dve.tensor_scalar(st["dst"], bank[6 + n % 2][:, 0:st["vw"]], c, None, ALU.mult)
                ins.then_inc(o_acc, 1)
            for m in range(len(steps) + 2):
                if m < len(steps):
                    st = steps[m]
                    n, w = st["at"], P * st["blocks"]
                    dve.wait_ge(s_done, n + 1)
                    if n >= 2:
                        dve.wait_ge(t_done, n - 1)
                    dve.tensor_tensor_reduce(out=biased[n % 2][:, 0:w], in0=bank[n % 3][:, 0:w], in1=st["bias"],
                                             scale=1.0, scalar=3e38, op0=ALU.add, op1=ALU.min,
                                             accum_out=mn[:, n % 4:n % 4 + 1]).then_inc(s_bias, 1)
                if m >= 2:
                    accumulate(steps[m - 2])

        def act_norm(act, link, r):
            for t in range(ND):
                n = ND * r + t
                if t >= 2:
                    act.wait_ge(sum_ok, n - 1)
                act.activation(sq[t % 2], resT[:, t, :], ACT.Square).then_inc(sq_ok, 1)
            act.wait_ge(sum_ok, ND * (r + 1))
            link(act.activation(rr[0], bank[0][:, :], ACT.Ln, scale=1.0 / D, bias=eps))
            act.activation(rr[0], rr[0], ACT.Exp, scale=-0.5).then_inc(rstd_ok, 1)

        def pe_norm(pe, r):
            for t in range(ND):
                pe.wait_ge(sq_ok, ND * r + t + 1)
                pe.matmul(bank[0][:, :], ones[:, :], sq[t % 2], start=(t == 0), stop=(t == ND - 1)).then_inc(sum_ok, 1)

        def dve_norm(dve, r, scale, done):
            dve.wait_ge(rstd_ok, r + 1)
            for t in range(ND):
                dve.scalar_tensor_tensor(out=hT[:, t, :], in0=resT[:, t, :], scalar=scale[:, t:t + 1], in1=rr[0],
                                         op0=ALU.mult, op1=ALU.mult).then_inc(done, 1)

        def act_shift(act, r, shift):
            for t in range(ND):
                act.wait_ge(hs_ok, ND * r + t + 1)
                act.activation(hT[:, t, :], hT[:, t, :], ACT.Identity, bias=shift[:, t:t + 1]).then_inc(h_ok, 1)

        def pe_out(pe, r, name, res0):
            for t in range(ND):
                if t >= 2:
                    pe.wait_ge(mixT_ok, ND * r + t - 1)
                for i in range(NT):
                    mm = pe.transpose(bank[t % 2][:, i * P:(i + 1) * P], omix[:, i, t * P:(t + 1) * P], ident[:, :])
                mm.then_inc(mixT_t, 1)
            pe.wait_ge(mixT_ok, ND * (r + 1))
            for n in range(ND):
                if n % 2 == 0:
                    arrived(pe, name, n // 2)
                if n >= 3:
                    pe.wait_ge(res_ok, res0 + n - 2)
                for k in range(ND):
                    mm = pe.matmul(bank[2 + n % 3][:, :], chunk(name, n // 2)[:, k, P * (n % 2):P * (n % 2) + P],
                                   hT[:, k, :], start=(k == 0), stop=(k == ND - 1))
                mm.then_inc(out_t, 1)
                if n % 2 and (r == 1 or n < ND - 1):
                    slots_read(pe)

        def act_out(act, r):
            for t in range(ND):
                act.wait_ge(mixT_t, ND * r + t + 1)
                act.activation(hT[:, t, :], bank[t % 2][:, :], ACT.Copy).then_inc(mixT_ok, 1)

        def dve_out(dve, r, scale, res0):
            for n in range(ND):
                dve.wait_ge(out_t, ND * r + n + 1)
                if scale is None:
                    ins = dve.tensor_tensor(resT[:, n, :], bank[2 + n % 3][:, :], resT[:, n, :], ALU.add)
                else:
                    ins = dve.scalar_tensor_tensor(out=resT[:, n, :], in0=bank[2 + n % 3][:, :],
                                                   scalar=scale[:, n:n + 1], in1=resT[:, n, :], op0=ALU.mult, op1=ALU.add)
                ins.then_inc(res_ok, 1)

        block = ctx.enter_context(nc.Block())

        @block.sync
        def _(sp):
            def rows(ap):
                return ap.rearrange("(k p) n -> p k n", p=P)

            def load(name, part, n, m):
                if n - SLOTS + m > FIRST_SLOT:
                    sp.wait_ge(slot_used, n - SLOTS + m - FIRST_SLOT)
                dst = ring[:, slot(n), :, :]
                if name == "ada":
                    sp.dma_start(dst, rows(ada_w[0])[:, :, SW * part:SW * (part + 1)]).then_inc(landed[slot(n)], 16)
                elif name == "q_nsa":
                    for t in range(2):
                        for g in range(2):
                            c0 = HD * (2 * part + t + 4 * g)
                            sp.dma_start(dst[:, :, P * t + HD * g:P * t + HD * (g + 1)], rows(w_in[0])[:, :, c0:c0 + HD])\
                              .then_inc(landed[slot(n)] if (t, g) == (1, 1) else q_in, 16)
                elif name == "cmp_w1":
                    src = nsa_cmp_w1[0, part].rearrange("(l d) h -> d l h", d=HD)
                    for a in range(2):
                        full = ringf[HD * a:HD * a + HD, slot(n) * 2048:(slot(n) + 2) * 2048]
                        sp.dma_start(full.rearrange("p (l h) -> p l h", h=P), src).then_inc(landed[slot(n + a)], 16)
                else:
                    src, c0 = {"kv_cmp": (w_in, 512), "kv_slc": (w_in, 768), "kv_win": (w_in, 1024),
                               "q_moba": (w_in, 1304), "k_moba": (w_in, 1816), "v_moba": (w_in, 2328),
                               "w_out": (w_out, 0), "w_in_2": (w_in_2, 0), "w_out_2": (w_out_2, 0)}[name]
                    c0 += SW * part
                    sp.dma_start(dst, rows(src[0])[:, :, c0:c0 + SW]).then_inc(landed[slot(n)], 16)

            for name, part, m in PLAN:
                load(name, part, PLACE[name, part], m)

            def expert(e, used, base, signal, fill):
                w1 = exp_w1[0].rearrange("e (k p) n -> p k e n", p=P)
                w2 = exp_w2[0].rearrange("e (k p) n -> p k e n", p=P)
                for j in range(4):
                    for half in range(2):
                        s = 2 * j + half
                        sp.wait_ge(used, base + s + 1)
                        c0 = FF * half + SW * j
                        sp.dma_start(ring[:, s, :, :], w1[:, :, bass.ds(e, 1), c0:c0 + SW].rearrange("p k e n -> p k (e n)"))\
                          .then_inc(signal[s], 16)
                for q in range(4):
                    s = 8 + q
                    sp.wait_ge(used, base + s + 1)
                    dst = ringf[:, s * 2048:(s + 1) * 2048].rearrange("p (k n) -> p k n", k=2)
                    sp.dma_start(dst, w2[:, 2 * q:2 * q + 2, bass.ds(e, 1), :].rearrange("p k e n -> p k (e n)"))\
                      .then_inc(signal[s], 16)

            with sp.Fori(0, NEXP) as e:
                expert(e, slot_used, e * SLOTS + (MOE0 - SLOTS - FIRST_SLOT), landed, None)

            sp.wait_ge(r_dv, 1)
            extra = sp.value_load(extra_i[0:1, 0:1], min_val=0, max_val=15)
            with sp.If(extra > 0):
                with sp.Fori(0, extra) as o:
                    sp.wait_ge(exp_ok, o + 1)
                    sp.sem_inc(waited_sp, 1)
                    e = sp.value_load(exp_i[0:1, 0:1], min_val=0, max_val=NEXP - 1)
                    w1 = exp_w1[0].rearrange("e (k p) n -> p k e n", p=P)
                    w2 = exp_w2[0].rearrange("e (k p) n -> p k e n", p=P)
                    for s in range(8):
                        c0 = FF * (s % 2) + SW * (s // 2)
                        sp.dma_start(ring[:, s, :, :], w1[:, :, bass.ds(e, 1), c0:c0 + SW].rearrange("p k e n -> p k (e n)"))\
                          .then_inc(over_in, 16)
                    for q in range(4):
                        dst = ringf[:, (8 + q) * 2048:(9 + q) * 2048].rearrange("p (k n) -> p k n", k=2)
                        sp.dma_start(dst, w2[:, 2 * q:2 * q + 2, bass.ds(e, 1), :].rearrange("p k e n -> p k (e n)"))\
                          .then_inc(over_in, 16)
            sp.wait_ge(over_done, 1)
            for name, part, m in AFTER:
                load(name, part, PLACE[name, part], m)

        @block.gpsimd
        def _(pool):
            count = [0]

            def link(ins):
                count[0] += 1
                ins.then_inc(pool_c, 1)
                pool.wait_ge(pool_c, count[0])

            pool.memset(ones[:, :], 1.0).then_inc(consts, 1)
            link(pool.memset(ident[:, :], 0.0))
            pool.affine_select(out=ident[:, :], in_=ident[:, :], compare_op=ALU.not_equal, fill=1.0, base=0,
                               pattern=[[-1, P]], channel_multiplier=1).then_inc(consts, 1)
            link(pool.memset(head_mean[:, :], 0.0))
            for a in range(2):
                pool.memset(head_mean[HD * a:HD * a + HD, HD * a:HD * a + HD], 1.0 / HD).then_inc(consts, 1)
            pool.wait_ge(consts, 4)
            pool.affine_select(out=before_tok[:, :], in_=ones[:, :], compare_op=ALU.is_gt, fill=0.0, base=0,
                               pattern=[[1, P]], channel_multiplier=-1).then_inc(consts, 1)
            pool.iota(iota_c[:, :], pattern=[[1, P]], base=0, channel_multiplier=0,
                      allow_small_or_imprecise_dtypes=True).then_inc(consts, 1)
            pool.iota(tok_id, pattern=[[P, NT]], base=0, channel_multiplier=1,
                      allow_small_or_imprecise_dtypes=True).then_inc(consts, 1)
            pool.iota(junk, pattern=[[1, 1]], base=JUNK, channel_multiplier=1,
                      allow_small_or_imprecise_dtypes=True).then_inc(consts, 1)
            pool.affine_select(out=row_ok, in_=ones[:, 0:NT], compare_op=ALU.is_ge, fill=0.0, base=-(CMP_L - 1),
                               pattern=[[P, NT]], channel_multiplier=1).then_inc(consts, 1)
            pool.memset(eps, EPS).then_inc(consts, 1)
            pool.iota(work[:, 0, :], pattern=[[-1, S]], base=S - P, channel_multiplier=1,
                      allow_small_or_imprecise_dtypes=True).then_inc(dist_ok, 1)
            for h in range(HEADS):
                pool.wait_ge(scaled_ok, h + 1)
                pool.affine_select(out=bias8[:, h, :], in_=bias8[:, h, :], compare_op=ALU.is_ge, fill=NEG,
                                   base=S - P, pattern=[[-1, S]], channel_multiplier=1).then_inc(bias_ok, 1)
            pool.wait_ge(c_dv, 8)
            pool.iota(cmp_bias, pattern=[[2 * P, NT], [0, HEADS], [-2 * CMP_STRIDE, CMP_N]],
                      base=-(CMP_L - 1), channel_multiplier=2, allow_small_or_imprecise_dtypes=True).then_inc(dist_ok, 1)
            for h in range(HEADS):
                pool.wait_ge(scaled_ok, HEADS + h + 1)
                pool.affine_select(out=cmp_bias[:, :, h, :], in_=cmp_bias[:, :, h, :], compare_op=ALU.is_ge, fill=NEG,
                                   base=-(CMP_L - 1), pattern=[[P, NT], [-CMP_STRIDE, CMP_N]],
                                   channel_multiplier=1).then_inc(bias_ok, 1)

            def fetch(sg, n):
                pool.wait_ge(sg.idx_ok, n)
                pool.sem_inc(waited_pool, 1)
                pool.indirect_dma_start(xg[:, :], None, h2_dram, bass.IndirectOffsetOnAxis(src_i[:, 0:1], 0))\
                    .then_inc(sg.got, 16)

            def put(sg, n, rows):
                pool.wait_ge(sg.y_ok, rows + 2)
                pool.wait_ge(sg.dst, n)
                pool.sem_inc(waited_pool, 1)
                pool.indirect_dma_start(y_dram, bass.IndirectOffsetOnAxis(dst_i[:, 0:1], 0), ybuf[:, :], None)\
                    .then_inc(sg.put, 16)
                pool.wait_ge(sg.put, n * 16)
                pool.sem_inc(sg.free, 1)

            for sg in (main, over):
                pool.sem_inc(sg.free, 1)
                pool.sem_inc(sg.y_ok, 2)
            pool.wait_ge(h2_out, 16 * NT)
            fetch(main, 1)
            with pool.Fori(0, NEXP - 1) as b:
                pool.wait_ge(main.xt, b * 2 + 2)
                fetch(main, b + 2)
                put(main, b + 1, b * 2 + 2)
            put(main, NEXP, 2 * NEXP)
            pool.wait_ge(r_dv, 1)
            extra = pool.value_load(extra_i[0:1, 0:1], min_val=0, max_val=15)
            with pool.If(extra > 0):
                with pool.Fori(0, extra) as o:
                    fetch(over, o + 1)
                    put(over, o + 1, o * 2 + 2)
            pool.wait_ge(res_ok, 2 * ND)
            pool.iota(bias4[:, 0, :], pattern=[[-1, 896]], base=384, channel_multiplier=1,
                      allow_small_or_imprecise_dtypes=True).then_inc(dist_ok, 1)
            pool.wait_ge(o_acc, O_DA)
            pool.wait_ge(s_bias, O_DA)
            pool.iota(ret_dist, pattern=[[448, 2], [1, 448]], base=-384, channel_multiplier=-1,
                      allow_small_or_imprecise_dtypes=True).then_inc(dist_ok, 1)

        @block.scalar
        def _(act):
            count = [0]

            def link(ins):
                count[0] += 1
                ins.then_inc(ac, 1)
                act.wait_ge(ac, count[0])

            def row(ap):
                return ap.rearrange("(a n) -> a n", a=1)
            for src, r0, n in ((ada_b, 0, 48), (ln1_g, 48, 8), (ln2_g, 56, 8), (norm_w_2, 64, 8), (c, 72, 8)):
                act.dma_start(arena[r0:r0 + n, WK + 512:WK + 512 + P], src[0].rearrange("(a b) -> a b", b=P)).then_inc(vec_in, 16)
            for n, src in enumerate((nsa_q_gain, nsa_k_gain, moba_q_gain, moba_k_gain, q_norm_w_2, k_norm_w_2)):
                for a in range(2):
                    act.dma_start(arena[80 + n:81 + n, WK + 512 + HD * a:WK + 512 + HD * a + HD], src).then_inc(vec_in, 16)
            act.dma_start(x_rows, x[0].rearrange("(i p) d -> p i d", p=P)).then_inc(x_in, 16)
            for kv in range(2):
                for a in range(2):
                    act.dma_start(arena[0:CMP_L, WK + 1024 + P * kv + HD * a:WK + 1024 + P * kv + HD * a + HD],
                                  nsa_cmp_pos[0, kv]).then_inc(vec_in, 16)
            act.dma_start(gate_w[:, :, :], w_in[0].rearrange("(k p) n -> p k n", p=P)[:, :, 1280:1304]).then_inc(gate_in, 16)
            act.dma_start(cw2[:, :, :],
                          nsa_cmp_w2[0].rearrange("k p n -> p k n")).then_inc(c_in, 16)
            act.dma_start(rb_row[:, :], router_b).then_inc(rt_in, 16)
            for n, src in enumerate((lambda_q1_2, lambda_k1_2, lambda_q2_2, lambda_k2_2)):
                act.dma_start(lam_rows[:, n, :], src.to_broadcast([P, HD])).then_inc(lam_in, 16)
            act.dma_start(subln[:, :], subln_w_2.to_broadcast([P, P])).then_inc(lam_in, 16)
            act.dma_start(lgam[:, 0, 0:4], ret_decay_fwd_2.to_broadcast([P, 4])).then_inc(lam_in, 16)
            act.dma_start(lgam[:, 0, 4:8], ret_decay_bwd_2.to_broadcast([P, 4])).then_inc(lam_in, 16)

            act.wait_ge(vec_ok, 1)
            act.activation(vecs[:, 88:96], vecs[:, 72:80], ACT.Exp, scale=-1.0).then_inc(silu_e, 1)
            for t in range(ND):
                act.wait_ge(xt_t, t + 1)
                act.activation(resT[:, t, :], bank[t % 4][:, :], ACT.Copy).then_inc(xt_ok, 1)
            act.wait_ge(consts, 10)
            act.wait_ge(xt_ok, ND)
            act.wait_ge(scaled_ok, HEADS)
            act_norm(act, link, 0)
            act.wait_ge(mod_ok, 1)
            act_shift(act, 0, mod[:, 0:8])

            act_project(act, link, nsa_jobs)

            act.wait_ge(c_dv, 7)
            act.activation(hid_t[:, :, :], hid_t[:, :, :], ACT.Exp, scale=-2.0 * 0.7978845608028654).then_inc(c_ac, 1)
            act.wait_ge(c_dv, 9)
            link(act.activation(cs[0:CMP_N, 0, 0:2], cs[0:CMP_N, 0, 0:2], ACT.Ln, bias=eps[0:CMP_N, :], scale=1.0 / HD))
            act.activation(cs[0:CMP_N, 0, 0:2], cs[0:CMP_N, 0, 0:2], ACT.Exp, scale=-0.5).then_inc(c_ac, 1)
            for i in range(NT):
                act.wait_ge(c_dv, CD0 + 3 * i + 1)
                act.activation(cmp_s, cmp_s, ACT.Exp, scale=-1.0).then_inc(c_ac, 1)
                act.wait_ge(c_pe, CP0 + 3 * i + 2)
                act.activation(cmp_pT, bank[2][:, 0:2 * P].rearrange("p (g q) -> p g q", g=2), ACT.Copy).then_inc(c_ac, 1)

            act_attend(act, nsa_steps)
            act_project(act, link, moba_jobs)
            act_attend(act, moba_steps)
            act_out(act, 0)

            act.wait_ge(mixT_ok, ND)
            act.dma_start(rw[:, :, :], router_w[0].rearrange("(k p) n -> p k n", p=P)).then_inc(rt_in, 16)
            act.dma_start(b1_rows, exp_b1[0]).then_inc(b_in, 16)
            act.dma_start(b2_keep, exp_b2[0]).then_inc(b_in, 16)
            act.wait_ge(res_ok, ND)
            act_norm(act, link, 1)
            act.wait_ge(mod_ok, 2)
            act_shift(act, 1, mod[:, 24:32])
            for i in range(NT):
                for a in range(2):
                    act.wait_ge(h2_t, 2 * i + a + 1)
                    act.activation(h2_rows[:, i, 512 * a:512 * a + 512], bank[4 + a][:, :], ACT.Copy).then_inc(h2_ok, 1)
                act.wait_ge(h2_ok, 2 * i + 2)
                act.dma_start(h2_dram[i * P:(i + 1) * P, :], h2_rows[:, i, :]).then_inc(h2_out, 16)
            act.wait_ge(lg_ok, 1)
            for i in range(NT):
                act.activation(gates[:, i, :], lg[:, i, :], ACT.Exp, bias=m8[:, i, 7:8]).then_inc(r_ac, 1)

            def sigmoids(sg, n):
                for j in range(8):
                    act.wait_ge(sg.g, n + (j + 1))
                    act.activation(s_t[:, j % 2, :], g_t[:, j % 2, :], ACT.Sigmoid, scale=ALPHA).then_inc(sg.sig, 1)

            def rows_in(sg, n):
                for a in range(2):
                    act.wait_ge(sg.xt, n + (a + 1))
                    act.activation(xgT[:, 4 * a:4 * a + 4, :], bank[5 + a][:, :].rearrange("p (k q) -> p k q", k=4),
                                   ACT.Copy).then_inc(sg.xt_ok, 1)

            def rows_done(sg, n):
                for a in range(2):
                    act.wait_ge(sg.y, n + (a + 1))
                    act.activation(ybuf[:, 512 * a:512 * a + 512], bank[3 + a][:, :], ACT.Copy,
                                   scale=meta_c[:, 2:3]).then_inc(sg.y_ok, 1)

            rows_in(main, 0)
            with act.Fori(0, NEXP - 1) as b:
                sigmoids(main, b * 8)
                rows_in(main, b * 2 + 2)
                act.wait_ge(main.free, b + 1)
                act.wait_ge(main.dst, b + 1)
                rows_done(main, b * 2)
            sigmoids(main, 8 * (NEXP - 1))
            act.wait_ge(main.free, NEXP)
            act.wait_ge(main.dst, NEXP)
            rows_done(main, 2 * (NEXP - 1))
            act.wait_ge(main.free, NEXP + 1)
            act.wait_ge(r_dv, 1)
            extra = act.value_load(extra_i[0:1, 0:1], min_val=0, max_val=15)
            with act.If(extra > 0):
                with act.Fori(0, extra) as o:
                    rows_in(over, o * 2)
                    sigmoids(over, o * 8)
                    act.wait_ge(over.dst, o + 1)
                    rows_done(over, o * 2)
                    act.wait_ge(over.free, o + 2)
            for i in range(NT):
                if i >= 2:
                    act.wait_ge(y_used, i - 1)
                act.dma_start(y_rows[i % 2], y_dram[TOPK * P * i:TOPK * P * (i + 1), :]
                              .rearrange("(p k) d -> p k d", k=TOPK)).then_inc(y_in[i % 2], 16)

            act.wait_ge(res_ok, 2 * ND)
            act_norm(act, link, 2)
            act.wait_ge(g_dv, 1)
            act.activation(lam[:, 2:4], lam[:, 0:2], ACT.Exp).then_inc(g_ac, 1)
            link(act.activation(lgam[:, 2, :], lgam[:, 1, :], ACT.Exp, scale=-1.0))
            act.activation(lgam[:, 4, :], lgam[:, 2, :], ACT.Ln, bias=ones[:, 0:1]).then_inc(g_ac, 1)
            act.wait_ge(h_ok, 3 * ND)
            act_project(act, link, da_jobs)
            act_attend(act, da_steps)

            def inverse_roots(n):
                act.wait_ge(rt_f, n + 1)
                link(act.activation(ms[:, :], ms[:, :], ACT.Ln, scale=1.0 / P, bias=eps))
                act.activation(ms[:, :], ms[:, :], ACT.Exp, scale=-0.5).then_inc(rt_o, 1)
            for i in range(NT):
                inverse_roots(i)
            act_project(act, link, ret_jobs)
            for h in range(4):
                act.wait_ge(g_dv, 2 + h)
                act.activation(decay[:, h, :], decay[:, h, :], ACT.Exp).then_inc(g_ac, 1)
            for h in range(4):
                inverse_roots(NT + h)
            act_out(act, 1)
            for i in range(NT):
                for a in range(2):
                    act.wait_ge(f_t, 2 * i + a + 1)
                    act.activation(rows_out[:, i, 512 * a:512 * a + 512], bank[5 + a][:, :], ACT.Copy).then_inc(f_ok, 1)
                act.wait_ge(f_ok, 2 * i + 2)
                act.dma_start(out[0].rearrange("(i p) d -> i p d", p=P)[i], rows_out[:, i, :]).then_inc(f_out, 16)
            act.wait_ge(f_out, 16 * NT)

        @block.tensor
        def _(pe):
            pe.wait_ge(vec_in, 21 * 16)
            pe.wait_ge(consts, 2)
            pe.transpose(bank[0][:, 0:86], vec_rows, ident[0:86, 0:86])
            for kv in range(2):
                mm = pe.transpose(bank[0][:, 96 + CMP_L * kv:96 + CMP_L * (kv + 1)], pos_rows[:, P * kv:P * kv + P],
                                  ident[0:CMP_L, 0:CMP_L])
            mm.then_inc(vec_t, 1)
            pe.wait_ge(vec_ok, 1)
            pe.wait_ge(x_in, 16)
            for t in range(ND):
                if t >= 4:
                    pe.wait_ge(xt_ok, t - 3)
                for i in range(NT):
                    mm = pe.transpose(bank[t % 4][:, i * P:(i + 1) * P], x_rows[:, i, t * P:(t + 1) * P], ident[:, :])
                mm.then_inc(xt_t, 1)

            def modulate(parts):
                for ch in parts:
                    arrived(pe, "ada", ch)
                    for m in (2 * ch, 2 * ch + 1):
                        for k in range(ND):
                            mm = pe.matmul(bank[5][:, m:m + 1], chunk("ada", ch)[:, k, P * (m % 2):P * (m % 2) + P],
                                           vecs[:, 80 + k:81 + k], start=(k == 0), stop=(k == ND - 1))
                    mm.then_inc(slot_used, 1)
            pe.wait_ge(silu_ok, 1)
            modulate(range(0, 7))
            modulate([7])
            pe.matmul(bank[7][:, 510:512], ident[:, :], ident[:, 0:2], start=True, stop=True).then_inc(mod_a, 1)
            pe.wait_ge(consts, 10)
            pe.wait_ge(xt_ok, ND)
            pe_norm(pe, 0)
            pe.wait_ge(h_ok, ND)
            pe_project(pe, nsa_jobs)

            pe.wait_ge(z_free, nsa_jobs[-1]["at"] + 1)
            pe.wait_ge(c_dv, 6)
            for kv in range(2):
                arrived(pe, "cmp_w1", kv, 2)
                s0 = slot(PLACE["cmp_w1", kv])
                w1 = ringf[:, s0 * 2048:(s0 + 2) * 2048].rearrange("p (l h) -> p l h", h=P)
                for g in range(2):
                    for l in range(CMP_L):
                        mm = pe.matmul(bank[2 * kv + g][:, 0:CMP_N], w1[HD * g:HD * g + HD, l, :],
                                       cmp_in[kv][HD * g:HD * g + HD, l, :], start=(l == 0), stop=(l == CMP_L - 1))
                slots_read(pe, 2)
            pe.matmul(bank[7][:, 510:512], ident[:, :], ident[:, 0:2], start=True, stop=True).then_inc(c_pe, 1)
            pe.wait_ge(c_dv, 8)
            pe.wait_ge(c_in, 16)
            for g in range(2):
                pe.matmul(bank[4][0:CMP_N, HD * g:HD * g + HD], hid[:, g, :], cw2[:, 0, :], start=True, stop=True)
                mm = pe.matmul(bank[5][:, HD * g:HD * g + HD], hid4[:, g, :, :].rearrange("p r n -> p (r n)"),
                               cw2[:, 1, :], start=True, stop=True)
            mm.then_inc(c_pe, 1)
            pe.wait_ge(c_dv, 10)
            pe.transpose(bank[6][:, 0:CMP_N], kc_n[:, :], ident[0:CMP_N, 0:CMP_N]).then_inc(c_pe, 1)
            pe.wait_ge(c_dv, CD0)
            for i in range(NT):
                for hh in range(4):
                    for g in range(2):
                        mm = pe.matmul(bank[g][:, CMP_N * hh:CMP_N * (hh + 1)],
                                       qkT[HD * g:HD * g + HD, hh, i * P:(i + 1) * P], kcT[HD * g:HD * g + HD, :],
                                       start=True, stop=True)
                mm.then_inc(c_pe, 1)
                pe.wait_ge(c_dv, CD0 + 3 * i + 2)
                for g in range(2):
                    mm = pe.transpose(bank[2][:, P * g:P * g + P], cmp_s[:, 4 * g:4 * g + 4, :].rearrange("p h n -> p (h n)"),
                                      ident[:, :])
                mm.then_inc(c_pe, 1)
                pe.wait_ge(c_ac, 2 + 2 * i + 2)
                if i >= 1:
                    pe.wait_ge(c_dv, CD0 + 3 * i)
                for g in range(2):
                    mm = pe.matmul(bank[3][:, SW * g:SW * g + SW], cmp_pT[:, g, :], vc_diag[:, g, :], start=True, stop=True)
                mm.then_inc(c_pe, 1)

            pe.wait_ge(c_dv, CD0 + 3 * NT)
            pe_attend(pe, nsa_steps)
            pe.wait_ge(o_acc, O_NSA)
            pe_project(pe, moba_jobs)
            pe.wait_ge(z_free, moba_jobs[-1]["at"] + 1)
            pe_attend(pe, moba_steps)
            modulate_late = range(8, 24)
            pe.wait_ge(t_ok, O_MOBA)
            modulate(modulate_late)
            pe.wait_ge(o_acc, O_MOBA)
            pe.matmul(bank[7][:, 510:512], ident[:, :], ident[:, 0:2], start=True, stop=True).then_inc(mod_a, 1)
            pe_out(pe, 0, "w_out", 0)
            pe.wait_ge(res_ok, ND)
            pe_norm(pe, 1)

            pe.wait_ge(b_in, 32)
            for m in range(16):
                mm = pe.transpose(bank[2][:, NEXP * m:NEXP * (m + 1)], b1_rows[:, P * m:P * (m + 1)],
                                  ident[0:NEXP, 0:NEXP])
            mm.then_inc(r_pe, 1)
            pe.wait_ge(h_ok, 2 * ND)
            pe.wait_ge(rt_in, 32)
            for i in range(NT):
                pe.matmul(bank[6][:, NEXP * i:NEXP * (i + 1)], ones[0:1, :], rb_row[0:1, :], start=True, stop=False)
                for k in range(ND):
                    mm = pe.matmul(bank[6][:, NEXP * i:NEXP * (i + 1)], hT[:, k, i * P:(i + 1) * P], rw[:, k, :],
                                   start=False, stop=(k == ND - 1))
            mm.then_inc(r_pe, 1)
            for i in range(NT):
                for a in range(2):
                    if i >= 1:
                        pe.wait_ge(h2_ok, 2 * (i - 1) + a + 1)
                    for k in range(4):
                        mm = pe.transpose(bank[4 + a][:, P * k:P * k + P], hT[:, 4 * a + k, i * P:(i + 1) * P], ident[:, :])
                    mm.then_inc(h2_t, 1)
            pe.wait_ge(sel_ok, 1)
            for i in range(NT):
                for j in range(i + 1):
                    mm = pe.matmul(bank[7][:, NEXP * i:NEXP * (i + 1)], (before_tok if j == i else ones)[:, :],
                                   sel[:, j, :], start=(j == 0), stop=(j == i))
            for j in range(NT):
                mm = pe.matmul(bank[7][:, NEXP * NT:NEXP * (NT + 1)], ones[:, :], sel[:, j, :],
                               start=(j == 0), stop=(j == NT - 1))
            mm.then_inc(r_pe, 1)
            pe.wait_ge(sel_ok, 2)
            for i in range(NT):
                mm = pe.transpose(bank[6][0:NEXP, i * P:(i + 1) * P], gates[:, i, :], ident[:, :])
            mm.then_inc(r_pe, 1)

            def indices(sg, e, n):
                pe.wait_ge(sg.hot, n)
                for i in range(NT):
                    r = route[:, i, bass.ds(e, 1), :].rearrange("p e c -> p (e c)")
                    mm = pe.matmul(bank[7][:, 0:4], onehot[:, i, :], r, start=(i == 0), stop=(i == NT - 1))
                mm.then_inc(sg.idx, 1)

            def turn_rows(sg, n):
                pe.wait_ge(sg.got, n)
                for a in range(2):
                    for k in range(4):
                        mm = pe.transpose(bank[5 + a][:, P * k:P * k + P], xg[:, P * (4 * a + k):P * (4 * a + k + 1)],
                                          ident[:, :])
                    mm.then_inc(sg.xt, 1)

            def first_layer(sg, n, wait_slot, used, middle=None):
                for j in range(8):
                    if j % 2 == 0:
                        wait_slot(j)
                        wait_slot(j + 1)
                    if j >= 2:
                        pe.wait_ge(sg.l, n + (j - 1))
                    for half in range(2):
                        w = ring[:, 2 * (j // 2) + half, :, :]
                        for k in range(ND):
                            mm = pe.matmul(bank[j % 2][:, CAP * half:CAP * half + CAP], w[:, k, P * (j % 2):P * (j % 2) + P],
                                           xgT[:, k, :], start=(k == 0), stop=(k == ND - 1))
                            if used and half == 0 and k == 0 and j % 2 == 0:
                                mm.then_inc(slot_used, 1)
                        if used and half == 0 and j % 2:
                            mm.then_inc(slot_used, 1)
                    mm.then_inc(sg.u, 1)
                    if j == 0 and middle:
                        middle()

            def second_layer(sg, n, wait_slot, used):
                for k in range(ND):
                    if k % 2 == 0:
                        wait_slot(8 + k // 2)
                    pe.wait_ge(sg.act, n + (k + 1))
                    w = ringf[:, (8 + k // 2) * 2048 + D * (k % 2):(8 + k // 2) * 2048 + D * (k % 2) + D]
                    for a in range(2):
                        mm = pe.matmul(bank[3 + a][:, :], actT[:, k, :], w[:, 512 * a:512 * a + 512],
                                       start=(k == 0), stop=(k == ND - 1))
                        if used and k % 2 == 0 and a == 0:
                            mm.then_inc(slot_used, 1)
                        if k == ND - 1:
                            mm.then_inc(sg.y, 1)

            FILLS = [fill_of(MOE0 + s) for s in range(SLOTS)]

            pe.wait_ge(gT_ok, 1)
            indices(main, 0, 1)
            turn_rows(main, 16)
            with pe.Fori(0, NEXP - 1) as b:
                def wait_slot(s):
                    pe.wait_ge(landed[s], b * 16 + 16 * FILLS[s])
                pe.wait_ge(main.xt_ok, b * 2 + 2)
                first_layer(main, b * 8, wait_slot, True, lambda: indices(main, b + 1, b + 2))
                turn_rows(main, b * 16 + 32)
                pe.wait_ge(main.y_ok, b * 2 + 2)
                second_layer(main, b * 8, wait_slot, True)

            def wait_slot(s):
                pe.wait_ge(landed[s], 16 * (NEXP - 1 + FILLS[s]))
            pe.wait_ge(main.xt_ok, 2 * NEXP)
            first_layer(main, 8 * (NEXP - 1), wait_slot, True)
            pe.wait_ge(main.y_ok, 2 * NEXP)
            second_layer(main, 8 * (NEXP - 1), wait_slot, True)
            pe.wait_ge(main.y_ok, 2 * NEXP + 2)
            slots_read(pe)
            pe.wait_ge(r_dv, 1)
            extra = pe.value_load(extra_i[0:1, 0:1], min_val=0, max_val=15)
            with pe.If(extra > 0):
                with pe.Fori(0, extra) as o:
                    pe.wait_ge(exp_ok, o + 1)
                    pe.sem_inc(waited_pe, 1)
                    e = pe.value_load(exp_i[0:1, 0:1], min_val=0, max_val=NEXP - 1)
                    indices(over, e, o + 1)
                    turn_rows(over, o * 16 + 16)
                    pe.wait_ge(over.xt_ok, o * 2 + 2)
                    pe.wait_ge(over_in, o * (16 * SLOTS) + 16 * SLOTS)
                    first_layer(over, o * 8, lambda s: None, False)
                    second_layer(over, o * 8, lambda s: None, False)
                    pe.wait_ge(over.y_ok, o * 2 + 4)
            pe.matmul(bank[2][:, 510:512], ident[:, :], ident[:, 0:2], start=True, stop=True).then_inc(over_done, 1)

            pe.wait_ge(gT_ok, 1)
            for t in range(ND):
                pe.matmul(bank[t][:, :], b2_keep[:, P * t:P * (t + 1)], gatesT, start=True, stop=False)
            for i in range(NT):
                pe.wait_ge(y_sum, i + 1)
                for t in range(ND):
                    mm = pe.matmul(bank[t][:, i * P:(i + 1) * P], y_rows[i % 2][:, 0, P * t:P * (t + 1)], ident[:, :],
                                   start=False, stop=(i == NT - 1))
                mm.then_inc(y_used, 1)

            pe.wait_ge(res_ok, 2 * ND)
            pe_norm(pe, 2)
            pe.wait_ge(h_ok, 3 * ND)
            pe_project(pe, da_jobs)
            pe.wait_ge(z_free, da_jobs[-1]["at"] + 1)
            pe_attend(pe, da_steps)
            pe.wait_ge(o_acc, O_DA)
            pe_project(pe, ret_jobs)
            pe.wait_ge(z_free, ret_jobs[-1]["at"] + 1)

            def ret_values(h):
                for i in range(NT):
                    for kt in range(NT):
                        if i == 0:
                            pe.wait_ge(rt_d, 4 * h + kt + 1)
                        if kt == 0 and h >= 1:
                            pe.wait_ge(rt_rd, 4 * (h - 1) + i + 1)
                        mm = pe.matmul(bank[4 + i][:, 0:P], ret_s[h % 2][:, kt, i * P:(i + 1) * P],
                                       vtok[:, kt, P * h:P * (h + 1)], start=(kt == 0), stop=(kt == NT - 1))
                    mm.then_inc(rt_pv, 1)
            for h in range(4):
                half = HD * (h % 2)
                for kt in range(NT):
                    if h >= 1:
                        pe.wait_ge(rt_d, 4 * (h - 1) + kt + 1)
                    pe.matmul(bank[kt][:, :], qkT[half:half + HD, 2 + h // 2, kt * P:(kt + 1) * P],
                              qkT[half:half + HD, h // 2, :], start=True, stop=True).then_inc(rt_s, 1)
                if h >= 1:
                    ret_values(h - 1)
            ret_values(3)
            pe.wait_ge(rt_m, 4)
            pe_out(pe, 1, "w_out_2", 2 * ND)
            pe.wait_ge(res_ok, 3 * ND)
            for i in range(NT):
                for a in range(2):
                    if i >= 1:
                        pe.wait_ge(f_ok, 2 * (i - 1) + a + 1)
                    for k in range(4):
                        mm = pe.transpose(bank[5 + a][:, P * k:P * k + P], resT[:, 4 * a + k, i * P:(i + 1) * P], ident[:, :])
                    mm.then_inc(f_t, 1)

        @block.vector
        def _(dve):
            count = [0]

            def link(ins):
                count[0] += 1
                ins.then_inc(dv, 1)
                dve.wait_ge(dv, count[0])

            def bc(ap, shape):
                return ap.to_broadcast(shape)

            dve.wait_ge(vec_t, 1)
            g2 = bank[0][:, 80:86].rearrange("p (a b) -> p a b", b=2)
            gv = gain.rearrange("p (a b) -> p a b", b=2)
            dve.tensor_scalar(gv[:, :, 0], g2[:, :, 0], -HD ** -0.5, None, ALU.mult)
            dve.tensor_copy(gv[:, :, 1], g2[:, :, 1])
            dve.tensor_copy(posT[:, :, :], bank[0][:, 96:96 + 2 * CMP_L].rearrange("p (k l) -> p k l", k=2))
            dve.tensor_copy(vecs[:, 0:80], bank[0][:, 0:80]).then_inc(vec_ok, 1)
            dve.wait_ge(silu_e, 1)
            link(dve.tensor_scalar(vecs[:, 88:96], vecs[:, 88:96], 1.0, None, ALU.add))
            link(dve.reciprocal(vecs[:, 88:96], vecs[:, 88:96]))
            dve.tensor_tensor(vecs[:, 80:88], vecs[:, 72:80], vecs[:, 88:96], ALU.mult).then_inc(silu_ok, 1)
            dve.wait_ge(dist_ok, 1)
            for h in range(HEADS):
                dve.tensor_scalar(bias8[:, h, :], work[:, 0, :], 2.0 ** -(h + 1), None, ALU.mult).then_inc(scaled_ok, 1)
            dve.wait_ge(mod_a, 1)
            link(dve.tensor_tensor(mod[:, 0:16], bank[5][:, 0:16], vecs[:, 0:16], ALU.add))
            dve.scalar_tensor_tensor(out=a1, in0=mod[:, 8:16], scalar=1.0, in1=vecs[:, 48:56],
                                     op0=ALU.add, op1=ALU.mult).then_inc(mod_ok, 1)
            dve.wait_ge(mod_ok, 1)
            dve_norm(dve, 0, a1, hs_ok)
            dve_project(dve, nsa_jobs)

            dve.wait_ge(z_free, nsa_jobs[-1]["at"] + 1)
            for kv in range(2):
                z = qkT[:, 6 + kv, :].rearrange("p (n l) -> p l n", l=CMP_STRIDE)
                dve.tensor_copy(cmp_in[kv][:, 0:16, 0:31], z[:, :, 0:31]).then_inc(c_dv, 1)
                dve.tensor_copy(cmp_in[kv][:, 16:32, 0:31], z[:, :, 1:32]).then_inc(c_dv, 1)
                dve.tensor_copy(cmp_in[kv][:, :, 31:32], posT[:, kv, :].rearrange("p (l a) -> p l a", a=1)).then_inc(c_dv, 1)
            dve.wait_ge(c_pe, 1)
            link(dve.memset(hid[:, :, :], 0.0))
            for m in range(4):
                ins = dve.tensor_scalar(hid[:, m, 0:31], bank[m][:, 0:31], bank[m][:, 31:32], None, ALU.add)
            link(ins)
            link(dve.tensor_tensor(hid_t[:, :, :], hid[:, :, :], hid[:, :, :], ALU.mult))
            link(dve.tensor_scalar(hid_t[:, :, :], hid_t[:, :, :], 0.044715, 1.0, ALU.mult, ALU.add))
            link(dve.tensor_tensor(hid_t[:, :, :], hid_t[:, :, :], hid[:, :, :], ALU.mult))
            dve.tensor_scalar(hid_t[:, :, :], hid_t[:, :, :], -50.0, None, ALU.max).then_inc(c_dv, 1)
            dve.wait_ge(c_ac, 1)
            link(dve.tensor_scalar(hid_t[:, :, :], hid_t[:, :, :], 1.0, None, ALU.add))
            link(dve.reciprocal(hid_t[:, :, :], hid_t[:, :, :]))
            link(dve.tensor_tensor(hid[:, :, :], hid[:, :, :], hid_t[:, :, :], ALU.mult))
            for r in range(4):
                ins = dve.tensor_copy(hid4[:, :, r, :], hid[:, 2:4, :])
            ins.then_inc(c_dv, 1)
            dve.wait_ge(c_pe, 2)
            kc = bank[4][0:CMP_N, 0:P]
            link(dve.tensor_copy(kc_n[:, :], kc))
            link(dve.tensor_tensor(kc_n[:, :], kc, kc_n[:, :], ALU.mult))
            dve.tensor_reduce(cs[0:CMP_N, 0, 0:2], kc_n[:, :].rearrange("p (g d) -> p g d", g=2), X, ALU.add).then_inc(c_dv, 1)
            dve.wait_ge(c_ac, 2)
            for g in range(2):
                ins = dve.tensor_scalar(kc_n[:, HD * g:HD * g + HD], kc[:, HD * g:HD * g + HD], cs[0:CMP_N, 0, g:g + 1],
                                        None, ALU.mult)
            ins.then_inc(c_dv, 1)
            link(dve.memset(vc_diag, 0.0))
            for g in range(2):
                for h in range(4):
                    ins = dve.tensor_copy(vc_diag[CMP_N * h:CMP_N * (h + 1), g, HD * h:HD * h + HD],
                                          bank[5][CMP_N * h:CMP_N * (h + 1), HD * g:HD * g + HD])
            ins.then_inc(c_dv, 1)
            dve.wait_ge(c_pe, 3)
            dve.tensor_scalar(kcT[:, :], bank[6][:, 0:CMP_N], gain[:, 1:2], None, ALU.mult).then_inc(c_dv, 1)
            dve.wait_ge(dist_ok, 2)
            for h in range(HEADS):
                dve.tensor_scalar(cmp_bias[:, :, h, :], cmp_bias[:, :, h, :], 0.5 * 2.0 ** -(h + 1), None,
                                  ALU.mult).then_inc(scaled_ok, 1)
            dve.wait_ge(bias_ok, 2 * HEADS)
            for i in range(NT):
                dve.wait_ge(c_pe, CP0 + 3 * i + 1)
                for g in range(2):
                    ins = dve.tensor_tensor(cmp_s[:, 4 * g:4 * g + 4, :],
                                            bank[g][:, 0:4 * CMP_N].rearrange("p (h n) -> p h n", n=CMP_N),
                                            cmp_bias[:, i, 4 * g:4 * g + 4, :], ALU.add)
                link(ins)
                link(dve.tensor_reduce(cs[:, 1, :], cmp_s, X, ALU.min))
                dve.tensor_tensor(cmp_s, cmp_s, bc(cs[:, 1, :].unsqueeze(2), [P, HEADS, CMP_N]), ALU.subtract).then_inc(c_dv, 1)
                dve.wait_ge(c_ac, 2 + 2 * i + 1)
                link(dve.tensor_reduce(cs[:, 2, :], cmp_s, X, ALU.add))
                link(dve.reciprocal(cs[:, 2, :], cs[:, 2, :]))
                link(dve.tensor_tensor(cs[:, 3, :], nsa_gate[:, i, 0:24:3], cs[:, 2, :], ALU.mult))
                link(dve.tensor_scalar(cs[:, 3, :], cs[:, 3, :], row_ok[:, i:i + 1], None, ALU.mult))
                dve.tensor_tensor(cmp_s, cmp_s, bc(cs[:, 3, :].unsqueeze(2), [P, HEADS, CMP_N]), ALU.mult).then_inc(c_dv, 1)
                dve.wait_ge(c_pe, CP0 + 3 * i + 3)
                dve.tensor_copy(omix[:, i, 0:512], bank[3][:, :]).then_inc(c_dv, 1)

            dve.wait_ge(c_dv, CD0 + 3 * NT)
            dve_attend(dve, link, nsa_steps)
            dve_project(dve, moba_jobs)
            dve_attend(dve, link, moba_steps)
            dve.wait_ge(mod_a, 2)
            link(dve.tensor_tensor(mod[:, 16:48], bank[5][:, 16:48], vecs[:, 16:48], ALU.add))
            dve.scalar_tensor_tensor(out=a2, in0=mod[:, 32:40], scalar=1.0, in1=vecs[:, 56:64],
                                     op0=ALU.add, op1=ALU.mult).then_inc(mod_ok, 1)
            dve.wait_ge(mod_ok, 2)
            dve_out(dve, 0, mod[:, 16:24], 0)
            dve_norm(dve, 1, a2, hs_ok)

            dve.wait_ge(r_pe, 1)
            bv = bank[2][:, :].rearrange("p (m e) -> p e m", e=NEXP)
            dve.tensor_copy(b1T[:, :, 0:8], bv[:, :, 0:8])
            link(dve.tensor_scalar(b1T[:, :, 8:16], bv[:, :, 8:16], 1.0, None, ALU.add))

            dve.wait_ge(r_pe, 2)
            link(dve.tensor_copy(lg, bank[6][:, 0:NT * NEXP].rearrange("p (i e) -> p i e", e=NEXP)))
            for i in range(NT):
                ins = dve.max(m8[:, i, :], lg[:, i, :])
            link(ins)
            link(dve.tensor_scalar(m8[:, :, 7:8], m8[:, :, 0:1], -1.0, None, ALU.mult))
            thr = bc(m8[:, :, TOPK - 1:TOPK], [P, NT, NEXP])
            link(dve.tensor_tensor(sel, lg, thr, ALU.is_gt))
            dve.tensor_tensor(lt, lg, thr, ALU.is_equal).then_inc(lg_ok, 1)
            dve.wait_ge(lg_ok, 1)
            link(dve.tensor_reduce(m8[:, :, 6:7], sel, X, ALU.add))
            link(dve.tensor_scalar(m8[:, :, 6:7], m8[:, :, 6:7], -1.0, float(TOPK), ALU.mult, ALU.add))
            for i in range(NT):
                ins = dve.tensor_tensor_scan(posm[:, i, :], ones[:, 0:NEXP], lt[:, i, :], 0.0, ALU.mult, ALU.add)
            link(ins)
            link(dve.tensor_tensor(posm, posm, bc(m8[:, :, 6:7], [P, NT, NEXP]), ALU.is_le))
            link(dve.tensor_tensor(posm, posm, lt, ALU.mult))
            dve.tensor_tensor(sel, sel, posm, ALU.add).then_inc(sel_ok, 1)
            dve.wait_ge(sel_ok, 1)
            dve.wait_ge(r_ac, NT)
            link(dve.tensor_tensor(gates, gates, sel, ALU.mult))
            link(dve.tensor_reduce(m8[:, :, 5:6], gates, X, ALU.add))
            link(dve.reciprocal(m8[:, :, 5:6], m8[:, :, 5:6]))
            dve.tensor_tensor(gates, gates, bc(m8[:, :, 5:6], [P, NT, NEXP]), ALU.mult).then_inc(sel_ok, 1)
            dve.wait_ge(sel_ok, 2)
            for i in range(NT):
                ins = dve.tensor_tensor_scan(lt[:, i, :], ones[:, 0:NEXP], sel[:, i, :], 0.0, ALU.mult, ALU.add)
            link(ins)
            tb = bc(tok_id.unsqueeze(2), [P, NT, NEXP])
            dve.tensor_copy(route[:, :, :, 0], tb)
            link(dve.scalar_tensor_tensor(out=route[:, :, :, 1], in0=tb, scalar=float(TOPK), in1=lt,
                                          op0=ALU.mult, op1=ALU.add))
            dve.tensor_scalar(route[:, :, :, 1], route[:, :, :, 1], -1.0, None, ALU.add)
            dve.tensor_copy(route[:, :, :, 2], gates)
            link(dve.memset(route[:, :, :, 3], 1.0))
            dve.wait_ge(r_pe, 3)
            link(dve.scalar_tensor_tensor(out=posm, in0=bank[7][:, 0:NT * NEXP].rearrange("p (i e) -> p i e", e=NEXP),
                                          scalar=1.0, in1=sel, op0=ALU.add, op1=ALU.mult))
            dve.tensor_scalar(posm, posm, -1.0, None, ALU.add)
            link(dve.tensor_copy(cnt[:, 0, :], bank[7][:, NT * NEXP:(NT + 1) * NEXP]))
            link(dve.tensor_scalar(cnt[:, 1, :], cnt[:, 0, :], float(CAP), None, ALU.is_gt))
            for m in (2, 3):
                link(dve.scalar_tensor_tensor(out=cnt[:, 1, :], in0=cnt[:, 0, :], scalar=float(CAP * m), in1=cnt[:, 1, :],
                                              op0=ALU.is_gt, op1=ALU.add))
            link(dve.tensor_tensor_scan(cnt[:, 2, :], ones[:, 0:NEXP], cnt[:, 1, :], 0.0, ALU.mult, ALU.add))
            dve.tensor_scalar(neg_junk, junk, -1.0, None, ALU.mult)
            dve.memset(o_cell[:, 0:1], 0.0)
            dve.tensor_copy(extra_i[0:1, 0:1], cnt[0:1, 2, NEXP - 1:NEXP]).then_inc(r_dv, 1)
            dve.wait_ge(r_dv, 1)
            dve.wait_ge(r_pe, 4)
            dve.tensor_copy(gatesT, bank[6][0:NEXP, :]).then_inc(gT_ok, 1)
            dve.wait_ge(gT_ok, 1)

            def who(sg, e, base):
                for i in range(NT):
                    ins = dve.tensor_scalar(onehot[:, i, :], base, posm[:, i, bass.ds(e, 1)], None, ALU.is_equal)
                ins.then_inc(sg.hot, 1)

            def sources(sg, n):
                dve.wait_ge(sg.idx, n)
                link_in(dve.tensor_copy(meta[:, :], bank[7][:, 0:4]))
                dve.tensor_copy(src_i[:, :], meta[:, 0:1]).then_inc(sg.idx_ok, 1)

            steps = [0]

            def link_in(ins):
                dve.drain()
                return ins

            def targets(sg):
                dve.tensor_copy(meta_c[:, :], meta[:, :])
                dve.drain()
                dve.tensor_scalar(dst_n[:, :], meta_c[:, 3:4], neg_junk, junk, ALU.mult, ALU.add)
                dve.drain()
                dve.tensor_tensor(dst_i[:, :], dst_n[:, :], meta_c[:, 1:2], ALU.add).then_inc(sg.dst, 1)

            def pair_in(sg, n, j):
                dve.wait_ge(sg.u, n + (j + 1))
                if j >= 2:
                    dve.wait_ge(sg.act, n + (j - 1))
                dve.tensor_scalar(g_t[:, j % 2, :], bank[j % 2][:, 0:CAP], b1c[:, j:j + 1], LIMIT,
                                  ALU.add, ALU.min).then_inc(sg.g, 1)
                dve.tensor_scalar(l_t[:, j % 2, :], bank[j % 2][:, CAP:2 * CAP], b1c[:, 8 + j:9 + j], 1.0 - LIMIT,
                                  ALU.add, ALU.max).then_inc(sg.l, 1)

            def pair_out(sg, n, j):
                dve.wait_ge(sg.sig, n + (j + 1))
                dve.tensor_tensor(s_t[:, j % 2, :], s_t[:, j % 2, :], g_t[:, j % 2, :], ALU.mult)
                dve.drain()
                dve.scalar_tensor_tensor(out=actT[:, j, :], in0=l_t[:, j % 2, :], scalar=1.0 + LIMIT,
                                         in1=s_t[:, j % 2, :], op0=ALU.min, op1=ALU.mult).then_inc(sg.act, 1)

            def biases(e):
                dve.tensor_copy(b1c[:, :], b1T[:, bass.ds(e, 1), :].rearrange("p e m -> p (e m)"))
                dve.drain()

            who(main, 0, iota_c[:, :])
            sources(main, 1)
            with dve.Fori(0, NEXP - 1) as b:
                biases(b)
                who(main, b + 1, iota_c[:, :])
                for j in range(8):
                    pair_in(main, b * 8, j)
                    if j >= 1:
                        pair_out(main, b * 8, j - 1)
                    if j == 3:
                        dve.wait_ge(main.y_ok, b * 2 + 2)
                        dve.wait_ge(main.free, b + 1)
                        targets(main)
                        dve.drain()
                        dve.wait_ge(main.got, b * 16 + 16)
                        sources(main, b + 2)
                pair_out(main, b * 8, 7)
            biases(NEXP - 1)
            dve.wait_ge(main.y_ok, 2 * NEXP)
            dve.wait_ge(main.free, NEXP)
            targets(main)
            for j in range(8):
                pair_in(main, 8 * (NEXP - 1), j)
                if j >= 1:
                    pair_out(main, 8 * (NEXP - 1), j - 1)
            pair_out(main, 8 * (NEXP - 1), 7)
            dve.wait_ge(main.free, NEXP + 1)
            extra = dve.value_load(extra_i[0:1, 0:1], min_val=0, max_val=15)
            with dve.If(extra > 0):
                with dve.Fori(0, extra) as o:
                    dve.wait_ge(over.free, o + 1)
                    dve.tensor_scalar(cnt[:, 3, :], cnt[:, 2, :], o_cell[:, 0:1], None, ALU.is_le)
                    dve.drain()
                    dve.tensor_reduce(o_cell[:, 1:2], cnt[:, 3, :], X, ALU.add)
                    dve.tensor_tensor(cnt[:, 3, :], cnt[:, 3, :], cnt[:, 1, :], ALU.mult)
                    dve.drain()
                    dve.tensor_reduce(o_cell[:, 2:3], cnt[:, 3, :], X, ALU.add)
                    dve.drain()
                    dve.tensor_tensor(o_cell[:, 3:4], o_cell[:, 0:1], o_cell[:, 2:3], ALU.subtract)
                    dve.drain()
                    dve.tensor_scalar(o_cell[:, 3:4], o_cell[:, 3:4], 1.0, float(CAP), ALU.add, ALU.mult)
                    dve.drain()
                    dve.tensor_scalar(iota_b[:, :], iota_c[:, :], o_cell[:, 3:4], None, ALU.add)
                    dve.tensor_scalar(o_cell[:, 0:1], o_cell[:, 0:1], 1.0, None, ALU.add)
                    dve.tensor_copy(exp_i[0:1, 0:1], o_cell[0:1, 1:2]).then_inc(exp_ok, 1)
                    dve.wait_ge(exp_ok, o + 1)
                    dve.sem_inc(waited_dve, 1)
                    e = dve.value_load(exp_i[0:1, 0:1], min_val=0, max_val=NEXP - 1)
                    biases(e)
                    who(over, e, iota_b[:, :])
                    sources(over, o + 1)
                    dve.drain()
                    targets(over)
                    for j in range(8):
                        pair_in(over, o * 8, j)
                        if j >= 1:
                            pair_out(over, o * 8, j - 1)
                    pair_out(over, o * 8, 7)
            for i in range(NT):
                y = y_rows[i % 2]
                dve.wait_ge(y_in[i % 2], 16 * (i // 2 + 1))
                link(dve.tensor_tensor(y[:, 0:2, :], y[:, 0:2, :], y[:, 2:4, :], ALU.add))
                dve.tensor_tensor(y[:, 0, :], y[:, 0, :], y[:, 1, :], ALU.add).then_inc(y_sum, 1)
            dve.wait_ge(y_used, NT)
            for t in range(ND):
                dve.scalar_tensor_tensor(out=resT[:, t, :], in0=bank[t][:, :], scalar=mod[:, 40 + t:41 + t],
                                         in1=resT[:, t, :], op0=ALU.mult, op1=ALU.add).then_inc(res_ok, 1)

            dve.wait_ge(lam_in, 7 * 16)
            for m in range(2):
                dve.tensor_tensor_reduce(out=lam_rows[:, 2 * m, :], in0=lam_rows[:, 2 * m, :], in1=lam_rows[:, 2 * m + 1, :],
                                         scale=1.0, scalar=0.0, op0=ALU.mult, op1=ALU.add, accum_out=lam[:, m:m + 1])
            dve.tensor_scalar(subln[:, :], subln[:, :], 1.0 - LAMBDA_INIT, None, ALU.mult)
            link(dve.tensor_scalar(lgam[:, 1, :], lgam[:, 0, :], -1.0, None, ALU.mult))
            dve.tensor_tensor(lgam[:, 1, :], lgam[:, 0, :], lgam[:, 1, :], ALU.max).then_inc(g_dv, 1)
            dve.wait_ge(g_ac, 2)
            link(dve.tensor_scalar(lam[:, 4:5], lam[:, 2:3], lam[:, 3:4], LAMBDA_INIT, ALU.subtract, ALU.add))
            dve.tensor_scalar(lam[:, 5:6], lam[:, 4:5], -1.0, None, ALU.mult)
            link(dve.tensor_scalar(lgam[:, 3, :], lgam[:, 2, :], 1.0, None, ALU.add))
            dve.tensor_scalar(lgam[:, 5, :], lgam[:, 3, :], 1.0, None, ALU.is_equal)
            link(dve.tensor_scalar(lgam[:, 3, :], lgam[:, 3, :], -1.0, 1e-30, ALU.add, ALU.max))
            link(dve.reciprocal(lgam[:, 3, :], lgam[:, 3, :]))
            link(dve.tensor_tensor(lgam[:, 3, :], lgam[:, 2, :], lgam[:, 3, :], ALU.mult))
            link(dve.tensor_tensor(lgam[:, 3, :], lgam[:, 3, :], lgam[:, 4, :], ALU.mult))
            link(dve.tensor_tensor(lgam[:, 5, :], lgam[:, 5, :], lgam[:, 2, :], ALU.mult))
            link(dve.tensor_tensor(lgam[:, 3, :], lgam[:, 3, :], lgam[:, 5, :], ALU.add))
            link(dve.scalar_tensor_tensor(out=lgam[:, 7, :], in0=lgam[:, 0, :], scalar=0.0, in1=lgam[:, 3, :],
                                          op0=ALU.min, op1=ALU.subtract))
            dve_norm(dve, 2, vecs[:, 64:72], h_ok)
            dve.wait_ge(dist_ok, 3)
            link(dve.tensor_scalar(bias4[:, 1, :], bias4[:, 0, :], -1.0, None, ALU.mult))
            link(dve.tensor_tensor(bias4[:, 0, :], bias4[:, 0, :], bias4[:, 1, :], ALU.max))
            for h in (3, 2, 1, 0):
                ins = dve.tensor_scalar(bias4[:, h, :], bias4[:, 0, :], 4.0 ** -(h + 1), None, ALU.mult)
            link(ins)
            dve_project(dve, da_jobs)
            dve_attend(dve, link, da_steps)
            dve.wait_ge(o_acc, O_DA)
            for i in range(NT):
                o4 = omix[:, i, 0:512].rearrange("p (h d) -> p h d", h=4)
                t4 = work[:, 0, :].rearrange("p (h d) -> p h d", h=4)
                link(dve.tensor_tensor(t4, o4, o4, ALU.mult))
                dve.tensor_reduce(ms[:, :], t4, X, ALU.add).then_inc(rt_f, 1)
                dve.wait_ge(rt_o, i + 1)
                link(dve.tensor_tensor(o4, o4, bc(ms[:, :].unsqueeze(2), [P, 4, P]), ALU.mult))
                link(dve.tensor_tensor(o4, o4, bc(subln[:, :].unsqueeze(1), [P, 4, P]), ALU.mult))
                link(dve.tensor_tensor(omix[:, i, 0:512], omix[:, i, 0:512], gtok[:, i, :], ALU.mult))
            dve_project(dve, ret_jobs)
            dve.wait_ge(dist_ok, 4)
            for h in range(4):
                d2 = decay[:, h, :].rearrange("p (a b) -> p a b", a=2)
                dve.tensor_scalar(d2, ret_dist, 0.0, lgam[:, 7, h:h + 1], ALU.max, ALU.mult)
                link(dve.tensor_scalar(ret_tmp, ret_dist, 0.0, lgam[:, 7, 4 + h:5 + h], ALU.min, ALU.mult))
                dve.tensor_tensor(d2, d2, ret_tmp, ALU.subtract).then_inc(g_dv, 1)
                dve.wait_ge(g_dv, 2 + h)

            def decayed(h):
                dve.wait_ge(g_ac, 3 + h)
                for kt in range(NT):
                    dve.wait_ge(rt_s, 4 * h + kt + 1)
                    if h >= 2:
                        dve.wait_ge(rt_pv, 4 * (h - 1))
                    dve.tensor_tensor(ret_s[h % 2][:, kt, :], bank[kt][:, :],
                                      decay[:, h, 384 - P * kt:384 - P * kt + S], ALU.mult).then_inc(rt_d, 1)

            def ret_norm(h):
                oh = omix[:, :, 512 + P * h:512 + P * (h + 1)]
                for i in range(NT):
                    dve.wait_ge(rt_pv, 4 * h + i + 1)
                    dve.tensor_copy(oh[:, i, :], bank[4 + i][:, 0:P]).then_inc(rt_rd, 1)
                dve.wait_ge(rt_rd, 4 * (h + 1))
                t4 = hT[:, 0, :].rearrange("p (i d) -> p i d", i=NT)
                link(dve.tensor_tensor(t4, oh, oh, ALU.mult))
                dve.tensor_reduce(ms[:, :], t4, X, ALU.add).then_inc(rt_f, 1)
                dve.wait_ge(rt_o, NT + h + 1)
                link(dve.tensor_tensor(oh, oh, bc(ms[:, :].unsqueeze(2), [P, NT, P]), ALU.mult))
                dve.tensor_tensor(oh, oh, gtok[:, :, P * h:P * (h + 1)], ALU.mult).then_inc(rt_m, 1)
            for h in range(5):
                if h < 4:
                    decayed(h)
                if h >= 1:
                    ret_norm(h - 1)
            dve_out(dve, 1, None, 2 * ND)


_INS = ["x", "c", "ada_w", "ada_b", "ln1_g", "ln2_g", "w_in", "nsa_q_gain", "nsa_k_gain", "nsa_cmp_pos",
        "nsa_cmp_w1", "nsa_cmp_w2", "moba_q_gain", "moba_k_gain", "w_out", "router_w", "router_b",
        "exp_w1", "exp_b1", "exp_w2", "exp_b2", "norm_w_2", "w_in_2", "q_norm_w_2", "k_norm_w_2",
        "lambda_q1_2", "lambda_k1_2", "lambda_q2_2", "lambda_k2_2", "subln_w_2",
        "ret_decay_fwd_2", "ret_decay_bwd_2", "w_out_2"]


def kernel(**inputs):
    import numpy as _np
    import concourse.bacc as _bacc
    from concourse.bass_utils import run_bass_kernel_spmd as _run

    nc = _bacc.Bacc("TRN2", target_bir_lowering=False, num_devices=1)
    arrays, args = {}, []
    for name in _INS:
        a = _np.ascontiguousarray(inputs[name])
        arrays[f"in_{name}_dram"] = a
        args.append(nc.dram_tensor(f"in_{name}_dram", a.shape, mybir.dt.from_np(a.dtype), kind="ExternalInput").ap())
    args.append(nc.dram_tensor("out_0_dram", (1, S, D), F32, kind="ExternalOutput").ap())
    two_block_layer(nc, *args)
    r = _run(nc, [arrays], core_ids=[0])
    return r.results[0]["out_0_dram"]
```

```python
from contextlib import ExitStack

import concourse.bass as bass
from concourse import mybir

F32 = mybir.dt.float32
I32 = mybir.dt.int32
U32 = mybir.dt.uint32
ALU = mybir.AluOpType
ACT = mybir.ActivationFunctionType
X = mybir.AxisListType.X

P = 128
S = 512
D = 1024
NT = S // P
ND = D // P
EPS = 1e-6
NEG = 1e30
HD = 64
HEADS = 8
CMP_N = 32
CMP_L, CMP_STRIDE = 32, 16
NEXP, TOPK, FF = 32, 4, 1024
CAP = 128
SLOTS = 12
SW = 256
FIRST_SLOT = 7
JUNK = S
EARLY = 8
ALPHA, LIMIT = 1.702, 7.0
LAMBDA_INIT = 0.2


def chunk_plan():
    plan = [("ada", i, 1) for i in range(EARLY)]
    plan += [("kv_cmp", 0, 1), ("q_nsa", 0, 1), ("q_nsa", 1, 1), ("kv_slc", 0, 1), ("kv_win", 0, 1)]
    plan += [("cmp_w1", 0, 1), ("cmp_w1", 1, 1)]
    plan += [("ada", i, 1) for i in range(EARLY, 24)]
    plan += [("q_moba", i, 1) for i in range(2)] + [("k_moba", i, 1) for i in range(2)]
    plan += [("v_moba", i, 1) for i in range(2)]
    plan += [("w_out", i, 1) for i in range(4)]
    at, before = FIRST_SLOT, {}
    for name, part, n in plan:
        before[name, part] = at
        at += n
    moe = at
    assert moe % SLOTS == 0
    after = [("w_in_2", i, 1) for i in range(14)] + [("w_out_2", i, 1) for i in range(4)]
    at = moe + SLOTS * NEXP
    for name, part, n in after:
        before[name, part] = at
        at += n
    return plan, after, before, moe


def two_block_layer(nc, x, vec_rows_in, misc_in, ada_w, w_in, nsa_cmp_pos, nsa_cmp_w1, nsa_cmp_w2, w_out, router_w,
                    exp_w1, exp_b1, exp_w2, exp_b2, w_in_2, w_out_2, out):
    PLAN, AFTER, PLACE, MOE0 = chunk_plan()

    h2_dram = nc.dram_tensor("h2_rows", (S, D), F32, kind="Internal").ap()
    y_dram = nc.dram_tensor("expert_sums", (JUNK + CAP, D), F32, kind="Internal").ap()

    with ExitStack() as ctx:
        def sb(name, shape, dt=F32):
            return ctx.enter_context(nc.sbuf_tensor(name, shape, dt))

        def sem(name):
            return ctx.enter_context(nc.semaphore(name))

        bank = [ctx.enter_context(nc.psum_tensor(f"bank{i}", [P, 512], F32)) for i in range(8)]

        ring = sb("ring", [P, SLOTS, 8, SW])
        ringf = ring[:, :, :, :].rearrange("p s k c -> p (s k c)")
        resT = sb("resT", [P, ND, S])
        hT = sb("hT", [P, ND, S])
        ident = sb("ident", [P, P])
        ones = sb("ones", [P, P])
        head_mean = sb("head_mean", [P, P])
        before_tok = sb("before_tok", [P, P])
        iota_c = sb("iota_c", [P, P])
        vecs = sb("vecs", [P, 96])
        mod = sb("mod", [P, 48])
        small = sb("small", [P, 64])
        ARENA = 18432
        arena = sb("arena", [P, ARENA])

        def room(at, shape, parts=P):
            n = 1
            for s in shape:
                n *= s
            assert at + n <= ARENA, (at, shape)
            ap = arena[0:parts, at:at + n]
            if len(shape) == 1:
                return ap
            if len(shape) == 2:
                return ap.rearrange("p (a b) -> p a b", b=shape[1])
            return ap.rearrange("p (a b c) -> p a b c", b=shape[1], c=shape[2])

        qkT = room(0, [8, S])
        vtok = room(4096, [NT, S])
        gtok = room(6144, [NT, S])
        OM = 8192
        omix = room(OM, [NT, D])
        x_rows = omix
        rows_out = omix
        BI = OM + 4096
        bias8 = room(BI, [HEADS, S])
        bias4 = room(BI, [4, 896])
        decay = room(BI, [4, 896])
        WK = BI + 4096
        work = room(WK, [4, S])
        biased = [work[:, 0, :], work[:, 1, :]]
        probT = [work[:, 2, :], work[:, 3, :]]
        sq = [work[:, 0, :], work[:, 1, :]]
        rr = [work[:, 2, :], work[:, 3, :]]
        cmp_in = [room(6144, [16, 2 * CMP_N]), room(7168, [16, 2 * CMP_N])]
        cmp_bias = room(6144, [2 * NT * 4, CMP_N])
        cmp_s = room(7168, [2 * NT * 4, CMP_N])
        cmp_pT = room(WK + 1024, [2, S])
        vc_diag = qkT[:, 6, :].rearrange("p (g c) -> p g c", g=2)
        ada_sum = ([room(6144 + SW * n, [SW]) for n in range(8)] +
                   [omix[:, n // 2, 512 + SW * (n % 2):512 + SW * (n % 2 + 1)] for n in range(8)])
        hid = room(WK, [4, CMP_N])
        hid4 = room(WK + 128, [2, 4, CMP_N])
        hid_t = room(WK + 384, [4, CMP_N])
        posT = sb("posT", [P, 2, CMP_L // 2])
        cw2 = sb("cw2", [P, 2, HD])
        kcT = room(WK + 512, [CMP_N])
        kc_n = room(WK + 640, [P], CMP_N)
        gate_w = room(OM + 2048, [8, 24])
        kv_turned = [room(OM, [S]), room(OM + 512, [S])]
        nsa_gate = sb("nsa_gate", [P, NT, 24])
        xg = room(0, [D])
        xgT = room(1024, [ND, CAP])
        actT = room(2048, [ND, CAP])
        ybuf = room(3072, [D])
        onehot = room(4096, [NT, CAP])
        route = room(4608, [NT, NEXP, 4])
        b1T = room(5120, [NEXP, 16])
        g_t = room(5632, [2, CAP])
        s_t = room(5888, [2, CAP])
        l_t = room(6144, [2, CAP])
        sel = room(6400, [NT, NEXP])
        posm = room(6528, [NT, NEXP])
        gates = room(6656, [NT, NEXP])
        lg = room(6784, [NT, NEXP])
        lt = room(6912, [NT, NEXP])
        cnt = room(7040, [4, NEXP])
        gatesT = room(7168, [S], NEXP)
        b1_rows = room(OM + 1024, [2 * FF], NEXP)
        y_rows = [room(D * i, [D]) for i in range(NT)]
        rw = room(OM + 3072, [ND, NEXP])
        b2_keep = room(OM, [D], NEXP)
        h2_rows = room(BI, [NT, D])
        vec_rows = room(WK + 512, [P], 86)
        pos_rows = room(WK + 1024, [2 * P], CMP_L // 2)
        ret_s = [work, qkT[:, 4:8, :]]
        ret_dist = omix[:, 2:4, 512:960]
        ret_tmp = omix[:, 0:2, 512:960]
        m8 = sb("m8", [P, NT, 8])
        b1c = sb("b1c", [P, 16])
        meta = sb("meta", [P, 4])
        meta_c = sb("meta_c", [P, 4])
        iota_b = room(7680, [CAP])
        src_i = sb("src_i", [P, 1], U32)
        dst_i = sb("dst_i", [P, 1], U32)
        dst_n = sb("dst_n", [P, 1])
        extra_i = sb("extra_i", [1, 1], I32)
        exp_i = sb("exp_i", [1, 1], I32)
        mn = sb("mn", [P, 4])
        ls = sb("ls", [P, 4])
        cf = sb("cf", [P, 4])
        cs = sb("cs", [P, 4, 32])
        MISC = 4 * HD + P + 8 + NEXP
        misc = sb("misc", [P, MISC])
        lam_rows = misc[:, 0:4 * HD].rearrange("p (a b) -> p a b", b=HD)
        subln = misc[:, 4 * HD:4 * HD + P]
        ret_decays = misc[:, 4 * HD + P:4 * HD + P + 8]
        rb_row = misc[0:1, 4 * HD + P + 8:MISC]
        lgam = sb("lgam", [P, 8, 8])
        ms = sb("ms", [P, 4])

        eps_c, tok_c, junk_c, valid_c = 0, 1, 5, 6
        a1_c, g_c, a2_c, lam_c, o_c = 10, 18, 24, 32, 40
        tok_id = small[:, tok_c:tok_c + NT]
        junk = small[:, junk_c:junk_c + 1]
        row_ok = small[:, valid_c:valid_c + NT]
        a1, a2 = small[:, a1_c:a1_c + 8], small[:, a2_c:a2_c + 8]
        gain = small[:, g_c:g_c + 6]
        lam = small[:, lam_c:lam_c + 6]
        o_cell = small[:, o_c:o_c + 4]
        neg_junk = small[:, 44:45]
        eps = small[:, eps_c:eps_c + 1]

        landed = [sem(f"landed{s}") for s in range(SLOTS)]
        ada_read, ada_done = sem("ada_read"), sem("ada_done")
        slot_used = sem("slot_used")
        vec_in, x_in, gate_in, small_in = sem("vec_in"), sem("x_in"), sem("gate_in"), sem("small_in")
        q_in = sem("q_in")
        rt_in, lam_in, b_in = sem("rt_in"), sem("lam_in"), sem("b_in")
        pool_c = sem("pool_c")
        consts = sem("consts")
        dv = sem("dv")
        ac = sem("ac")
        vec_t, vec_ok = sem("vec_t"), sem("vec_ok")
        xt_t, xt_ok = sem("xt_t"), sem("xt_ok")
        silu_e, silu_ok = sem("silu_e"), sem("silu_ok")
        mod_a, mod_ok = sem("mod_a"), sem("mod_ok")
        sq_ok, sum_ok, rstd_ok, hs_ok, h_ok = sem("sq_ok"), sem("sum_ok"), sem("rstd_ok"), sem("hs_ok"), sem("h_ok")
        z_done, z_sq, z_mean, z_r, z_free = sem("z_done"), sem("z_sq"), sem("z_mean"), sem("z_r"), sem("z_free")
        dist_ok, scaled_ok, bias_ok = sem("dist_ok"), sem("scaled_ok"), sem("bias_ok")
        s_done, s_bias, s_exp, t_done, t_ok, o_done, o_acc = (
            sem(n) for n in ("s_done", "s_bias", "s_exp", "t_done", "t_ok", "o_done", "o_acc"))
        c_in, c_pe, c_dv, c_ac = sem("c_in"), sem("c_pe"), sem("c_dv"), sem("c_ac")
        mixT_t, mixT_ok, out_t, res_ok = sem("mixT_t"), sem("mixT_ok"), sem("out_t"), sem("res_ok")
        r_pe, r_dv, r_ac, h2_t, h2_ok, h2_out = (
            sem(n) for n in ("r_pe", "r_dv", "r_ac", "h2_t", "h2_ok", "h2_out"))

        class BlockSignals:
            def __init__(self, n):
                self.hot, self.idx, self.idx_ok, self.got, self.xt, self.xt_ok = (
                    sem(n + w) for w in ("hot", "idx", "idx_ok", "got", "xt", "xt_ok"))
                self.u, self.g, self.sig, self.act, self.y, self.y_ok, self.put = (
                    sem(n + w) for w in ("u", "g", "sig", "act", "y", "y_ok", "put"))
                self.free, self.dst, self.l = sem(n + "free"), sem(n + "dst"), sem(n + "l")
        main, over = BlockSignals("m_"), BlockSignals("o_")
        waited_sp, waited_pe, waited_dve, waited_pool = (sem("waited_" + n) for n in ("sp", "pe", "dve", "pool"))
        exp_ok, over_done, over_in, over_used = sem("exp_ok"), sem("over_done"), sem("over_in"), sem("over_used")
        y_in = [sem(f"y_in{i}") for i in range(NT)]
        y_zero, turned = sem("y_zero"), sem("turned")
        y_sum, y_t, y_used = sem("y_sum"), sem("y_t"), sem("y_used")
        f_t, f_ok, f_out = sem("f_t"), sem("f_ok"), sem("f_out")
        g_pe, g_dv, g_ac = sem("g_pe"), sem("g_dv"), sem("g_ac")
        rt_s, rt_d, rt_o, rt_f = sem("rt_s"), sem("rt_d"), sem("rt_o"), sem("rt_f")
        rt_pv, rt_rd, rt_m = sem("rt_pv"), sem("rt_rd"), sem("rt_m")
        lg_ok, sel_ok, gT_ok = sem("lg_ok"), sem("sel_ok"), sem("gT_ok")
        C_LAID, C_CUBE, C_HID, C_SQ, C_KN, C_VD, C_KT, C_S, C_P, C_O = 1, 2, 3, 4, 5, 6, 7, 8, 10, 15

        last_of, reads, by_pe, by_dve = {}, {}, 0, 0
        for name, part, _ in PLAN:
            if name == "ada" and part >= EARLY:
                by_dve += 1
            else:
                by_pe += 1
            reads[PLACE[name, part]] = -by_dve if name == "ada" and part >= EARLY else by_pe
        USED0 = by_pe
        for name, part, _ in PLAN:
            last_of[PLACE[name, part]] = reads.get(PLACE[name, part] - SLOTS, 0)
        for n, (name, part, _) in enumerate(AFTER):
            last_of[PLACE[name, part]] = USED0 + SLOTS * (NEXP - 1) + n + 1

        def slot(n):
            return n % SLOTS

        def fill_of(n):
            return (n - slot(n)) // SLOTS + (0 if slot(n) < FIRST_SLOT else 1)

        def arrived(eng, name, part=0, slots=1):
            n = PLACE[name, part]
            for m in range(n, n + slots):
                eng.wait_ge(landed[slot(m)], 16 * fill_of(m))

        def chunk(name, part=0):
            return ring[:, slot(PLACE[name, part]), :, :]

        def t_job(name, part, col, dst, g=None, scale=None):
            return dict(kind="T", name=name, part=part, col=col, dst=dst,
                        how="norm" if g is not None else "plain", g=g, scale=scale)

        def v_job(name, part, col, width, i0, dst, how="plain"):
            return dict(kind="V", name=name, part=part, col=col, width=width, i0=i0, dst=dst, how=how,
                        g=None, scale=None)

        nsa_jobs = [t_job("kv_cmp", 0, 0, qkT[:, 6, :]), t_job("kv_cmp", 0, P, qkT[:, 7, :])]
        nsa_jobs += [t_job("q_nsa", t // 2, P * (t % 2), qkT[:, t, :], 0) for t in range(4)]
        nsa_jobs += [t_job("kv_slc", 0, 0, qkT[:, 4, :], 1),
                     v_job("kv_slc", 0, P, P, 0, vtok[:, :, 0:P])]
        nsa_jobs += [t_job("kv_win", 0, 0, qkT[:, 5, :], 1),
                     v_job("kv_win", 0, P, P, 0, vtok[:, :, P:2 * P])]
        nsa_jobs += [dict(kind="G", how="sigmoid", dst=nsa_gate[:, :, :], name=None, g=None, scale=None)]
        moba_jobs = [t_job("q_moba", t // 2, P * (t % 2), qkT[:, t, :], 2) for t in range(4)]
        moba_jobs += [t_job("k_moba", t // 2, P * (t % 2), qkT[:, 4 + t, :], 3) for t in range(4)]
        moba_jobs += [v_job("v_moba", c, 0, SW, 2 * i, vtok[:, 2 * i:2 * i + 2, SW * c:SW * c + SW])
                      for c in range(2) for i in range(2)]
        da_jobs = [t_job("w_in_2", t // 2, P * (t % 2), qkT[:, t, :], 4) for t in range(4)]
        da_jobs += [t_job("w_in_2", 2 + t // 2, P * (t % 2), qkT[:, 4 + t, :], 5) for t in range(4)]
        da_jobs += [v_job("w_in_2", 4 + c, 0, SW, 2 * i, vtok[:, 2 * i:2 * i + 2, SW * c:SW * c + SW])
                    for c in range(2) for i in range(2)]
        da_jobs += [v_job("w_in_2", 6 + c, 0, SW, 2 * i, gtok[:, 2 * i:2 * i + 2, SW * c:SW * c + SW], "silu")
                    for c in range(2) for i in range(2)]
        ret_jobs = [t_job("w_in_2", 8, P * t, qkT[:, t, :], scale=HD ** -0.5) for t in range(2)]
        ret_jobs += [t_job("w_in_2", 9, P * t, qkT[:, 2 + t, :]) for t in range(2)]
        ret_jobs += [v_job("w_in_2", 10 + c, 0, SW, 2 * i, vtok[:, 2 * i:2 * i + 2, SW * c:SW * c + SW])
                     for c in range(2) for i in range(2)]
        ret_jobs += [v_job("w_in_2", 12 + c, 0, SW, 2 * i, gtok[:, 2 * i:2 * i + 2, SW * c:SW * c + SW], "silu")
                     for c in range(2) for i in range(2)]
        at = norms = rs = 0
        for jobs in (nsa_jobs, moba_jobs, da_jobs, ret_jobs):
            for n, j in enumerate(jobs):
                j.update(at=at, norm_at=norms, r_at=rs)
                j["last_of_chunk"] = j["name"] is not None and (
                    n + 1 == len(jobs) or (jobs[n + 1]["name"], jobs[n + 1].get("part")) != (j["name"], j.get("part")))
                at += 1
                norms += j["how"] == "norm"
                rs += j["how"] != "plain"

        def z_bank(j):
            return bank[j["at"] % 3]

        def mean_bank(j):
            return bank[3 + j["norm_at"] % 2]

        def pe_project(pe, jobs, h0=None):
            def mean(j):
                pe.wait_ge(z_sq, j["norm_at"] + 1)
                if j["norm_at"] >= 2:
                    pe.wait_ge(z_free, n_done_before(ALL_JOBS, j["norm_at"] - 2))
                pe.matmul(mean_bank(j)[:, :], head_mean[:, :], sq[j["norm_at"] % 2], start=True, stop=True)\
                  .then_inc(z_mean, 1)
            waiting = None
            for j in jobs:
                if j["at"] >= 3:
                    pe.wait_ge(z_free, j["at"] - 2)
                if j["name"]:
                    arrived(pe, j["name"], j["part"])
                if j["name"] == "q_nsa":
                    pe.wait_ge(q_in, 16 * 6)
                z = z_bank(j)
                if j["kind"] == "T":
                    for k in range(ND):
                        if j is jobs[0] and h0 is not None:
                            pe.wait_ge(h_ok, h0 + k + 1)
                        w = chunk(j["name"], j["part"])[:, k, j["col"]:j["col"] + P]
                        mm = pe.matmul(z[:, :], w, hT[:, k, :], start=(k == 0), stop=(k == ND - 1))
                elif j["kind"] == "V":
                    wd = j["width"]
                    for n in range(S // wd):
                        for k in range(ND):
                            i = j["i0"] + n
                            mm = pe.matmul(z[:, n * wd:(n + 1) * wd], hT[:, k, i * P:(i + 1) * P],
                                           chunk(j["name"], j["part"])[:, k, j["col"]:j["col"] + wd],
                                           start=(k == 0), stop=(k == ND - 1))
                else:
                    pe.wait_ge(gate_in, 16)
                    for i in range(NT):
                        for k in range(ND):
                            mm = pe.matmul(z[:, 24 * i:24 * i + 24], hT[:, k, i * P:(i + 1) * P],
                                           gate_w[:, k, :], start=(k == 0), stop=(k == ND - 1))
                mm.then_inc(z_done, 1)
                if j["last_of_chunk"]:
                    slots_read(pe)
                if waiting is not None:
                    mean(waiting)
                    waiting = None
                if j["how"] == "norm":
                    waiting = j
            if waiting is not None:
                mean(waiting)

        def slots_read(pe, n=1):
            pe.matmul(bank[7][0:32, 510:512], ident[:, 0:32], ident[:, 0:2], start=True, stop=True,
                      skip_group_check=True).then_inc(slot_used, n)

        def job_z(j):
            z = z_bank(j)
            if j["kind"] == "T":
                return z[:, :]
            if j["kind"] == "V":
                return z[:, :].rearrange("p (n w) -> p n w", w=j["width"])
            return z[:, 0:96].rearrange("p (n w) -> p n w", w=24)

        def job_r(j):
            r = rr[j["r_at"] % 2]
            if j["kind"] == "T":
                return r
            if j["kind"] == "V":
                return r.rearrange("p (n w) -> p n w", w=j["width"])
            return r[:, 0:96].rearrange("p (n w) -> p n w", w=24)

        def refine_root(dve, link, r, m, t):
            link(dve.tensor_tensor(t, r, r, ALU.mult))
            link(dve.tensor_tensor(t, m, t, ALU.mult))
            link(dve.tensor_scalar(t, t, -0.5, 1.5, ALU.mult, ALU.add))
            link(dve.tensor_tensor(r, r, t, ALU.mult))

        def refine_root_of(dve, link, r, z, scale, t):
            link(dve.tensor_tensor(t, r, r, ALU.mult))
            if scale != 1.0:
                link(dve.tensor_scalar(t, t, scale, None, ALU.mult))
            link(dve.scalar_tensor_tensor(out=t, in0=z, scalar=EPS / scale, in1=t, op0=ALU.add, op1=ALU.mult))
            link(dve.tensor_scalar(t, t, -0.5, 1.5, ALU.mult, ALU.add))
            link(dve.tensor_tensor(r, r, t, ALU.mult))

        def r_done_before(jobs_all, n):
            for j in jobs_all:
                if j["how"] != "plain" and j["r_at"] == n:
                    return j["at"] + 1

        def n_done_before(jobs_all, n):
            for j in jobs_all:
                if j["how"] == "norm" and j["norm_at"] == n:
                    return j["at"] + 1

        ALL_JOBS = nsa_jobs + moba_jobs + da_jobs + ret_jobs

        def act_project(act, link, jobs):
            for j in jobs:
                if j["how"] == "plain":
                    continue
                act.wait_ge(z_done, j["at"] + 1)
                if j["r_at"] >= 2:
                    act.wait_ge(z_free, r_done_before(ALL_JOBS, j["r_at"] - 2))
                if j["how"] == "norm":
                    if j["norm_at"] >= 2:
                        act.wait_ge(z_free, n_done_before(ALL_JOBS, j["norm_at"] - 2))
                    act.activation(sq[j["norm_at"] % 2], z_bank(j)[:, :], ACT.Square).then_inc(z_sq, 1)
                    act.wait_ge(z_mean, j["norm_at"] + 1)
                    link(act.activation(job_r(j), mean_bank(j)[:, :], ACT.Ln, bias=eps))
                    act.activation(job_r(j), job_r(j), ACT.Exp, scale=-0.5).then_inc(z_r, 1)
                else:
                    act.activation(job_r(j), job_z(j), ACT.Sigmoid).then_inc(z_r, 1)

        def dve_project(dve, link, jobs):
            for j in jobs:
                if j["how"] == "plain":
                    dve.wait_ge(z_done, j["at"] + 1)
                    if j["scale"] is not None:
                        ins = dve.tensor_scalar(j["dst"], job_z(j), j["scale"], None, ALU.mult)
                    else:
                        ins = dve.tensor_copy(j["dst"], job_z(j))
                else:
                    dve.wait_ge(z_r, j["r_at"] + 1)
                    if j["how"] == "norm":
                        g = gain[:, j["g"]:j["g"] + 1]
                        refine_root_of(dve, link, job_r(j), mean_bank(j)[:, :], 1.0, sq[j["norm_at"] % 2])
                        ins = dve.scalar_tensor_tensor(out=j["dst"], in0=job_z(j), scalar=g, in1=job_r(j),
                                                       op0=ALU.mult, op1=ALU.mult)
                    elif j["how"] == "silu":
                        ins = dve.tensor_tensor(j["dst"], job_z(j), job_r(j), ALU.mult)
                    else:
                        ins = dve.tensor_copy(j["dst"], job_r(j))
                ins.then_inc(z_free, 1)

        nsa_steps, moba_steps, da_steps = [], [], []
        for br in range(2):
            for h in [0, 4, 1, 5, 2, 6, 3, 7]:
                half = HD * (h // 4)
                for i in range(NT):
                    nsa_steps.append(dict(
                        q=qkT[half:half + HD, h % 4, i * P:(i + 1) * P], k=qkT[half:half + HD, 4 + br, 0:P * (i + 1)],
                        v=lambda kt, br=br: vtok[:, kt, P * br:P * br + P], vw=HD, v0=half,
                        bias=bias8[:, h, S - P * (i + 1):S], blocks=i + 1,
                        over=nsa_gate[:, i, 3 * h + br + 1:3 * h + br + 2], dst=omix[:, i, HD * h:HD * h + HD], add=True))
        for h in range(HEADS):
            half = HD * (h % 2)
            for i in range(NT):
                moba_steps.append(dict(
                    q=qkT[half:half + HD, h // 2, i * P:(i + 1) * P], k=qkT[half:half + HD, 4 + h // 2, 0:P * (i + 1)],
                    v=lambda kt, h=h: vtok[:, kt, P * (h // 2):P * (h // 2) + P], vw=HD, v0=half,
                    bias=bias8[:, h, S - P * (i + 1):S], blocks=i + 1,
                    over=None, dst=omix[:, i, 512 + HD * h:512 + HD * h + HD], add=False))
        for h in range(4):
            for m in range(2):
                for i in range(NT):
                    da_steps.append(dict(
                        q=qkT[HD * m:HD * m + HD, h, i * P:(i + 1) * P], k=qkT[HD * m:HD * m + HD, 4 + h, :],
                        v=lambda kt, h=h: vtok[:, kt, P * h:P * h + P], vw=P, v0=0,
                        bias=bias4[:, h, 384 - P * i:384 - P * i + S], blocks=NT,
                        over=None if m == 0 else lam[:, 5:6], dst=omix[:, i, P * h:P * h + P], add=(m == 1)))
        at = 0
        for steps in (nsa_steps, moba_steps, da_steps):
            for st in steps:
                st["at"] = at
                at += 1
        O_NSA, O_MOBA, O_DA = len(nsa_steps), len(nsa_steps) + len(moba_steps), at

        def pe_attend(pe, steps):
            def scores(st):
                n = st["at"]
                if n >= 3:
                    pe.wait_ge(s_bias, n - 2)
                pe.matmul(bank[n % 3][:, 0:P * st["blocks"]], st["q"], st["k"], start=True, stop=True)\
                  .then_inc(s_done, 1)

            def turn(st):
                n = st["at"]
                pe.wait_ge(s_exp, n + 1)
                if n >= 3:
                    pe.wait_ge(t_ok, n - 2)
                for b in range(st["blocks"]):
                    mm = pe.transpose(bank[3 + n % 3][:, b * P:(b + 1) * P], biased[n % 2][:, b * P:(b + 1) * P],
                                      ident[:, :])
                mm.then_inc(t_done, 1)

            def values(st):
                n = st["at"]
                pe.wait_ge(t_ok, n + 1)
                if n >= 2:
                    pe.wait_ge(o_acc, n - 1)
                for b in range(st["blocks"]):
                    mm = pe.matmul(bank[6 + n % 2][:, 0:P], probT[n % 2][:, b * P:(b + 1) * P], st["v"](b),
                                   start=(b == 0), stop=(b == st["blocks"] - 1))
                mm.then_inc(o_done, 1)
            for n in range(len(steps) + 2):
                if n < len(steps):
                    scores(steps[n])
                if 1 <= n <= len(steps):
                    turn(steps[n - 1])
                if n >= 2:
                    values(steps[n - 2])

        def act_attend(act, steps):
            def copy(st):
                n = st["at"]
                act.wait_ge(t_done, n + 1)
                if n >= 2:
                    act.wait_ge(o_done, n - 1)
                w = P * st["blocks"]
                act.activation(probT[n % 2][:, 0:w], bank[3 + n % 3][:, 0:w], ACT.Copy).then_inc(t_ok, 1)
            for m, st in enumerate(steps):
                n, w = st["at"], P * st["blocks"]
                act.wait_ge(s_bias, n + 1)
                if n >= 4:
                    act.wait_ge(o_acc, n - 3)
                act.activation(biased[n % 2][:, 0:w], biased[n % 2][:, 0:w], ACT.Exp, scale=-1.0,
                               bias=mn[:, n % 4:n % 4 + 1], accum_out=ls[:, n % 4:n % 4 + 1]).then_inc(s_exp, 1)
                if m >= 1:
                    copy(steps[m - 1])
            copy(steps[-1])

        def modulate_part(dve, m):
            ch, k = EARLY + m // ND, m % ND
            if k == 0:
                arrived(dve, "ada", ch)
            w, s = chunk("ada", ch)[:, k, :], vecs[:, 80 + k:81 + k]
            if k == 0:
                ins = dve.tensor_scalar(ada_sum[ch - EARLY], w, s, None, ALU.mult)
            else:
                dve.wait_ge(ada_done, m)
                ins = dve.scalar_tensor_tensor(out=ada_sum[ch - EARLY], in0=w, scalar=s, in1=ada_sum[ch - EARLY],
                                               op0=ALU.mult, op1=ALU.add)
            ins.then_inc(ada_done, 1)
            if k == ND - 1:
                dve.wait_ge(ada_done, m + 1)
                dve.sem_inc(ada_read, 1)

        def dve_attend(dve, link, steps, beside=False):
            def accumulate(st):
                n = st["at"]
                c = cf[:, n % 4:n % 4 + 1]
                dve.wait_ge(s_exp, n + 1)
                link(dve.reciprocal(c, ls[:, n % 4:n % 4 + 1]))
                if st["over"] is not None:
                    link(dve.tensor_tensor(c, st["over"], c, ALU.mult))
                dve.wait_ge(o_done, n + 1)
                if n >= 1:
                    dve.wait_ge(o_acc, n)
                if st["add"]:
                    ins = dve.scalar_tensor_tensor(out=st["dst"], in0=bank[6 + n % 2][:, st["v0"]:st["v0"] + st["vw"]], scalar=c,
                                                   in1=st["dst"], op0=ALU.mult, op1=ALU.add)
                else:
                    ins = dve.tensor_scalar(st["dst"], bank[6 + n % 2][:, st["v0"]:st["v0"] + st["vw"]], c, None, ALU.mult)
                ins.then_inc(o_acc, 1)
            for m in range(len(steps) + 2):
                if m < len(steps):
                    st = steps[m]
                    n, w = st["at"], P * st["blocks"]
                    dve.wait_ge(s_done, n + 1)
                    if n >= 2:
                        dve.wait_ge(t_done, n - 1)
                    dve.tensor_tensor_reduce(out=biased[n % 2][:, 0:w], in0=bank[n % 3][:, 0:w], in1=st["bias"],
                                             scale=1.0, scalar=3e38, op0=ALU.add, op1=ALU.min,
                                             accum_out=mn[:, n % 4:n % 4 + 1]).then_inc(s_bias, 1)
                if beside and m < len(steps):
                    for a in range(2):
                        modulate_part(dve, 2 * m + a)
                if m >= 2:
                    accumulate(steps[m - 2])

        def act_norm(act, link, r):
            for t in range(ND):
                n = ND * r + t
                if t >= 2:
                    act.wait_ge(sum_ok, n - 1)
                act.activation(sq[t % 2], resT[:, t, :], ACT.Square).then_inc(sq_ok, 1)
            act.wait_ge(sum_ok, ND * (r + 1))
            link(act.activation(rr[0], bank[0][:, :], ACT.Ln, scale=1.0 / D, bias=eps))
            act.activation(rr[0], rr[0], ACT.Exp, scale=-0.5).then_inc(rstd_ok, 1)

        def pe_norm(pe, r):
            for t in range(ND):
                pe.wait_ge(sq_ok, ND * r + t + 1)
                pe.matmul(bank[0][:, :], ones[:, :], sq[t % 2], start=(t == 0), stop=(t == ND - 1)).then_inc(sum_ok, 1)

        def dve_norm(dve, link, r, scale, done):
            dve.wait_ge(rstd_ok, r + 1)
            refine_root_of(dve, link, rr[0], bank[0][:, :], 1.0 / D, sq[0])
            for t in range(ND):
                dve.scalar_tensor_tensor(out=hT[:, t, :], in0=resT[:, t, :], scalar=scale[:, t:t + 1], in1=rr[0],
                                         op0=ALU.mult, op1=ALU.mult).then_inc(done, 1)

        def act_shift(act, r, shift):
            for t in range(ND):
                act.wait_ge(hs_ok, ND * r + t + 1)
                act.activation(hT[:, t, :], hT[:, t, :], ACT.Identity, bias=shift[:, t:t + 1]).then_inc(h_ok, 1)

        def pe_out(pe, r, name, res0):
            for t in range(ND):
                if t >= 2:
                    pe.wait_ge(mixT_ok, ND * r + t - 1)
                for i in range(NT):
                    mm = pe.transpose(bank[t % 2][:, i * P:(i + 1) * P], omix[:, i, t * P:(t + 1) * P], ident[:, :])
                mm.then_inc(mixT_t, 1)
            pe.wait_ge(mixT_ok, ND * (r + 1))
            for n in range(ND):
                if n % 2 == 0:
                    arrived(pe, name, n // 2)
                if n >= 3:
                    pe.wait_ge(res_ok, res0 + n - 2)
                for k in range(ND):
                    mm = pe.matmul(bank[2 + n % 3][:, :], chunk(name, n // 2)[:, k, P * (n % 2):P * (n % 2) + P],
                                   hT[:, k, :], start=(k == 0), stop=(k == ND - 1))
                mm.then_inc(out_t, 1)
                if n % 2 and (r == 1 or n < ND - 1):
                    slots_read(pe)

        def act_out(act, r):
            for t in range(ND):
                act.wait_ge(mixT_t, ND * r + t + 1)
                act.activation(hT[:, t, :], bank[t % 2][:, :], ACT.Copy).then_inc(mixT_ok, 1)

        def dve_out(dve, r, scale, res0):
            for n in range(ND):
                dve.wait_ge(out_t, ND * r + n + 1)
                if scale is None:
                    ins = dve.tensor_tensor(resT[:, n, :], bank[2 + n % 3][:, :], resT[:, n, :], ALU.add)
                else:
                    ins = dve.scalar_tensor_tensor(out=resT[:, n, :], in0=bank[2 + n % 3][:, :],
                                                   scalar=scale[:, n:n + 1], in1=resT[:, n, :], op0=ALU.mult, op1=ALU.add)
                ins.then_inc(res_ok, 1)

        block = ctx.enter_context(nc.Block())

        @block.sync
        def _(sp):
            def rows(ap):
                return ap.rearrange("(k p) n -> p k n", p=P)

            def load(name, part, n, m):
                if n - SLOTS >= FIRST_SLOT:
                    if last_of[n] < 0:
                        sp.wait_ge(ada_read, -last_of[n])
                    else:
                        sp.wait_ge(slot_used, last_of[n])
                dst = ring[:, slot(n), :, :]
                if name == "ada":
                    sp.dma_start(dst, rows(ada_w[0])[:, :, SW * part:SW * (part + 1)]).then_inc(landed[slot(n)], 16)
                elif name == "q_nsa":
                    for t in range(2):
                        for g in range(2):
                            c0 = HD * (2 * part + t + 4 * g)
                            sp.dma_start(dst[:, :, P * t + HD * g:P * t + HD * (g + 1)], rows(w_in[0])[:, :, c0:c0 + HD])\
                              .then_inc(landed[slot(n)] if (t, g) == (1, 1) else q_in, 16)
                elif name == "cmp_w1":
                    sp.dma_start(dst.rearrange("p k c -> p (k c)").rearrange("p (m h) -> p m h", h=P),
                                 nsa_cmp_w1[0, part].rearrange("(m q) h -> q m h", q=P)).then_inc(landed[slot(n)], 16)
                else:
                    src, c0 = {"kv_cmp": (w_in, 512), "kv_slc": (w_in, 768), "kv_win": (w_in, 1024),
                               "q_moba": (w_in, 1304), "k_moba": (w_in, 1816), "v_moba": (w_in, 2328),
                               "w_out": (w_out, 0), "w_in_2": (w_in_2, 0), "w_out_2": (w_out_2, 0)}[name]
                    c0 += SW * part
                    sp.dma_start(dst, rows(src[0])[:, :, c0:c0 + SW]).then_inc(landed[slot(n)], 16)

            for name, part, m in PLAN:
                load(name, part, PLACE[name, part], m)

            def expert(e, used, base, signal):
                w1 = exp_w1[0].rearrange("e (k p) n -> p k e n", p=P)
                w2 = exp_w2[0].rearrange("e (k p) n -> p k e n", p=P)
                for j in range(4):
                    for half in range(2):
                        s = 2 * j + half
                        sp.wait_ge(used, base + s + 1)
                        c0 = FF * half + SW * j
                        sp.dma_start(ring[:, s, :, :], w1[:, :, bass.ds(e, 1), c0:c0 + SW].rearrange("p k e n -> p k (e n)"))\
                          .then_inc(signal[s], 16)
                for q in range(4):
                    s = 8 + q
                    sp.wait_ge(used, base + s + 1)
                    dst = ringf[:, s * 2048:(s + 1) * 2048].rearrange("p (k n) -> p k n", k=2)
                    sp.dma_start(dst, w2[:, 2 * q:2 * q + 2, bass.ds(e, 1), :].rearrange("p k e n -> p k (e n)"))\
                      .then_inc(signal[s], 16)

            sp.wait_ge(ada_read, 24 - EARLY)
            with sp.Fori(0, NEXP) as e:
                expert(e, slot_used, e * SLOTS + (USED0 - SLOTS), landed)

            sp.wait_ge(r_dv, 1)
            extra = sp.value_load(extra_i[0:1, 0:1], min_val=0, max_val=15)
            with sp.If(extra > 0):
                with sp.Fori(0, extra) as o:
                    sp.wait_ge(exp_ok, o + 1)
                    sp.sem_inc(waited_sp, 1)
                    e = sp.value_load(exp_i[0:1, 0:1], min_val=0, max_val=NEXP - 1)
                    w1 = exp_w1[0].rearrange("e (k p) n -> p k e n", p=P)
                    w2 = exp_w2[0].rearrange("e (k p) n -> p k e n", p=P)
                    for s in range(8):
                        c0 = FF * (s % 2) + SW * (s // 2)
                        sp.dma_start(ring[:, s, :, :], w1[:, :, bass.ds(e, 1), c0:c0 + SW].rearrange("p k e n -> p k (e n)"))\
                          .then_inc(over_in, 16)
                    for q in range(4):
                        dst = ringf[:, (8 + q) * 2048:(9 + q) * 2048].rearrange("p (k n) -> p k n", k=2)
                        sp.dma_start(dst, w2[:, 2 * q:2 * q + 2, bass.ds(e, 1), :].rearrange("p k e n -> p k (e n)"))\
                          .then_inc(over_in, 16)
            sp.wait_ge(over_done, 1)
            for i in range(NT):
                sp.wait_ge(y_in[i], 16)
            for name, part, m in AFTER:
                load(name, part, PLACE[name, part], m)

        @block.gpsimd
        def _(pool):
            count = [0]

            def link(ins):
                count[0] += 1
                ins.then_inc(pool_c, 1)
                pool.wait_ge(pool_c, count[0])

            pool.memset(ones[:, :], 1.0).then_inc(consts, 1)
            link(pool.memset(ident[:, :], 0.0))
            pool.affine_select(out=ident[:, :], in_=ident[:, :], compare_op=ALU.not_equal, fill=1.0, base=0,
                               pattern=[[-1, P]], channel_multiplier=1).then_inc(consts, 1)
            link(pool.memset(head_mean[:, :], 0.0))
            for a in range(2):
                pool.memset(head_mean[HD * a:HD * a + HD, HD * a:HD * a + HD], 1.0 / HD).then_inc(consts, 1)
            pool.wait_ge(consts, 4)
            pool.affine_select(out=before_tok[:, :], in_=ones[:, :], compare_op=ALU.is_gt, fill=0.0, base=0,
                               pattern=[[1, P]], channel_multiplier=-1).then_inc(consts, 1)
            pool.iota(iota_c[:, :], pattern=[[1, P]], base=0, channel_multiplier=0,
                      allow_small_or_imprecise_dtypes=True).then_inc(consts, 1)
            pool.iota(tok_id, pattern=[[P, NT]], base=0, channel_multiplier=1,
                      allow_small_or_imprecise_dtypes=True).then_inc(consts, 1)
            pool.iota(junk, pattern=[[1, 1]], base=JUNK, channel_multiplier=1,
                      allow_small_or_imprecise_dtypes=True).then_inc(consts, 1)
            pool.affine_select(out=row_ok, in_=ones[:, 0:NT], compare_op=ALU.is_ge, fill=0.0, base=-(CMP_L - 1),
                               pattern=[[P, NT]], channel_multiplier=1).then_inc(consts, 1)
            pool.memset(eps, EPS).then_inc(consts, 1)
            pool.iota(work[:, 0, :], pattern=[[-1, S]], base=S - P, channel_multiplier=1,
                      allow_small_or_imprecise_dtypes=True).then_inc(dist_ok, 1)
            for h in range(HEADS):
                pool.wait_ge(scaled_ok, h + 1)
                pool.affine_select(out=bias8[:, h, :], in_=bias8[:, h, :], compare_op=ALU.is_ge, fill=NEG,
                                   base=S - P, pattern=[[-1, S]], channel_multiplier=1).then_inc(bias_ok, 1)
            for kv in range(2):
                pool.wait_ge(xt_ok, ND)
                pool.wait_ge(z_free, kv + 1)
                for g in range(2):
                    pool.dma_start(kv_turned[kv][HD * (1 - g):HD * (2 - g), :], qkT[HD * g:HD * (g + 1), 6 + kv, :])\
                        .then_inc(turned, 16)
            pool.wait_ge(c_pe, 1)
            pool.iota(cmp_bias.rearrange("p (g i h) n -> p g i h n", g=2, i=NT),
                      pattern=[[0, 2], [2 * P, NT], [0, 4], [-2 * CMP_STRIDE, CMP_N]],
                      base=-(CMP_L - 1), channel_multiplier=2, allow_small_or_imprecise_dtypes=True).then_inc(dist_ok, 1)
            for h in range(HEADS):
                pool.wait_ge(scaled_ok, HEADS + h + 1)
                part = cmp_bias.rearrange("p (g i h) n -> p g i h n", g=2, i=NT)[:, h // 4, :, h % 4, :]
                pool.affine_select(out=part, in_=part, compare_op=ALU.is_ge, fill=NEG,
                                   base=-(CMP_L - 1), pattern=[[P, NT], [-CMP_STRIDE, CMP_N]],
                                   channel_multiplier=1).then_inc(bias_ok, 1)
            pool.wait_ge(o_acc, O_MOBA)
            pool.wait_ge(s_bias, O_MOBA)
            link(pool.memset(ybuf[:, :], 0.0))
            for i in range(NT + 1):
                pool.dma_start(y_dram[i * P:(i + 1) * P, :], ybuf[:, :]).then_inc(y_zero, 16)
            pool.wait_ge(y_zero, 16 * (NT + 1))

            def fetch(sg, n):
                pool.wait_ge(sg.idx_ok, n)
                pool.sem_inc(waited_pool, 1)
                pool.indirect_dma_start(xg[:, :], None, h2_dram, bass.IndirectOffsetOnAxis(src_i[:, 0:1], 0))\
                    .then_inc(sg.got, 16)

            def put(sg, n, rows):
                pool.wait_ge(sg.y_ok, rows + 2)
                pool.wait_ge(sg.dst, n)
                pool.sem_inc(waited_pool, 1)
                pool.indirect_dma_start(y_dram, bass.IndirectOffsetOnAxis(dst_i[:, 0:1], 0), ybuf[:, :], None,
                                        bounds_check=JUNK + CAP - 1, compute_op=ALU.add)\
                    .then_inc(sg.put, 16)
                pool.wait_ge(sg.put, n * 16)
                pool.sem_inc(sg.free, 1)

            for sg in (main, over):
                pool.sem_inc(sg.free, 1)
                pool.sem_inc(sg.y_ok, 2)
            pool.wait_ge(h2_out, 16 * NT)
            fetch(main, 1)
            with pool.Fori(0, NEXP - 1) as b:
                pool.wait_ge(main.xt, b * 2 + 2)
                fetch(main, b + 2)
                put(main, b + 1, b * 2 + 2)
            put(main, NEXP, 2 * NEXP)
            pool.wait_ge(r_dv, 1)
            extra = pool.value_load(extra_i[0:1, 0:1], min_val=0, max_val=15)
            with pool.If(extra > 0):
                with pool.Fori(0, extra) as o:
                    fetch(over, o + 1)
                    put(over, o + 1, o * 2 + 2)
            pool.wait_ge(res_ok, 2 * ND)
            pool.iota(bias4[:, 0, :], pattern=[[-1, 896]], base=384, channel_multiplier=1,
                      allow_small_or_imprecise_dtypes=True).then_inc(dist_ok, 1)
            pool.wait_ge(o_acc, O_DA)
            pool.wait_ge(s_bias, O_DA)
            pool.iota(ret_dist, pattern=[[448, 2], [1, 448]], base=-384, channel_multiplier=-1,
                      allow_small_or_imprecise_dtypes=True).then_inc(dist_ok, 1)

        @block.scalar
        def _(act):
            count = [0]

            def link(ins):
                count[0] += 1
                ins.then_inc(ac, 1)
                act.wait_ge(ac, count[0])

            act.dma_start(vec_rows, vec_rows_in).then_inc(vec_in, 16)
            act.dma_start(pos_rows.rearrange("m (k q) -> m k q", k=2),
                          nsa_cmp_pos[0].rearrange("k (m r) d -> m k (r d)", r=2)).then_inc(vec_in, 16)
            act.dma_start(x_rows, x[0].rearrange("(i p) d -> p i d", p=P)).then_inc(x_in, 16)
            act.dma_start(cw2[:, :, :], nsa_cmp_w2[0].rearrange("k p n -> p k n")).then_inc(c_in, 16)
            act.dma_start(misc[:, :], misc_in.to_broadcast([P, MISC])).then_inc(lam_in, 16)

            act.wait_ge(vec_ok, 1)
            act.activation(vecs[:, 88:96], vecs[:, 72:80], ACT.Exp, scale=-1.0).then_inc(silu_e, 1)
            for t in range(ND):
                act.wait_ge(xt_t, t + 1)
                act.activation(resT[:, t, :], bank[t % 4][:, :], ACT.Copy).then_inc(xt_ok, 1)
            act.dma_start(gate_w[:, :, :], w_in[0].rearrange("(k p) n -> p k n", p=P)[:, :, 1280:1304]).then_inc(gate_in, 16)
            act.wait_ge(consts, 10)
            act.wait_ge(xt_ok, ND)
            act.wait_ge(scaled_ok, HEADS)
            act_norm(act, link, 0)
            act.wait_ge(mod_ok, 1)
            act_shift(act, 0, mod[:, 0:8])

            act_project(act, link, nsa_jobs)

            act.wait_ge(c_dv, C_CUBE)
            act.activation(hid_t[:, :, :], hid_t[:, :, :], ACT.Exp, scale=-2.0 * 0.7978845608028654).then_inc(c_ac, 1)
            act.wait_ge(c_dv, C_SQ)
            link(act.activation(cs[0:CMP_N, 0, 0:2], cs[0:CMP_N, 1, 0:2], ACT.Ln, bias=eps[0:CMP_N, :], scale=1.0 / HD))
            act.activation(cs[0:CMP_N, 0, 0:2], cs[0:CMP_N, 0, 0:2], ACT.Exp, scale=-0.5).then_inc(c_ac, 1)
            for g in range(2):
                act.wait_ge(c_dv, C_S + g)
                act.activation(cmp_s[:, 16 * g:16 * g + 16, :], cmp_s[:, 16 * g:16 * g + 16, :], ACT.Exp, scale=-1.0)\
                    .then_inc(c_ac, 1)
            for g in range(2):
                act.wait_ge(c_pe, 6 + g)
                act.activation(cmp_pT[:, g, :], bank[2 + g][:, :], ACT.Copy).then_inc(c_ac, 1)

            act_attend(act, nsa_steps)
            act_project(act, link, moba_jobs)
            act_attend(act, moba_steps)
            act_out(act, 0)

            act.wait_ge(mixT_ok, ND)
            act.dma_start(rw[:, :, :], router_w[0].rearrange("(k p) n -> p k n", p=P)).then_inc(rt_in, 16)
            act.dma_start(b1_rows, exp_b1[0]).then_inc(b_in, 16)
            act.dma_start(b2_keep, exp_b2[0]).then_inc(b_in, 16)
            act.wait_ge(res_ok, ND)
            act_norm(act, link, 1)
            act.wait_ge(mod_ok, 2)
            act_shift(act, 1, mod[:, 24:32])
            for i in range(NT):
                for a in range(2):
                    act.wait_ge(h2_t, 2 * i + a + 1)
                    act.activation(h2_rows[:, i, 512 * a:512 * a + 512], bank[4 + a][:, :], ACT.Copy).then_inc(h2_ok, 1)
                act.wait_ge(h2_ok, 2 * i + 2)
                act.dma_start(h2_dram[i * P:(i + 1) * P, :], h2_rows[:, i, :]).then_inc(h2_out, 16)
            act.wait_ge(lg_ok, 1)
            for i in range(NT):
                act.activation(gates[:, i, :], lg[:, i, :], ACT.Exp, bias=m8[:, i, 7:8]).then_inc(r_ac, 1)

            def sigmoids(sg, n):
                for j in range(8):
                    act.wait_ge(sg.g, n + (j + 1))
                    act.activation(s_t[:, j % 2, :], g_t[:, j % 2, :], ACT.Sigmoid, scale=ALPHA).then_inc(sg.sig, 1)

            def rows_in(sg, n):
                for a in range(2):
                    act.wait_ge(sg.xt, n + (a + 1))
                    act.activation(xgT[:, 4 * a:4 * a + 4, :], bank[5 + a][:, :].rearrange("p (k q) -> p k q", k=4),
                                   ACT.Copy).then_inc(sg.xt_ok, 1)

            def rows_done(sg, n):
                for a in range(2):
                    act.wait_ge(sg.y, n + (a + 1))
                    act.activation(ybuf[:, 512 * a:512 * a + 512], bank[3 + a][:, :], ACT.Copy,
                                   scale=meta_c[:, 2:3]).then_inc(sg.y_ok, 1)

            rows_in(main, 0)
            with act.Fori(0, NEXP - 1) as b:
                sigmoids(main, b * 8)
                rows_in(main, b * 2 + 2)
                act.wait_ge(main.free, b + 1)
                act.wait_ge(main.dst, b + 1)
                rows_done(main, b * 2)
            sigmoids(main, 8 * (NEXP - 1))
            act.wait_ge(main.free, NEXP)
            act.wait_ge(main.dst, NEXP)
            rows_done(main, 2 * (NEXP - 1))
            act.wait_ge(main.free, NEXP + 1)
            act.wait_ge(r_dv, 1)
            extra = act.value_load(extra_i[0:1, 0:1], min_val=0, max_val=15)
            with act.If(extra > 0):
                with act.Fori(0, extra) as o:
                    rows_in(over, o * 2)
                    sigmoids(over, o * 8)
                    act.wait_ge(over.dst, o + 1)
                    rows_done(over, o * 2)
                    act.wait_ge(over.free, o + 2)
            for i in range(NT):
                act.dma_start(y_rows[i], y_dram[P * i:P * (i + 1), :]).then_inc(y_in[i], 16)

            act.wait_ge(res_ok, 2 * ND)
            act_norm(act, link, 2)
            act.wait_ge(g_dv, 1)
            act.activation(lam[:, 2:4], lam[:, 0:2], ACT.Exp).then_inc(g_ac, 1)
            link(act.activation(lgam[:, 2, :], lgam[:, 1, :], ACT.Exp, scale=-1.0))
            act.activation(lgam[:, 4, :], lgam[:, 2, :], ACT.Ln, bias=ones[:, 0:1]).then_inc(g_ac, 1)
            act.wait_ge(h_ok, 3 * ND)
            act_project(act, link, da_jobs)
            act_attend(act, da_steps)

            def inverse_roots(n):
                act.wait_ge(rt_f, n + 1)
                link(act.activation(ms[:, :], ms[:, :], ACT.Ln, scale=1.0 / P, bias=eps))
                act.activation(ms[:, :], ms[:, :], ACT.Exp, scale=-0.5).then_inc(rt_o, 1)
            for i in range(NT):
                inverse_roots(i)
            act_project(act, link, ret_jobs)
            for h in range(4):
                act.wait_ge(g_dv, 2 + h)
                act.activation(decay[:, h, :], decay[:, h, :], ACT.Exp).then_inc(g_ac, 1)
            for h in range(4):
                inverse_roots(NT + h)
            act_out(act, 1)
            for i in range(NT):
                for a in range(2):
                    act.wait_ge(f_t, 2 * i + a + 1)
                    act.activation(rows_out[:, i, 512 * a:512 * a + 512], bank[5 + a][:, :], ACT.Copy).then_inc(f_ok, 1)
                act.wait_ge(f_ok, 2 * i + 2)
                act.dma_start(out[0].rearrange("(i p) d -> i p d", p=P)[i], rows_out[:, i, :]).then_inc(f_out, 16)
            act.wait_ge(f_out, 16 * NT)

        @block.tensor
        def _(pe):
            pe.wait_ge(vec_in, 2 * 16)
            pe.wait_ge(consts, 2)
            pe.transpose(bank[0][:, 0:86], vec_rows, ident[0:86, 0:86])
            for kv in range(2):
                mm = pe.transpose(bank[0][:, 96 + 16 * kv:96 + 16 * (kv + 1)], pos_rows[:, P * kv:P * kv + P],
                                  ident[0:CMP_L // 2, 0:CMP_L // 2])
            mm.then_inc(vec_t, 1)
            pe.wait_ge(vec_ok, 1)
            pe.wait_ge(x_in, 16)
            for t in range(ND):
                if t >= 4:
                    pe.wait_ge(xt_ok, t - 3)
                for i in range(NT):
                    mm = pe.transpose(bank[t % 4][:, i * P:(i + 1) * P], x_rows[:, i, t * P:(t + 1) * P], ident[:, :])
                mm.then_inc(xt_t, 1)

            def modulate(parts):
                for ch in parts:
                    arrived(pe, "ada", ch)
                    for m in (2 * ch, 2 * ch + 1):
                        for k in range(ND):
                            mm = pe.matmul(bank[5][:, m:m + 1], chunk("ada", ch)[:, k, P * (m % 2):P * (m % 2) + P],
                                           vecs[:, 80 + k:81 + k], start=(k == 0), stop=(k == ND - 1))
                    mm.then_inc(slot_used, 1)
            pe.wait_ge(consts, 10)
            pe.wait_ge(xt_ok, ND)
            pe_norm(pe, 0)
            pe.wait_ge(silu_ok, 1)
            modulate(range(EARLY))
            pe.matmul(bank[7][:, 510:512], ident[:, :], ident[:, 0:2], start=True, stop=True).then_inc(mod_a, 1)
            pe_project(pe, nsa_jobs, 0)

            pe.wait_ge(z_free, nsa_jobs[-1]["at"] + 1)
            pe.wait_ge(c_dv, C_LAID)
            for kv in range(2):
                arrived(pe, "cmp_w1", kv)
                w1 = chunk("cmp_w1", kv).rearrange("p k c -> p (k c)")
                for m in range(CMP_L // 2):
                    mm = pe.matmul(bank[kv][:, 0:2 * CMP_N], w1[:, P * m:P * (m + 1)], cmp_in[kv][:, m, :],
                                   start=(m == 0), stop=(m == CMP_L // 2 - 1))
                mm.then_inc(slot_used, 1)
            pe.matmul(bank[7][:, 510:512], ident[:, :], ident[:, 0:2], start=True, stop=True).then_inc(c_pe, 1)
            pe.wait_ge(c_dv, C_HID)
            pe.wait_ge(c_in, 16)
            for g in range(2):
                pe.matmul(bank[4][0:CMP_N, HD * g:HD * g + HD], hid[:, g, :], cw2[:, 0, :], start=True, stop=True)
                mm = pe.matmul(bank[5][:, HD * g:HD * g + HD], hid4[:, g, :, :].rearrange("p r n -> p (r n)"),
                               cw2[:, 1, :], start=True, stop=True)
            mm.then_inc(c_pe, 1)
            pe.wait_ge(c_dv, C_KN)
            pe.transpose(bank[6][:, 0:CMP_N], kc_n[:, :], ident[0:CMP_N, 0:CMP_N]).then_inc(c_pe, 1)
            pe.wait_ge(c_dv, C_KT)
            for g in range(2):
                for n in range(4 * NT):
                    i, hh = n // 4, n % 4
                    mm = pe.matmul(bank[g][:, CMP_N * n:CMP_N * (n + 1)],
                                   qkT[HD * g:HD * g + HD, hh, i * P:(i + 1) * P], kcT[HD * g:HD * g + HD, :],
                                   start=True, stop=True)
                mm.then_inc(c_pe, 1)
            for g in range(2):
                pe.wait_ge(c_dv, C_P + g)
                for i in range(NT):
                    n = 4 * (NT * g + i)
                    mm = pe.transpose(bank[2 + g][:, P * i:P * i + P], cmp_s[:, n:n + 4, :].rearrange("p h n -> p (h n)"),
                                      ident[:, :])
                mm.then_inc(c_pe, 1)
            for g in range(2):
                pe.wait_ge(c_ac, 5 + g)
                for i in range(NT):
                    mm = pe.matmul(bank[4 + i][:, SW * g:SW * g + SW], cmp_pT[:, g, P * i:P * i + P], vc_diag[:, g, :],
                                   start=True, stop=True)
                    if g == 1:
                        mm.then_inc(c_pe, 1)

            pe.wait_ge(c_dv, C_O)
            pe_attend(pe, nsa_steps)
            pe.wait_ge(t_ok, O_NSA)
            pe.wait_ge(ada_done, (24 - EARLY) * ND)
            for m in range(2 * EARLY, 48):
                mm = pe.matmul(bank[5][:, m:m + 1], ada_sum[m // 2 - EARLY][:, P * (m % 2):P * (m % 2) + P], ones[:, 0:1],
                               start=True, stop=True)
            mm.then_inc(mod_a, 1)
            pe.wait_ge(o_acc, O_NSA)
            pe_project(pe, moba_jobs)
            pe.wait_ge(z_free, moba_jobs[-1]["at"] + 1)
            pe_attend(pe, moba_steps)
            pe.wait_ge(o_acc, O_MOBA)
            pe_out(pe, 0, "w_out", 0)
            pe.wait_ge(res_ok, ND)
            pe_norm(pe, 1)

            pe.wait_ge(b_in, 32)
            for m in range(16):
                mm = pe.transpose(bank[2][:, NEXP * m:NEXP * (m + 1)], b1_rows[:, P * m:P * (m + 1)],
                                  ident[0:NEXP, 0:NEXP])
            mm.then_inc(r_pe, 1)
            pe.wait_ge(h_ok, 2 * ND)
            pe.wait_ge(rt_in, 16)
            pe.wait_ge(lam_in, 16)
            for i in range(NT):
                pe.matmul(bank[6][:, NEXP * i:NEXP * (i + 1)], ones[0:1, :], rb_row, start=True, stop=False)
                for k in range(ND):
                    mm = pe.matmul(bank[6][:, NEXP * i:NEXP * (i + 1)], hT[:, k, i * P:(i + 1) * P], rw[:, k, :],
                                   start=False, stop=(k == ND - 1))
            mm.then_inc(r_pe, 1)
            for i in range(NT):
                for a in range(2):
                    if i >= 1:
                        pe.wait_ge(h2_ok, 2 * (i - 1) + a + 1)
                    for k in range(4):
                        mm = pe.transpose(bank[4 + a][:, P * k:P * k + P], hT[:, 4 * a + k, i * P:(i + 1) * P], ident[:, :])
                    mm.then_inc(h2_t, 1)
            pe.wait_ge(sel_ok, 1)
            for i in range(NT):
                for j in range(i + 1):
                    mm = pe.matmul(bank[7][:, NEXP * i:NEXP * (i + 1)], (before_tok if j == i else ones)[:, :],
                                   sel[:, j, :], start=(j == 0), stop=(j == i))
            for j in range(NT):
                mm = pe.matmul(bank[7][:, NEXP * NT:NEXP * (NT + 1)], ones[:, :], sel[:, j, :],
                               start=(j == 0), stop=(j == NT - 1))
            mm.then_inc(r_pe, 1)
            pe.wait_ge(sel_ok, 2)
            for i in range(NT):
                mm = pe.transpose(bank[6][0:NEXP, i * P:(i + 1) * P], gates[:, i, :], ident[:, :])
            mm.then_inc(r_pe, 1)

            def indices(sg, e, n):
                pe.wait_ge(sg.hot, n)
                for i in range(NT):
                    r = route[:, i, bass.ds(e, 1), :].rearrange("p e c -> p (e c)")
                    mm = pe.matmul(bank[7][:, 0:4], onehot[:, i, :], r, start=(i == 0), stop=(i == NT - 1))
                mm.then_inc(sg.idx, 1)

            def turn_rows(sg, n):
                pe.wait_ge(sg.got, n)
                for a in range(2):
                    for k in range(4):
                        mm = pe.transpose(bank[5 + a][:, P * k:P * k + P], xg[:, P * (4 * a + k):P * (4 * a + k + 1)],
                                          ident[:, :])
                    mm.then_inc(sg.xt, 1)

            def first_layer(sg, n, wait_slot, used, middle=None):
                for j in range(8):
                    if j % 2 == 0:
                        wait_slot(j)
                        wait_slot(j + 1)
                    if j >= 2:
                        pe.wait_ge(sg.l, n + (j - 1))
                    for half in range(2):
                        w = ring[:, 2 * (j // 2) + half, :, :]
                        for k in range(ND):
                            mm = pe.matmul(bank[j % 2][:, CAP * half:CAP * half + CAP], w[:, k, P * (j % 2):P * (j % 2) + P],
                                           xgT[:, k, :], start=(k == 0), stop=(k == ND - 1))
                            if used and half == 0 and k == 0 and j % 2 == 0:
                                mm.then_inc(slot_used, 1)
                        if used and half == 0 and j % 2:
                            mm.then_inc(slot_used, 1)
                    mm.then_inc(sg.u, 1)
                    if j == 0 and middle:
                        middle()

            def second_layer(sg, n, wait_slot, used):
                for k in range(ND):
                    if k % 2 == 0:
                        wait_slot(8 + k // 2)
                    pe.wait_ge(sg.act, n + (k + 1))
                    w = ringf[:, (8 + k // 2) * 2048 + D * (k % 2):(8 + k // 2) * 2048 + D * (k % 2) + D]
                    for a in range(2):
                        mm = pe.matmul(bank[3 + a][:, :], actT[:, k, :], w[:, 512 * a:512 * a + 512],
                                       start=(k == 0), stop=(k == ND - 1))
                        if used and k % 2 == 0 and a == 0:
                            mm.then_inc(slot_used, 1)
                        if k == ND - 1:
                            mm.then_inc(sg.y, 1)

            FILLS = [fill_of(MOE0 + s) for s in range(SLOTS)]

            pe.wait_ge(gT_ok, 1)
            indices(main, 0, 1)
            turn_rows(main, 16)
            with pe.Fori(0, NEXP - 1) as b:
                def wait_slot(s):
                    pe.wait_ge(landed[s], b * 16 + 16 * FILLS[s])
                pe.wait_ge(main.xt_ok, b * 2 + 2)
                first_layer(main, b * 8, wait_slot, True, lambda: indices(main, b + 1, b + 2))
                turn_rows(main, b * 16 + 32)
                pe.wait_ge(main.y_ok, b * 2 + 2)
                second_layer(main, b * 8, wait_slot, True)

            def wait_slot(s):
                pe.wait_ge(landed[s], 16 * (NEXP - 1 + FILLS[s]))
            pe.wait_ge(main.xt_ok, 2 * NEXP)
            first_layer(main, 8 * (NEXP - 1), wait_slot, True)
            pe.wait_ge(main.y_ok, 2 * NEXP)
            second_layer(main, 8 * (NEXP - 1), wait_slot, True)
            pe.wait_ge(main.y_ok, 2 * NEXP + 2)
            slots_read(pe)
            pe.wait_ge(r_dv, 1)
            extra = pe.value_load(extra_i[0:1, 0:1], min_val=0, max_val=15)
            with pe.If(extra > 0):
                with pe.Fori(0, extra) as o:
                    pe.wait_ge(exp_ok, o + 1)
                    pe.sem_inc(waited_pe, 1)
                    e = pe.value_load(exp_i[0:1, 0:1], min_val=0, max_val=NEXP - 1)
                    indices(over, e, o + 1)
                    turn_rows(over, o * 16 + 16)
                    pe.wait_ge(over.xt_ok, o * 2 + 2)
                    pe.wait_ge(over_in, o * (16 * SLOTS) + 16 * SLOTS)
                    first_layer(over, o * 8, lambda s: None, False)
                    second_layer(over, o * 8, lambda s: None, False)
                    pe.wait_ge(over.y_ok, o * 2 + 4)
            pe.matmul(bank[2][:, 510:512], ident[:, :], ident[:, 0:2], start=True, stop=True).then_inc(over_done, 1)

            pe.wait_ge(gT_ok, 1)
            for t in range(ND):
                pe.matmul(bank[t][:, :], b2_keep[:, P * t:P * (t + 1)], gatesT, start=True, stop=False)
            for i in range(NT):
                pe.wait_ge(y_in[i], 16)
                for t in range(ND):
                    mm = pe.matmul(bank[t][:, i * P:(i + 1) * P], y_rows[i][:, P * t:P * (t + 1)], ident[:, :],
                                   start=False, stop=(i == NT - 1))
                mm.then_inc(y_used, 1)

            pe.wait_ge(res_ok, 2 * ND)
            pe_norm(pe, 2)
            pe_project(pe, da_jobs, 2 * ND)
            pe.wait_ge(z_free, da_jobs[-1]["at"] + 1)
            pe_attend(pe, da_steps)
            pe.wait_ge(o_acc, O_DA)
            pe_project(pe, ret_jobs)
            pe.wait_ge(z_free, ret_jobs[-1]["at"] + 1)

            def ret_values(h):
                for i in range(NT):
                    for kt in range(NT):
                        if i == 0:
                            pe.wait_ge(rt_d, 4 * h + kt + 1)
                        if kt == 0 and h >= 1:
                            pe.wait_ge(rt_rd, 4 * (h - 1) + i + 1)
                        mm = pe.matmul(bank[4 + i][:, 0:P], ret_s[h % 2][:, kt, i * P:(i + 1) * P],
                                       vtok[:, kt, P * h:P * (h + 1)], start=(kt == 0), stop=(kt == NT - 1))
                    mm.then_inc(rt_pv, 1)
            for h in range(4):
                half = HD * (h % 2)
                for kt in range(NT):
                    if h >= 1:
                        pe.wait_ge(rt_d, 4 * (h - 1) + kt + 1)
                    pe.matmul(bank[kt][:, :], qkT[half:half + HD, 2 + h // 2, kt * P:(kt + 1) * P],
                              qkT[half:half + HD, h // 2, :], start=True, stop=True).then_inc(rt_s, 1)
                if h >= 1:
                    ret_values(h - 1)
            ret_values(3)
            pe.wait_ge(rt_m, 4)
            pe_out(pe, 1, "w_out_2", 2 * ND)
            pe.wait_ge(res_ok, 3 * ND)
            for i in range(NT):
                for a in range(2):
                    if i >= 1:
                        pe.wait_ge(f_ok, 2 * (i - 1) + a + 1)
                    for k in range(4):
                        mm = pe.transpose(bank[5 + a][:, P * k:P * k + P], resT[:, 4 * a + k, i * P:(i + 1) * P], ident[:, :])
                    mm.then_inc(f_t, 1)

        @block.vector
        def _(dve):
            count = [0]

            def link(ins):
                count[0] += 1
                ins.then_inc(dv, 1)
                dve.wait_ge(dv, count[0])

            def bc(ap, shape):
                return ap.to_broadcast(shape)

            dve.wait_ge(vec_t, 1)
            g2 = bank[0][:, 80:86].rearrange("p (a b) -> p a b", b=2)
            gv = gain.rearrange("p (a b) -> p a b", b=2)
            dve.tensor_scalar(gv[:, :, 0], g2[:, :, 0], -HD ** -0.5, None, ALU.mult)
            dve.tensor_copy(gv[:, :, 1], g2[:, :, 1])
            dve.tensor_copy(posT[:, :, :], bank[0][:, 96:96 + CMP_L].rearrange("p (k l) -> p k l", k=2))
            dve.tensor_copy(vecs[:, 0:80], bank[0][:, 0:80]).then_inc(vec_ok, 1)
            dve.wait_ge(silu_e, 1)
            link(dve.tensor_scalar(vecs[:, 88:96], vecs[:, 88:96], 1.0, None, ALU.add))
            link(dve.reciprocal(vecs[:, 88:96], vecs[:, 88:96]))
            dve.tensor_tensor(vecs[:, 80:88], vecs[:, 72:80], vecs[:, 88:96], ALU.mult).then_inc(silu_ok, 1)
            dve.wait_ge(dist_ok, 1)
            for h in range(HEADS):
                dve.tensor_scalar(bias8[:, h, :], work[:, 0, :], 2.0 ** -(h + 1), None, ALU.mult).then_inc(scaled_ok, 1)
            dve.wait_ge(mod_a, 1)
            link(dve.tensor_tensor(mod[:, 0:16], bank[5][:, 0:16], vecs[:, 0:16], ALU.add))
            dve.scalar_tensor_tensor(out=a1, in0=mod[:, 8:16], scalar=1.0, in1=vecs[:, 48:56],
                                     op0=ALU.add, op1=ALU.mult).then_inc(mod_ok, 1)
            dve.wait_ge(mod_ok, 1)
            dve_norm(dve, link, 0, a1, hs_ok)
            dve_project(dve, link, nsa_jobs[:6])

            dve.wait_ge(z_free, 2)
            dve.wait_ge(turned, 4 * 16)
            for kv in range(2):
                for r in range(2):
                    for g in range(2):
                        lanes = slice(HD * r, HD * (r + 1))
                        z = (qkT[lanes, 6 + kv, :] if r == g else kv_turned[kv][lanes, :])\
                            .rearrange("p (n l) -> p l n", l=CMP_STRIDE)[:, r:CMP_STRIDE:2, :]
                        dst = cmp_in[kv][lanes, :, CMP_N * g:CMP_N * g + CMP_N - 1]
                        dve.tensor_copy(dst[:, 0:8, :], z[:, :, 0:CMP_N - 1])
                        dve.tensor_copy(dst[:, 8:16, :], z[:, :, 1:CMP_N])
                for g in range(2):
                    ins = dve.tensor_copy(cmp_in[kv][:, :, CMP_N * (g + 1) - 1:CMP_N * (g + 1)],
                                          posT[:, kv, :].rearrange("p (l a) -> p l a", a=1))
            ins.then_inc(c_dv, 1)
            dve_project(dve, link, nsa_jobs[6:])
            dve.wait_ge(c_pe, 1)
            link(dve.memset(hid[:, :, :], 0.0))
            for m in range(4):
                z = bank[m // 2][:, CMP_N * (m % 2):CMP_N * (m % 2 + 1)]
                ins = dve.tensor_scalar(hid[:, m, 0:31], z[:, 0:31], z[:, 31:32], None, ALU.add)
            link(ins)
            link(dve.tensor_tensor(hid_t[:, :, :], hid[:, :, :], hid[:, :, :], ALU.mult))
            link(dve.tensor_scalar(hid_t[:, :, :], hid_t[:, :, :], 0.044715, 1.0, ALU.mult, ALU.add))
            link(dve.tensor_tensor(hid_t[:, :, :], hid_t[:, :, :], hid[:, :, :], ALU.mult))
            dve.tensor_scalar(hid_t[:, :, :], hid_t[:, :, :], -50.0, None, ALU.max).then_inc(c_dv, 1)
            dve.wait_ge(c_ac, 1)
            link(dve.tensor_scalar(hid_t[:, :, :], hid_t[:, :, :], 1.0, None, ALU.add))
            link(dve.reciprocal(hid_t[:, :, :], hid_t[:, :, :]))
            link(dve.tensor_tensor(hid[:, :, :], hid[:, :, :], hid_t[:, :, :], ALU.mult))
            for r in range(4):
                ins = dve.tensor_copy(hid4[:, :, r, :], hid[:, 2:4, :])
            ins.then_inc(c_dv, 1)
            dve.wait_ge(c_pe, 2)
            kc = bank[4][0:CMP_N, 0:P]
            link(dve.tensor_copy(kc_n[:, :], kc))
            link(dve.tensor_tensor(kc_n[:, :], kc, kc_n[:, :], ALU.mult))
            dve.tensor_reduce(cs[0:CMP_N, 1, 0:2], kc_n[:, :].rearrange("p (g d) -> p g d", g=2), X, ALU.add).then_inc(c_dv, 1)
            dve.wait_ge(c_ac, 2)
            r2, m2, t2 = (cs[0:CMP_N, a, 0:2] for a in (0, 1, 2))
            link(dve.tensor_scalar(m2, m2, 1.0 / HD, EPS, ALU.mult, ALU.add))
            refine_root(dve, link, r2, m2, t2)
            for g in range(2):
                ins = dve.tensor_scalar(kc_n[:, HD * g:HD * g + HD], kc[:, HD * g:HD * g + HD], cs[0:CMP_N, 0, g:g + 1],
                                        None, ALU.mult)
            ins.then_inc(c_dv, 1)
            link(dve.memset(vc_diag, 0.0))
            for g in range(2):
                for h in range(4):
                    ins = dve.tensor_copy(vc_diag[CMP_N * h:CMP_N * (h + 1), g, HD * h:HD * h + HD],
                                          bank[5][CMP_N * h:CMP_N * (h + 1), HD * g:HD * g + HD])
            ins.then_inc(c_dv, 1)
            dve.wait_ge(c_pe, 3)
            dve.tensor_scalar(kcT[:, :], bank[6][:, 0:CMP_N], gain[:, 1:2], None, ALU.mult).then_inc(c_dv, 1)
            dve.wait_ge(dist_ok, 2)
            cb = cmp_bias.rearrange("p (g i h) n -> p g i h n", g=2, i=NT)
            for h in range(HEADS):
                dve.tensor_scalar(cb[:, h // 4, :, h % 4, :], cb[:, h // 4, :, h % 4, :], 0.5 * 2.0 ** -(h + 1), None,
                                  ALU.mult).then_inc(scaled_ok, 1)
            for g in range(2):
                part = slice(16 * g, 16 * g + 16)
                dve.wait_ge(bias_ok, HEADS + 4 * (g + 1))
                dve.wait_ge(c_pe, 4 + g)
                link(dve.tensor_tensor(cmp_s[:, part, :], bank[g][:, :].rearrange("p (h n) -> p h n", n=CMP_N),
                                       cmp_bias[:, part, :], ALU.add))
                link(dve.tensor_reduce(cs[:, 1, part], cmp_s[:, part, :], X, ALU.min))
                dve.tensor_tensor(cmp_s[:, part, :], cmp_s[:, part, :], bc(cs[:, 1, part].unsqueeze(2), [P, 16, CMP_N]),
                                  ALU.subtract).then_inc(c_dv, 1)
            for g in range(2):
                part = slice(16 * g, 16 * g + 16)
                dve.wait_ge(c_ac, 3 + g)
                link(dve.tensor_reduce(cs[:, 2, part], cmp_s[:, part, :], X, ALU.add))
                link(dve.reciprocal(cs[:, 2, part], cs[:, 2, part]))
                c4 = cs[:, 3, part].rearrange("p (i h) -> p i h", i=NT)
                link(dve.tensor_tensor(c4, nsa_gate[:, :, 12 * g:12 * g + 12:3],
                                       cs[:, 2, part].rearrange("p (i h) -> p i h", i=NT), ALU.mult))
                link(dve.tensor_scalar(c4[:, 0, :], c4[:, 0, :], row_ok[:, 0:1], None, ALU.mult))
                dve.tensor_tensor(cmp_s[:, part, :], cmp_s[:, part, :], bc(cs[:, 3, part].unsqueeze(2), [P, 16, CMP_N]),
                                  ALU.mult).then_inc(c_dv, 1)
            for i in range(NT):
                dve.wait_ge(c_pe, 8 + i)
                dve.tensor_copy(omix[:, i, 0:512], bank[4 + i][:, :]).then_inc(c_dv, 1)

            dve.wait_ge(c_dv, C_O)
            dve_attend(dve, link, nsa_steps, True)
            dve.wait_ge(mod_a, 2)
            link(dve.tensor_tensor(mod[:, 16:48], bank[5][:, 16:48], vecs[:, 16:48], ALU.add))
            dve.scalar_tensor_tensor(out=a2, in0=mod[:, 32:40], scalar=1.0, in1=vecs[:, 56:64],
                                     op0=ALU.add, op1=ALU.mult).then_inc(mod_ok, 1)
            dve.wait_ge(mod_ok, 2)
            dve_project(dve, link, moba_jobs)
            dve_attend(dve, link, moba_steps)
            dve_out(dve, 0, mod[:, 16:24], 0)
            dve_norm(dve, link, 1, a2, hs_ok)

            dve.wait_ge(r_pe, 1)
            bv = bank[2][:, :].rearrange("p (m e) -> p e m", e=NEXP)
            dve.tensor_copy(b1T[:, :, 0:8], bv[:, :, 0:8])
            link(dve.tensor_scalar(b1T[:, :, 8:16], bv[:, :, 8:16], 1.0, None, ALU.add))

            dve.wait_ge(r_pe, 2)
            link(dve.tensor_copy(lg, bank[6][:, 0:NT * NEXP].rearrange("p (i e) -> p i e", e=NEXP)))
            for i in range(NT):
                ins = dve.max(m8[:, i, :], lg[:, i, :])
            link(ins)
            link(dve.tensor_scalar(m8[:, :, 7:8], m8[:, :, 0:1], -1.0, None, ALU.mult))
            thr = bc(m8[:, :, TOPK - 1:TOPK], [P, NT, NEXP])
            link(dve.tensor_tensor(sel, lg, thr, ALU.is_gt))
            dve.tensor_tensor(lt, lg, thr, ALU.is_equal).then_inc(lg_ok, 1)
            dve.wait_ge(lg_ok, 1)
            link(dve.tensor_reduce(m8[:, :, 6:7], sel, X, ALU.add))
            link(dve.tensor_scalar(m8[:, :, 6:7], m8[:, :, 6:7], -1.0, float(TOPK), ALU.mult, ALU.add))
            for i in range(NT):
                ins = dve.tensor_tensor_scan(posm[:, i, :], ones[:, 0:NEXP], lt[:, i, :], 0.0, ALU.mult, ALU.add)
            link(ins)
            link(dve.tensor_tensor(posm, posm, bc(m8[:, :, 6:7], [P, NT, NEXP]), ALU.is_le))
            link(dve.tensor_tensor(posm, posm, lt, ALU.mult))
            dve.tensor_tensor(sel, sel, posm, ALU.add).then_inc(sel_ok, 1)
            dve.wait_ge(sel_ok, 1)
            dve.wait_ge(r_ac, NT)
            link(dve.tensor_tensor(gates, gates, sel, ALU.mult))
            link(dve.tensor_reduce(m8[:, :, 5:6], gates, X, ALU.add))
            link(dve.reciprocal(m8[:, :, 5:6], m8[:, :, 5:6]))
            dve.tensor_tensor(gates, gates, bc(m8[:, :, 5:6], [P, NT, NEXP]), ALU.mult).then_inc(sel_ok, 1)
            dve.wait_ge(sel_ok, 2)
            tb = bc(tok_id.unsqueeze(2), [P, NT, NEXP])
            dve.tensor_copy(route[:, :, :, 0], tb)
            dve.tensor_copy(route[:, :, :, 1], tb)
            dve.tensor_copy(route[:, :, :, 2], gates)
            link(dve.memset(route[:, :, :, 3], 1.0))
            dve.wait_ge(r_pe, 3)
            link(dve.scalar_tensor_tensor(out=posm, in0=bank[7][:, 0:NT * NEXP].rearrange("p (i e) -> p i e", e=NEXP),
                                          scalar=1.0, in1=sel, op0=ALU.add, op1=ALU.mult))
            dve.tensor_scalar(posm, posm, -1.0, None, ALU.add)
            link(dve.tensor_copy(cnt[:, 0, :], bank[7][:, NT * NEXP:(NT + 1) * NEXP]))
            link(dve.tensor_scalar(cnt[:, 1, :], cnt[:, 0, :], float(CAP), None, ALU.is_gt))
            for m in (2, 3):
                link(dve.scalar_tensor_tensor(out=cnt[:, 1, :], in0=cnt[:, 0, :], scalar=float(CAP * m), in1=cnt[:, 1, :],
                                              op0=ALU.is_gt, op1=ALU.add))
            link(dve.tensor_tensor_scan(cnt[:, 2, :], ones[:, 0:NEXP], cnt[:, 1, :], 0.0, ALU.mult, ALU.add))
            dve.tensor_scalar(neg_junk, junk, -1.0, None, ALU.mult)
            dve.memset(o_cell[:, 0:1], 0.0)
            dve.tensor_copy(extra_i[0:1, 0:1], cnt[0:1, 2, NEXP - 1:NEXP]).then_inc(r_dv, 1)
            dve.wait_ge(r_dv, 1)
            dve.wait_ge(r_pe, 4)
            dve.tensor_copy(gatesT, bank[6][0:NEXP, :]).then_inc(gT_ok, 1)
            dve.wait_ge(gT_ok, 1)

            def who(sg, e, base):
                for i in range(NT):
                    ins = dve.tensor_scalar(onehot[:, i, :], base, posm[:, i, bass.ds(e, 1)], None, ALU.is_equal)
                ins.then_inc(sg.hot, 1)

            def sources(sg, n):
                dve.wait_ge(sg.idx, n)
                link_in(dve.tensor_copy(meta[:, :], bank[7][:, 0:4]))
                dve.tensor_copy(src_i[:, :], meta[:, 0:1]).then_inc(sg.idx_ok, 1)

            steps = [0]

            def link_in(ins):
                dve.drain()
                return ins

            def targets(sg):
                dve.tensor_copy(meta_c[:, :], meta[:, :])
                dve.drain()
                dve.tensor_scalar(dst_n[:, :], meta_c[:, 3:4], neg_junk, junk, ALU.mult, ALU.add)
                dve.drain()
                dve.tensor_tensor(dst_i[:, :], dst_n[:, :], meta_c[:, 1:2], ALU.add).then_inc(sg.dst, 1)

            def pair_in(sg, n, j):
                dve.wait_ge(sg.u, n + (j + 1))
                if j >= 2:
                    dve.wait_ge(sg.act, n + (j - 1))
                dve.tensor_scalar(g_t[:, j % 2, :], bank[j % 2][:, 0:CAP], b1c[:, j:j + 1], LIMIT,
                                  ALU.add, ALU.min).then_inc(sg.g, 1)
                dve.tensor_scalar(l_t[:, j % 2, :], bank[j % 2][:, CAP:2 * CAP], b1c[:, 8 + j:9 + j], 1.0 - LIMIT,
                                  ALU.add, ALU.max).then_inc(sg.l, 1)

            def pair_out(sg, n, j):
                dve.wait_ge(sg.sig, n + (j + 1))
                dve.tensor_tensor(s_t[:, j % 2, :], s_t[:, j % 2, :], g_t[:, j % 2, :], ALU.mult)
                dve.drain()
                dve.scalar_tensor_tensor(out=actT[:, j, :], in0=l_t[:, j % 2, :], scalar=1.0 + LIMIT,
                                         in1=s_t[:, j % 2, :], op0=ALU.min, op1=ALU.mult).then_inc(sg.act, 1)

            def biases(e):
                dve.tensor_copy(b1c[:, :], b1T[:, bass.ds(e, 1), :].rearrange("p e m -> p (e m)"))
                dve.drain()

            who(main, 0, iota_c[:, :])
            sources(main, 1)
            with dve.Fori(0, NEXP - 1) as b:
                biases(b)
                who(main, b + 1, iota_c[:, :])
                for j in range(8):
                    pair_in(main, b * 8, j)
                    if j >= 1:
                        pair_out(main, b * 8, j - 1)
                    if j == 3:
                        dve.wait_ge(main.y_ok, b * 2 + 2)
                        dve.wait_ge(main.free, b + 1)
                        targets(main)
                        dve.drain()
                        dve.wait_ge(main.got, b * 16 + 16)
                        sources(main, b + 2)
                pair_out(main, b * 8, 7)
            biases(NEXP - 1)
            dve.wait_ge(main.y_ok, 2 * NEXP)
            dve.wait_ge(main.free, NEXP)
            targets(main)
            for j in range(8):
                pair_in(main, 8 * (NEXP - 1), j)
                if j >= 1:
                    pair_out(main, 8 * (NEXP - 1), j - 1)
            pair_out(main, 8 * (NEXP - 1), 7)
            dve.wait_ge(main.free, NEXP + 1)
            extra = dve.value_load(extra_i[0:1, 0:1], min_val=0, max_val=15)
            with dve.If(extra > 0):
                with dve.Fori(0, extra) as o:
                    dve.wait_ge(over.free, o + 1)
                    dve.tensor_scalar(cnt[:, 3, :], cnt[:, 2, :], o_cell[:, 0:1], None, ALU.is_le)
                    dve.drain()
                    dve.tensor_reduce(o_cell[:, 1:2], cnt[:, 3, :], X, ALU.add)
                    dve.tensor_tensor(cnt[:, 3, :], cnt[:, 3, :], cnt[:, 1, :], ALU.mult)
                    dve.drain()
                    dve.tensor_reduce(o_cell[:, 2:3], cnt[:, 3, :], X, ALU.add)
                    dve.drain()
                    dve.tensor_tensor(o_cell[:, 3:4], o_cell[:, 0:1], o_cell[:, 2:3], ALU.subtract)
                    dve.drain()
                    dve.tensor_scalar(o_cell[:, 3:4], o_cell[:, 3:4], 1.0, float(CAP), ALU.add, ALU.mult)
                    dve.drain()
                    dve.tensor_scalar(iota_b[:, :], iota_c[:, :], o_cell[:, 3:4], None, ALU.add)
                    dve.tensor_scalar(o_cell[:, 0:1], o_cell[:, 0:1], 1.0, None, ALU.add)
                    dve.tensor_copy(exp_i[0:1, 0:1], o_cell[0:1, 1:2]).then_inc(exp_ok, 1)
                    dve.wait_ge(exp_ok, o + 1)
                    dve.sem_inc(waited_dve, 1)
                    e = dve.value_load(exp_i[0:1, 0:1], min_val=0, max_val=NEXP - 1)
                    biases(e)
                    who(over, e, iota_b[:, :])
                    sources(over, o + 1)
                    dve.drain()
                    targets(over)
                    for j in range(8):
                        pair_in(over, o * 8, j)
                        if j >= 1:
                            pair_out(over, o * 8, j - 1)
                    pair_out(over, o * 8, 7)
            dve.wait_ge(y_used, NT)
            for t in range(ND):
                dve.scalar_tensor_tensor(out=resT[:, t, :], in0=bank[t][:, :], scalar=mod[:, 40 + t:41 + t],
                                         in1=resT[:, t, :], op0=ALU.mult, op1=ALU.add).then_inc(res_ok, 1)

            dve.wait_ge(lam_in, 16)
            for m in range(2):
                dve.tensor_tensor_reduce(out=lam_rows[:, 2 * m, :], in0=lam_rows[:, 2 * m, :], in1=lam_rows[:, 2 * m + 1, :],
                                         scale=1.0, scalar=0.0, op0=ALU.mult, op1=ALU.add, accum_out=lam[:, m:m + 1])
            dve.tensor_scalar(subln, subln, 1.0 - LAMBDA_INIT, None, ALU.mult)
            link(dve.tensor_copy(lgam[:, 0, :], ret_decays))
            link(dve.tensor_scalar(lgam[:, 1, :], lgam[:, 0, :], -1.0, None, ALU.mult))
            dve.tensor_tensor(lgam[:, 1, :], lgam[:, 0, :], lgam[:, 1, :], ALU.max).then_inc(g_dv, 1)
            dve.wait_ge(g_ac, 2)
            link(dve.tensor_scalar(lam[:, 4:5], lam[:, 2:3], lam[:, 3:4], LAMBDA_INIT, ALU.subtract, ALU.add))
            dve.tensor_scalar(lam[:, 5:6], lam[:, 4:5], -1.0, None, ALU.mult)
            link(dve.tensor_scalar(lgam[:, 3, :], lgam[:, 2, :], 1.0, None, ALU.add))
            dve.tensor_scalar(lgam[:, 5, :], lgam[:, 3, :], 1.0, None, ALU.is_equal)
            link(dve.tensor_scalar(lgam[:, 3, :], lgam[:, 3, :], -1.0, 1e-30, ALU.add, ALU.max))
            link(dve.reciprocal(lgam[:, 3, :], lgam[:, 3, :]))
            link(dve.tensor_tensor(lgam[:, 3, :], lgam[:, 2, :], lgam[:, 3, :], ALU.mult))
            link(dve.tensor_tensor(lgam[:, 3, :], lgam[:, 3, :], lgam[:, 4, :], ALU.mult))
            link(dve.tensor_tensor(lgam[:, 5, :], lgam[:, 5, :], lgam[:, 2, :], ALU.mult))
            link(dve.tensor_tensor(lgam[:, 3, :], lgam[:, 3, :], lgam[:, 5, :], ALU.add))
            link(dve.scalar_tensor_tensor(out=lgam[:, 7, :], in0=lgam[:, 0, :], scalar=0.0, in1=lgam[:, 3, :],
                                          op0=ALU.min, op1=ALU.subtract))
            dve_norm(dve, link, 2, vecs[:, 64:72], h_ok)
            dve.wait_ge(dist_ok, 3)
            link(dve.tensor_scalar(bias4[:, 1, :], bias4[:, 0, :], -1.0, None, ALU.mult))
            link(dve.tensor_tensor(bias4[:, 0, :], bias4[:, 0, :], bias4[:, 1, :], ALU.max))
            for h in (3, 2, 1, 0):
                ins = dve.tensor_scalar(bias4[:, h, :], bias4[:, 0, :], 4.0 ** -(h + 1), None, ALU.mult)
            link(ins)
            dve_project(dve, link, da_jobs)
            dve_attend(dve, link, da_steps)
            dve.wait_ge(o_acc, O_DA)
            for i in range(NT):
                o4 = omix[:, i, 0:512].rearrange("p (h d) -> p h d", h=4)
                t4 = work[:, 0, :].rearrange("p (h d) -> p h d", h=4)
                link(dve.tensor_tensor(t4, o4, o4, ALU.mult))
                dve.tensor_reduce(ms[:, :], t4, X, ALU.add).then_inc(rt_f, 1)
                dve.wait_ge(rt_o, i + 1)
                link(dve.tensor_tensor(o4, o4, bc(ms[:, :].unsqueeze(2), [P, 4, P]), ALU.mult))
                link(dve.tensor_tensor(o4, o4, bc(subln.unsqueeze(1), [P, 4, P]), ALU.mult))
                link(dve.tensor_tensor(omix[:, i, 0:512], omix[:, i, 0:512], gtok[:, i, :], ALU.mult))
            dve_project(dve, link, ret_jobs)
            dve.wait_ge(dist_ok, 4)
            for h in range(4):
                d2 = decay[:, h, :].rearrange("p (a b) -> p a b", a=2)
                dve.tensor_scalar(d2, ret_dist, 0.0, lgam[:, 7, h:h + 1], ALU.max, ALU.mult)
                link(dve.tensor_scalar(ret_tmp, ret_dist, 0.0, lgam[:, 7, 4 + h:5 + h], ALU.min, ALU.mult))
                dve.tensor_tensor(d2, d2, ret_tmp, ALU.subtract).then_inc(g_dv, 1)
                dve.wait_ge(g_dv, 2 + h)

            def decayed(h):
                dve.wait_ge(g_ac, 3 + h)
                for kt in range(NT):
                    dve.wait_ge(rt_s, 4 * h + kt + 1)
                    if h >= 2:
                        dve.wait_ge(rt_pv, 4 * (h - 1))
                    dve.tensor_tensor(ret_s[h % 2][:, kt, :], bank[kt][:, :],
                                      decay[:, h, 384 - P * kt:384 - P * kt + S], ALU.mult).then_inc(rt_d, 1)

            def ret_norm(h):
                oh = omix[:, :, 512 + P * h:512 + P * (h + 1)]
                for i in range(NT):
                    dve.wait_ge(rt_pv, 4 * h + i + 1)
                    dve.tensor_copy(oh[:, i, :], bank[4 + i][:, 0:P]).then_inc(rt_rd, 1)
                dve.wait_ge(rt_rd, 4 * (h + 1))
                t4 = hT[:, 0, :].rearrange("p (i d) -> p i d", i=NT)
                link(dve.tensor_tensor(t4, oh, oh, ALU.mult))
                dve.tensor_reduce(ms[:, :], t4, X, ALU.add).then_inc(rt_f, 1)
                dve.wait_ge(rt_o, NT + h + 1)
                link(dve.tensor_tensor(oh, oh, bc(ms[:, :].unsqueeze(2), [P, NT, P]), ALU.mult))
                dve.tensor_tensor(oh, oh, gtok[:, :, P * h:P * (h + 1)], ALU.mult).then_inc(rt_m, 1)
            for h in range(5):
                if h < 4:
                    decayed(h)
                if h >= 1:
                    ret_norm(h - 1)
            dve_out(dve, 1, None, 2 * ND)


_INS = ["x", "vec_rows", "misc", "ada_w", "w_in", "nsa_cmp_pos", "nsa_cmp_w1", "nsa_cmp_w2", "w_out", "router_w",
        "exp_w1", "exp_b1", "exp_w2", "exp_b2", "w_in_2", "w_out_2"]


def packed(inputs):
    import numpy as _np

    rows = [_np.asarray(inputs[n]).reshape(-1, P) for n in ("ada_b", "ln1_g", "ln2_g", "norm_w_2", "c")]
    for n in ("nsa_q_gain", "nsa_k_gain", "moba_q_gain", "moba_k_gain", "q_norm_w_2", "k_norm_w_2"):
        gain = _np.asarray(inputs[n])
        rows.append(_np.concatenate([gain, gain], axis=1))
    flat = [_np.asarray(inputs[n]) for n in ("lambda_q1_2", "lambda_k1_2", "lambda_q2_2", "lambda_k2_2", "subln_w_2",
                                             "ret_decay_fwd_2", "ret_decay_bwd_2", "router_b")]
    return {**inputs, "vec_rows": _np.concatenate(rows, axis=0), "misc": _np.concatenate(flat, axis=1)}


def kernel(**inputs):
    import numpy as _np
    import concourse.bacc as _bacc
    from concourse.bass_utils import run_bass_kernel_spmd as _run

    nc = _bacc.Bacc("TRN2", target_bir_lowering=False, num_devices=1)
    arrays, args = {}, []
    inputs = packed(inputs)
    for name in _INS:
        a = _np.ascontiguousarray(inputs[name])
        arrays[f"in_{name}_dram"] = a
        args.append(nc.dram_tensor(f"in_{name}_dram", a.shape, mybir.dt.from_np(a.dtype), kind="ExternalInput").ap())
    args.append(nc.dram_tensor("out_0_dram", (1, S, D), F32, kind="ExternalOutput").ap())
    two_block_layer(nc, *args)
    r = _run(nc, [arrays], core_ids=[0])
    return r.results[0]["out_0_dram"]
```

```python
from contextlib import ExitStack

import concourse.bass as bass
from concourse import mybir

F32 = mybir.dt.float32
I32 = mybir.dt.int32
U32 = mybir.dt.uint32
ALU = mybir.AluOpType
ACT = mybir.ActivationFunctionType
X = mybir.AxisListType.X

P = 128
S = 512
D = 1024
NT = S // P
ND = D // P
EPS = 1e-6
NEG = 1e30
HD = 64
HEADS = 8
CMP_N = 32
CMP_L, CMP_STRIDE = 32, 16
NEXP, TOPK, FF = 32, 4, 1024
CAP = 128
SLOTS = 12
SW = 256
FIRST_SLOT = 7
JUNK = S
EARLY = 8
ADA_PE = (1, 4)
ALPHA, LIMIT = 1.702, 7.0
LAMBDA_INIT = 0.2


def chunk_plan():
    plan = [("ada", i, 1) for i in range(EARLY)]
    plan += [("kv_cmp", 0, 1), ("q_nsa", 0, 1), ("q_nsa", 1, 1), ("cmp_w1", 0, 1), ("cmp_w1", 1, 1)]
    plan += [("kv_slc", 0, 1), ("kv_win", 0, 1)]
    plan += [("ada", i, 1) for i in range(EARLY, 16)]
    for i, name in enumerate(("q_moba", "q_moba", "k_moba", "k_moba", "v_moba", "v_moba")):
        plan += [(name, i % 2, 1)]
        plan += [("ada", n, 1) for n in range(16 + 4 * i // 3, 16 + 4 * (i + 1) // 3)]
    plan += [("w_out", i, 1) for i in range(4)]
    at, before = FIRST_SLOT, {}
    for name, part, n in plan:
        before[name, part] = at
        at += n
    moe = at
    assert moe % SLOTS == 0
    after = [("w_in_2", i, 1) for i in range(14)] + [("w_out_2", i, 1) for i in range(4)]
    at = moe + SLOTS * NEXP
    for name, part, n in after:
        before[name, part] = at
        at += n
    return plan, after, before, moe


def two_block_layer(nc, x, vec_rows_in, misc_in, ada_w, w_in, nsa_cmp_pos, nsa_cmp_w1, nsa_cmp_w2, w_out, router_w,
                    exp_w1, exp_b1, exp_w2, exp_b2, w_in_2, w_out_2, out):
    PLAN, AFTER, PLACE, MOE0 = chunk_plan()

    h2_dram = nc.dram_tensor("h2_rows", (S, D), F32, kind="Internal").ap()
    y_dram = nc.dram_tensor("expert_sums", (JUNK + CAP, D), F32, kind="Internal").ap()

    with ExitStack() as ctx:
        def sb(name, shape, dt=F32):
            return ctx.enter_context(nc.sbuf_tensor(name, shape, dt))

        def sem(name):
            return ctx.enter_context(nc.semaphore(name))

        bank = [ctx.enter_context(nc.psum_tensor(f"bank{i}", [P, 512], F32)) for i in range(8)]

        ring = sb("ring", [P, SLOTS, 8, SW])
        ringf = ring[:, :, :, :].rearrange("p s k c -> p (s k c)")
        resT = sb("resT", [P, ND, S])
        hT = sb("hT", [P, ND, S])
        ident = sb("ident", [P, P])
        ones = sb("ones", [P, P])
        head_mean = sb("head_mean", [P, P])
        before_tok = sb("before_tok", [P, P])
        iota_c = sb("iota_c", [P, P])
        vecs = sb("vecs", [P, 96])
        mod = sb("mod", [P, 48])
        small = sb("small", [P, 64])
        ARENA = 18432
        arena = sb("arena", [P, ARENA])

        def room(at, shape, parts=P):
            n = 1
            for s in shape:
                n *= s
            assert at + n <= ARENA, (at, shape)
            ap = arena[0:parts, at:at + n]
            if len(shape) == 1:
                return ap
            if len(shape) == 2:
                return ap.rearrange("p (a b) -> p a b", b=shape[1])
            return ap.rearrange("p (a b c) -> p a b c", b=shape[1], c=shape[2])

        qkT = room(0, [8, S])
        vtok = room(4096, [NT, S])
        gtok = room(6144, [NT, S])
        OM = 8192
        omix = room(OM, [NT, D])
        x_rows = omix
        rows_out = omix
        BI = OM + 4096
        bias8 = room(BI, [HEADS, S])
        bias4 = room(BI, [4, 896])
        decay = room(BI, [4, 896])
        WK = BI + 4096
        work = room(WK, [4, S])
        biased = [work[:, 0, :], work[:, 1, :]]
        probT = [work[:, 2, :], work[:, 3, :]]
        p_nsa, p_moba = qkT[:, 6, :], room(6144, [S])
        sq = [work[:, 0, :], work[:, 1, :]]
        rr = [work[:, 2, :], work[:, 3, :]]
        cmp_in = [room(6144, [16, 2 * CMP_N]), room(7168, [16, 2 * CMP_N])]
        cmp_bias = room(6144, [2 * NT * 4, CMP_N])
        cmp_s = room(7168, [2 * NT * 4, CMP_N])
        cmp_pT = room(WK + 1024, [2, S])
        vc_diag = qkT[:, 6, :].rearrange("p (g c) -> p g c", g=2)
        ada_sum = (2 * [room(6144 + SW * n, [SW]) for n in range(8)] +
                   [omix[:, n // 2, 512 + SW * (n % 2):512 + SW * (n % 2 + 1)] for n in range(8)])
        hid = room(OM + 1536, [4, CMP_N])
        hid4 = room(OM + 1664, [2, 4, CMP_N])
        hid_t = room(OM + 1920, [4, CMP_N])
        posT = sb("posT", [P, 2, CMP_L // 2])
        cw2 = sb("cw2", [P, 2, HD])
        kcT = room(OM + 2560, [CMP_N])
        kc_n = room(OM + 2560 + CMP_N, [P], CMP_N)
        gate_w = room(OM + 2048, [8, 24])
        kv_turned = [room(OM, [S]), room(OM + 512, [S])]
        nsa_gate = sb("nsa_gate", [P, NT, 24])
        xg = room(0, [D])
        xgT = room(1024, [ND, CAP])
        actT = room(2048, [ND, CAP])
        ybuf = room(3072, [D])
        onehot = room(4096, [NT, CAP])
        route = room(4608, [NT, NEXP, 4])
        b1T = room(5120, [NEXP, 16])
        g_t = room(5632, [2, CAP])
        s_t = room(5888, [2, CAP])
        l_t = room(6144, [2, CAP])
        sel = room(6400, [NT, NEXP])
        posm = room(6528, [NT, NEXP])
        gates = room(6656, [NT, NEXP])
        lg = room(6784, [NT, NEXP])
        lt = room(6912, [NT, NEXP])
        cnt = room(7040, [4, NEXP])
        gatesT = room(7168, [S], NEXP)
        lgT = room(7168, [S], NEXP)
        b1_rows = room(OM + 1024, [2 * FF], NEXP)
        y_rows = [room(D * i, [D]) for i in range(NT)]
        rw = room(OM + 3072, [ND, NEXP])
        b2_keep = room(OM, [D], NEXP)
        h2_rows = room(BI, [NT, D])
        vec_rows = room(WK + 512, [P], 86)
        pos_rows = room(WK + 1024, [2 * P], CMP_L // 2)
        da_p = [[biased[0], biased[1]], *([omix[:, a, 512:1024], omix[:, a + 1, 512:1024]] for a in (0, 2))]
        ret_s = [work, qkT[:, 4:8, :]]
        ret_dist = omix[:, 2:4, 512:960]
        ret_tmp = omix[:, 0:2, 512:960]
        m8 = sb("m8", [P, NT, 8])
        b1c = sb("b1c", [P, 16])
        meta = sb("meta", [P, 4])
        meta_c = sb("meta_c", [P, 4])
        iota_b = room(7680, [CAP])
        src_i = sb("src_i", [P, 1], U32)
        dst_i = sb("dst_i", [P, 1], U32)
        dst_n = sb("dst_n", [P, 1])
        extra_i = sb("extra_i", [1, 1], I32)
        exp_i = sb("exp_i", [1, 1], I32)
        mn = sb("mn", [P, 4])
        ls = sb("ls", [P, 4])
        cf = sb("cf", [P, 4])
        cs = sb("cs", [P, 4, 32])
        MISC = 4 * HD + P + 8 + NEXP
        misc = sb("misc", [P, MISC])
        lam_rows = misc[:, 0:4 * HD].rearrange("p (a b) -> p a b", b=HD)
        subln = misc[:, 4 * HD:4 * HD + P]
        ret_decays = misc[:, 4 * HD + P:4 * HD + P + 8]
        rb_row = misc[:, 4 * HD + P + 8:MISC]
        lgam = sb("lgam", [P, 8, 8])
        ms = sb("ms", [P, 4])

        eps_c, tok_c, junk_c, valid_c = 0, 1, 5, 6
        a1_c, g_c, a2_c, lam_c, o_c = 10, 18, 24, 32, 40
        tok_id = small[:, tok_c:tok_c + NT]
        junk = small[:, junk_c:junk_c + 1]
        row_ok = small[:, valid_c:valid_c + NT]
        a1, a2 = small[:, a1_c:a1_c + 8], small[:, a2_c:a2_c + 8]
        gain = small[:, g_c:g_c + 6]
        lam = small[:, lam_c:lam_c + 6]
        o_cell = small[:, o_c:o_c + 4]
        neg_junk = small[:, 44:45]
        eps = small[:, eps_c:eps_c + 1]

        landed = [sem(f"landed{s}") for s in range(SLOTS)]
        ada_read, ada_done = sem("ada_read"), sem("ada_done")
        slot_used = sem("slot_used")
        vec_in, x_in, gate_in = sem("vec_in"), sem("x_in"), sem("gate_in")
        q_in = sem("q_in")
        rt_in, lam_in, b_in = sem("rt_in"), sem("lam_in"), sem("b_in")
        pool_c = sem("pool_c")
        consts = sem("consts")
        dv = sem("dv")
        ac = sem("ac")
        vec_t, vec_ok = sem("vec_t"), sem("vec_ok")
        xt_t, xt_ok = sem("xt_t"), sem("xt_ok")
        silu_e, silu_ok = sem("silu_e"), sem("silu_ok")
        mod_a, mod_ok = sem("mod_a"), sem("mod_ok")
        sq_ok, sum_ok, rstd_ok, hs_ok, h_ok = sem("sq_ok"), sem("sum_ok"), sem("rstd_ok"), sem("hs_ok"), sem("h_ok")
        z_done, z_sq, z_mean, z_r, z_free = sem("z_done"), sem("z_sq"), sem("z_mean"), sem("z_r"), sem("z_free")
        dist_ok, scaled_ok, bias_ok = sem("dist_ok"), sem("scaled_ok"), sem("bias_ok")
        s_done, s_bias, s_exp, t_done, t_ok, o_done, o_acc = (
            sem(n) for n in ("s_done", "s_bias", "s_exp", "t_done", "t_ok", "o_done", "o_acc"))
        w_ok = sem("w_ok")
        c_in, c_pe, c_dv, c_ac = sem("c_in"), sem("c_pe"), sem("c_dv"), sem("c_ac")
        mixT_t, mixT_ok, out_t, res_ok = sem("mixT_t"), sem("mixT_ok"), sem("out_t"), sem("res_ok")
        r_pe, r_dv, r_ac, h2_t, h2_ok, h2_out = (
            sem(n) for n in ("r_pe", "r_dv", "r_ac", "h2_t", "h2_ok", "h2_out"))

        class BlockSignals:
            def __init__(self, n):
                self.hot, self.idx, self.idx_ok, self.got, self.xt, self.xt_ok = (
                    sem(n + w) for w in ("hot", "idx", "idx_ok", "got", "xt", "xt_ok"))
                self.u, self.g, self.sig, self.act, self.y, self.y_ok, self.put = (
                    sem(n + w) for w in ("u", "g", "sig", "act", "y", "y_ok", "put"))
                self.free, self.dst, self.l = sem(n + "free"), sem(n + "dst"), sem(n + "l")
        main, over = BlockSignals("m_"), BlockSignals("o_")
        waited_sp, waited_pe, waited_dve, waited_pool = (sem("waited_" + n) for n in ("sp", "pe", "dve", "pool"))
        exp_ok, over_done, over_in = sem("exp_ok"), sem("over_done"), sem("over_in")
        y_in = [sem(f"y_in{i}") for i in range(NT)]
        y_zero, turned = sem("y_zero"), sem("turned")
        y_used = sem("y_used")
        f_t, f_ok, f_out = sem("f_t"), sem("f_ok"), sem("f_out")
        g_dv, g_ac = sem("g_dv"), sem("g_ac")
        rt_s, rt_d, rt_o, rt_f = sem("rt_s"), sem("rt_d"), sem("rt_o"), sem("rt_f")
        rt_pv, rt_rd, rt_m = sem("rt_pv"), sem("rt_rd"), sem("rt_m")
        lgT_ok, lg_ok, sel_ok, gT_ok = sem("lgT_ok"), sem("lg_ok"), sem("sel_ok"), sem("gT_ok")
        CMP_BANK = (3, 4, 7, 5)
        C_LAID, C_CUBE, C_HID, C_SQ, C_KN, C_VD, C_KT, C_S, C_P, C_O = 1, 2, 3, 4, 5, 6, 7, 8, 10, 15

        last_of, reads, by_pe, by_dve = {}, {}, 0, 0
        for name, part, _ in PLAN:
            dve_reads = name == "ada" and part not in ADA_PE
            by_dve, by_pe = by_dve + dve_reads, by_pe + (not dve_reads)
            reads[PLACE[name, part]] = -by_dve if dve_reads else by_pe
        USED0 = by_pe
        for name, part, _ in PLAN:
            last_of[PLACE[name, part]] = reads.get(PLACE[name, part] - SLOTS, 0)
        for n, (name, part, _) in enumerate(AFTER):
            last_of[PLACE[name, part]] = USED0 + SLOTS * (NEXP - 1) + n + 1

        def slot(n):
            return n % SLOTS

        def fill_of(n):
            return (n - slot(n)) // SLOTS + (0 if slot(n) < FIRST_SLOT else 1)

        def arrived(eng, name, part=0, slots=1):
            n = PLACE[name, part]
            for m in range(n, n + slots):
                eng.wait_ge(landed[slot(m)], 16 * fill_of(m))

        def chunk(name, part=0):
            return ring[:, slot(PLACE[name, part]), :, :]

        def t_job(name, part, col, dst, g=None, scale=None):
            return dict(kind="T", name=name, part=part, col=col, dst=dst,
                        how="norm" if g is not None else "plain", g=g, scale=scale)

        def v_job(name, part, col, width, i0, dst, how="plain"):
            return dict(kind="V", name=name, part=part, col=col, width=width, i0=i0, dst=dst, how=how,
                        g=None, scale=None)

        nsa_jobs = [t_job("kv_cmp", 0, 0, qkT[:, 6, :]), t_job("kv_cmp", 0, P, qkT[:, 7, :])]
        nsa_jobs += [t_job("q_nsa", t // 2, P * (t % 2), qkT[:, t, :], 0) for t in range(4)]
        nsa_jobs += [dict(kind="G", how="sigmoid", dst=nsa_gate[:, :, :], name=None, g=None, scale=None)]
        nsa_jobs += [t_job("kv_slc", 0, 0, qkT[:, 4, :], 1),
                     v_job("kv_slc", 0, P, P, 0, vtok[:, :, 0:P])]
        nsa_jobs += [t_job("kv_win", 0, 0, qkT[:, 5, :], 1),
                     v_job("kv_win", 0, P, P, 0, vtok[:, :, P:2 * P])]
        moba_jobs = [t_job("q_moba", t // 2, P * (t % 2), qkT[:, t, :], 2) for t in range(4)]
        moba_jobs += [t_job("k_moba", t // 2, P * (t % 2), qkT[:, 4 + t, :], 3) for t in range(4)]
        moba_jobs += [v_job("v_moba", c, 0, SW, 2 * i, vtok[:, 2 * i:2 * i + 2, SW * c:SW * c + SW])
                      for c in range(2) for i in range(2)]
        da_jobs = [t_job("w_in_2", t // 2, P * (t % 2), qkT[:, t, :], 4) for t in range(4)]
        da_jobs += [t_job("w_in_2", 2 + t // 2, P * (t % 2), qkT[:, 4 + t, :], 5) for t in range(4)]
        da_jobs += [v_job("w_in_2", 4 + c, 0, SW, 2 * i, vtok[:, 2 * i:2 * i + 2, SW * c:SW * c + SW])
                    for c in range(2) for i in range(2)]
        da_jobs += [v_job("w_in_2", 6 + c, 0, SW, 2 * i, gtok[:, 2 * i:2 * i + 2, SW * c:SW * c + SW], "silu")
                    for c in range(2) for i in range(2)]
        ret_jobs = [t_job("w_in_2", 8, P * t, qkT[:, t, :], scale=HD ** -0.5) for t in range(2)]
        ret_jobs += [t_job("w_in_2", 9, P * t, qkT[:, 2 + t, :]) for t in range(2)]
        ret_jobs += [v_job("w_in_2", 10 + c, 0, SW, 2 * i, vtok[:, 2 * i:2 * i + 2, SW * c:SW * c + SW])
                     for c in range(2) for i in range(2)]
        ret_jobs += [v_job("w_in_2", 12 + c, 0, SW, 2 * i, gtok[:, 2 * i:2 * i + 2, SW * c:SW * c + SW], "silu")
                     for c in range(2) for i in range(2)]
        at = norms = rs = 0
        for jobs in (nsa_jobs, moba_jobs, da_jobs, ret_jobs):
            for n, j in enumerate(jobs):
                j.update(at=at, norm_at=norms, r_at=rs)
                j["last_of_chunk"] = j["name"] is not None and (
                    n + 1 == len(jobs) or (jobs[n + 1]["name"], jobs[n + 1].get("part")) != (j["name"], j.get("part")))
                at += 1
                norms += j["how"] == "norm"
                rs += j["how"] != "plain"

        def z_bank(j):
            return bank[j["at"] % 3]

        def mean_bank(j):
            return bank[3 + j["norm_at"] % 2]

        def pe_project(pe, jobs, h0=None, after={}):
            def mean(j):
                pe.wait_ge(z_sq, j["norm_at"] + 1)
                if j["norm_at"] >= 2:
                    pe.wait_ge(z_free, n_done_before(ALL_JOBS, j["norm_at"] - 2))
                pe.matmul(mean_bank(j)[:, :], head_mean[:, :], sq[j["norm_at"] % 2], start=True, stop=True)\
                  .then_inc(z_mean, 1)
            waiting = []
            for j in jobs:
                if j["at"] >= 3:
                    pe.wait_ge(z_free, j["at"] - 2)
                if j["name"]:
                    arrived(pe, j["name"], j["part"])
                if j["name"] == "q_nsa":
                    pe.wait_ge(q_in, 16 * 6)
                z = z_bank(j)
                if j["kind"] == "T":
                    for k in range(ND):
                        if j is jobs[0] and h0 is not None:
                            pe.wait_ge(h_ok, h0 + k + 1)
                        w = chunk(j["name"], j["part"])[:, k, j["col"]:j["col"] + P]
                        mm = pe.matmul(z[:, :], w, hT[:, k, :], start=(k == 0), stop=(k == ND - 1))
                        if k == 1 and waiting:
                            mean(waiting.pop())
                elif j["kind"] == "V":
                    wd = j["width"]
                    for n in range(S // wd):
                        for k in range(ND):
                            i = j["i0"] + n
                            mm = pe.matmul(z[:, n * wd:(n + 1) * wd], hT[:, k, i * P:(i + 1) * P],
                                           chunk(j["name"], j["part"])[:, k, j["col"]:j["col"] + wd],
                                           start=(k == 0), stop=(k == ND - 1))
                        if n == 0 and waiting:
                            mean(waiting.pop())
                else:
                    pe.wait_ge(gate_in, 16)
                    for i in range(NT):
                        for k in range(ND):
                            mm = pe.matmul(z[:, 24 * i:24 * i + 24], hT[:, k, i * P:(i + 1) * P],
                                           gate_w[:, k, :], start=(k == 0), stop=(k == ND - 1))
                        if i == 0 and waiting:
                            mean(waiting.pop())
                mm.then_inc(z_done, 1)
                if j["last_of_chunk"]:
                    slots_read(pe)
                if j["how"] == "norm":
                    waiting.append(j)
                if j["at"] in after:
                    after[j["at"]]()
            if waiting:
                mean(waiting.pop())

        def slots_read(pe, n=1):
            pe.matmul(bank[7][0:32, 510:512], ident[:, 0:32], ident[:, 0:2], start=True, stop=True,
                      skip_group_check=True).then_inc(slot_used, n)

        def job_z(j):
            z = z_bank(j)
            if j["kind"] == "T":
                return z[:, :]
            if j["kind"] == "V":
                return z[:, :].rearrange("p (n w) -> p n w", w=j["width"])
            return z[:, 0:96].rearrange("p (n w) -> p n w", w=24)

        def job_r(j):
            r = rr[j["r_at"] % 2]
            if j["kind"] == "T":
                return r
            if j["kind"] == "V":
                return r.rearrange("p (n w) -> p n w", w=j["width"])
            return r[:, 0:96].rearrange("p (n w) -> p n w", w=24)

        def refine_root(dve, link, r, m, t):
            link(dve.tensor_tensor(t, r, r, ALU.mult))
            link(dve.tensor_tensor(t, m, t, ALU.mult))
            link(dve.tensor_scalar(t, t, -0.5, 1.5, ALU.mult, ALU.add))
            link(dve.tensor_tensor(r, r, t, ALU.mult))

        def refine_root_of(dve, link, r, z, scale, t):
            link(dve.tensor_tensor(t, r, r, ALU.mult))
            link(dve.scalar_tensor_tensor(out=t, in0=z, scalar=EPS / scale, in1=t, op0=ALU.add, op1=ALU.mult))
            link(dve.tensor_scalar(t, t, -0.5 * scale, 1.5, ALU.mult, ALU.add))
            link(dve.tensor_tensor(r, r, t, ALU.mult))

        def r_done_before(jobs_all, n):
            for j in jobs_all:
                if j["how"] != "plain" and j["r_at"] == n:
                    return j["at"] + 1

        def n_done_before(jobs_all, n):
            for j in jobs_all:
                if j["how"] == "norm" and j["norm_at"] == n:
                    return j["at"] + 1

        ALL_JOBS = nsa_jobs + moba_jobs + da_jobs + ret_jobs

        def act_project(act, link, jobs, after={}):
            for j in jobs:
                if j["how"] == "plain":
                    continue
                act.wait_ge(z_done, j["at"] + 1)
                if j["r_at"] >= 2:
                    act.wait_ge(z_free, r_done_before(ALL_JOBS, j["r_at"] - 2))
                if j["how"] == "norm":
                    if j["norm_at"] >= 2:
                        act.wait_ge(z_free, n_done_before(ALL_JOBS, j["norm_at"] - 2))
                    act.activation(sq[j["norm_at"] % 2], z_bank(j)[:, :], ACT.Square).then_inc(z_sq, 1)
                    act.wait_ge(z_mean, j["norm_at"] + 1)
                    link(act.activation(job_r(j), mean_bank(j)[:, :], ACT.Ln, bias=eps))
                    act.activation(job_r(j), job_r(j), ACT.Exp, scale=-0.5).then_inc(z_r, 1)
                else:
                    act.activation(job_r(j), job_z(j), ACT.Sigmoid).then_inc(z_r, 1)
                if j["at"] in after:
                    after[j["at"]]()

        def dve_project(dve, link, jobs, after={}):
            for j in jobs:
                if j["how"] == "plain":
                    dve.wait_ge(z_done, j["at"] + 1)
                    if j["scale"] is not None:
                        ins = dve.tensor_scalar(j["dst"], job_z(j), j["scale"], None, ALU.mult)
                    else:
                        ins = dve.tensor_copy(j["dst"], job_z(j))
                else:
                    dve.wait_ge(z_r, j["r_at"] + 1)
                    if j["how"] == "norm":
                        g = gain[:, j["g"]:j["g"] + 1]
                        refine_root_of(dve, link, job_r(j), mean_bank(j)[:, :], 1.0, sq[j["norm_at"] % 2])
                        ins = dve.scalar_tensor_tensor(out=j["dst"], in0=job_z(j), scalar=g, in1=job_r(j),
                                                       op0=ALU.mult, op1=ALU.mult)
                    elif j["how"] == "silu":
                        ins = dve.tensor_tensor(j["dst"], job_z(j), job_r(j), ALU.mult)
                    else:
                        ins = dve.tensor_copy(j["dst"], job_r(j))
                ins.then_inc(z_free, 1)
                if j["at"] in after:
                    after[j["at"]]()

        nsa_steps, moba_steps, da_steps = [], [], []
        for br in range(2):
            for h in [0, 4, 1, 5, 2, 6, 3, 7]:
                half = HD * (h // 4)
                for i in range(NT):
                    nsa_steps.append(dict(
                        q=qkT[half:half + HD, h % 4, i * P:(i + 1) * P], k=qkT[half:half + HD, 4 + br, 0:P * (i + 1)],
                        v=lambda kt, br=br: vtok[:, kt, P * br:P * br + P], vw=HD, v0=half,
                        bias=bias8[:, h, S - P * (i + 1):S], blocks=i + 1,
                        over=nsa_gate[:, i, 3 * h + br + 1:3 * h + br + 2], dst=omix[:, i, HD * h:HD * h + HD], add=True))
        for h in range(HEADS):
            half = HD * (h % 2)
            for i in range(NT):
                moba_steps.append(dict(
                    q=qkT[half:half + HD, h // 2, i * P:(i + 1) * P], k=qkT[half:half + HD, 4 + h // 2, 0:P * (i + 1)],
                    v=lambda kt, h=h: vtok[:, kt, P * (h // 2):P * (h // 2) + P], vw=HD, v0=half,
                    bias=bias8[:, h, S - P * (i + 1):S], blocks=i + 1,
                    over=None, dst=omix[:, i, 512 + HD * h:512 + HD * h + HD], add=False))
        for h in range(4):
            for i in range(NT):
                da_steps.append(dict(
                    q=[qkT[HD * m:HD * m + HD, h, i * P:(i + 1) * P] for m in range(2)],
                    k=[qkT[HD * m:HD * m + HD, 4 + h, :] for m in range(2)],
                    v=lambda kt, h=h: vtok[:, kt, P * h:P * h + P],
                    bias=bias4[:, h, 384 - P * i:384 - P * i + S], dst=omix[:, i, P * h:P * h + P]))
        at = 0
        for steps in (nsa_steps, moba_steps, da_steps):
            for st in steps:
                st["at"] = at
                if steps is not da_steps:
                    st["p"] = (*biased, p_nsa if steps is nsa_steps else p_moba)[at % 3]
                at += 1
        O_NSA, O_MOBA, O_DA = len(nsa_steps), len(nsa_steps) + len(moba_steps), at
        S_DA = O_MOBA + 2 * len(da_steps)

        def pe_attend(pe, steps, banks_free=None):
            def scores(st):
                n = st["at"]
                if n >= 3:
                    pe.wait_ge(s_bias, n - 2)
                pe.matmul(bank[n % 3][:, 0:P * st["blocks"]], st["q"], st["k"], start=True, stop=True)\
                  .then_inc(s_done, 1)

            def turn(st):
                n = st["at"]
                pe.wait_ge(s_exp, n + 1)
                if st is steps[0] and banks_free:
                    banks_free()
                if n >= 3:
                    pe.wait_ge(t_ok, n - 2)
                for b in range(st["blocks"]):
                    mm = pe.transpose(bank[3 + n % 3][:, b * P:(b + 1) * P], st["p"][:, b * P:(b + 1) * P],
                                      ident[:, :])
                mm.then_inc(t_done, 1)

            def values(st):
                n = st["at"]
                pe.wait_ge(t_ok, n + 1)
                if n >= 2:
                    pe.wait_ge(o_acc, n - 1)
                for b in range(st["blocks"]):
                    mm = pe.matmul(bank[6 + n % 2][:, 0:P], probT[n % 2][:, b * P:(b + 1) * P], st["v"](b),
                                   start=(b == 0), stop=(b == st["blocks"] - 1))
                mm.then_inc(o_done, 1)
            for n in range(len(steps) + 3):
                if n < len(steps):
                    scores(steps[n])
                if 2 <= n <= len(steps) + 1:
                    turn(steps[n - 2])
                if n >= 3:
                    values(steps[n - 3])

        def act_attend(act, steps):
            def copy(st):
                n = st["at"]
                act.wait_ge(t_done, n + 1)
                if n >= 2:
                    act.wait_ge(o_done, n - 1)
                w = P * st["blocks"]
                act.activation(probT[n % 2][:, 0:w], bank[3 + n % 3][:, 0:w], ACT.Copy).then_inc(t_ok, 1)
            for m, st in enumerate(steps):
                n, w = st["at"], P * st["blocks"]
                if m >= 2:
                    copy(steps[m - 2])
                act.wait_ge(s_bias, n + 1)
                if n >= 4:
                    act.wait_ge(o_acc, n - 3)
                act.activation(st["p"][:, 0:w], st["p"][:, 0:w], ACT.Exp, scale=-1.0,
                               bias=mn[:, n % 4:n % 4 + 1], accum_out=ls[:, n % 4:n % 4 + 1]).then_inc(s_exp, 1)
            for st in steps[-2:]:
                copy(st)

        ADA_DVE = [ch for ch in range(24) if ch not in ADA_PE]
        EARLY_DVE = EARLY - len(ADA_PE)

        def modulate_part(dve, m):
            ch, k = ADA_DVE[m // ND], m % ND
            if k == 0:
                arrived(dve, "ada", ch)
            w, s = chunk("ada", ch)[:, k, :], vecs[:, 80 + k:81 + k]
            if k == 0:
                ins = dve.tensor_scalar(ada_sum[ch], w, s, None, ALU.mult)
            else:
                dve.wait_ge(ada_done, m)
                ins = dve.scalar_tensor_tensor(out=ada_sum[ch], in0=w, scalar=s, in1=ada_sum[ch],
                                               op0=ALU.mult, op1=ALU.add)
            ins.then_inc(ada_done, 1)
            if k == ND - 1:
                dve.wait_ge(ada_done, m + 1)
                dve.sem_inc(ada_read, 1)

        def dve_attend(dve, link, steps, beside=False):
            def accumulate(st):
                n = st["at"]
                c = cf[:, n % 4:n % 4 + 1]
                dve.wait_ge(s_exp, n + 1)
                link(dve.reciprocal(c, ls[:, n % 4:n % 4 + 1]))
                if st["over"] is not None:
                    link(dve.tensor_tensor(c, st["over"], c, ALU.mult))
                dve.wait_ge(o_done, n + 1)
                if n >= 1:
                    dve.wait_ge(o_acc, n)
                if st["add"]:
                    ins = dve.scalar_tensor_tensor(out=st["dst"], in0=bank[6 + n % 2][:, st["v0"]:st["v0"] + st["vw"]], scalar=c,
                                                   in1=st["dst"], op0=ALU.mult, op1=ALU.add)
                else:
                    ins = dve.tensor_scalar(st["dst"], bank[6 + n % 2][:, st["v0"]:st["v0"] + st["vw"]], c, None, ALU.mult)
                ins.then_inc(o_acc, 1)
            for m in range(len(steps) + 3):
                if m < len(steps):
                    st = steps[m]
                    n, w = st["at"], P * st["blocks"]
                    dve.wait_ge(s_done, n + 1)
                    if n >= 3:
                        dve.wait_ge(t_done, n - 2)
                    dve.tensor_tensor_reduce(out=st["p"][:, 0:w], in0=bank[n % 3][:, 0:w], in1=st["bias"],
                                             scale=1.0, scalar=3e38, op0=ALU.add, op1=ALU.min,
                                             accum_out=mn[:, n % 4:n % 4 + 1]).then_inc(s_bias, 1)
                if beside and m < len(steps):
                    modulate_part(dve, EARLY_DVE * ND + m)
                if m >= 3:
                    accumulate(steps[m - 3])

        def pe_da(pe):
            def scores(st):
                for m in range(2):
                    n = O_MOBA + 2 * (st["at"] - O_MOBA) + m
                    if n >= O_MOBA + 4:
                        pe.wait_ge(s_bias, n - 3)
                    pe.matmul(bank[n % 4][:, :], st["q"][m], st["k"][m], start=True, stop=True).then_inc(s_done, 1)

            def turn(st):
                n = st["at"]
                pe.wait_ge(w_ok, n - O_MOBA + 1)
                if n >= O_MOBA + 2:
                    pe.wait_ge(t_ok, n - 1)
                for b in range(NT):
                    mm = pe.transpose(bank[4 + n % 2][:, b * P:(b + 1) * P], da_p[(n - O_MOBA) % 3][0][:, b * P:(b + 1) * P],
                                      ident[:, :])
                mm.then_inc(t_done, 1)

            def values(st):
                n = st["at"]
                pe.wait_ge(t_ok, n + 1)
                pe.wait_ge(o_acc, n - 1)
                for b in range(NT):
                    mm = pe.matmul(bank[6 + n % 2][:, 0:P], probT[n % 2][:, b * P:(b + 1) * P], st["v"](b),
                                   start=(b == 0), stop=(b == NT - 1))
                mm.then_inc(o_done, 1)
            for n in range(len(da_steps) + 3):
                if n < len(da_steps):
                    scores(da_steps[n])
                if 2 <= n <= len(da_steps) + 1:
                    turn(da_steps[n - 2])
                if n >= 3:
                    values(da_steps[n - 3])

        def act_da(act):
            def copy(st):
                n = st["at"]
                act.wait_ge(t_done, n + 1)
                act.wait_ge(o_done, n - 1)
                act.activation(probT[n % 2], bank[4 + n % 2][:, :], ACT.Copy).then_inc(t_ok, 1)
            for j, st in enumerate(da_steps):
                for m in range(2):
                    n = O_MOBA + 2 * j + m
                    act.wait_ge(s_bias, n + 1)
                    if j >= 2:
                        act.wait_ge(w_ok, j - 1)
                    act.activation(da_p[j % 3][m], da_p[j % 3][m], ACT.Exp, scale=-1.0,
                                   bias=mn[:, n % 4:n % 4 + 1], accum_out=ls[:, n % 4:n % 4 + 1]).then_inc(s_exp, 1)
                if j >= 2:
                    copy(da_steps[j - 2])
            for st in da_steps[-2:]:
                copy(st)

        def dve_da(dve, link):
            def difference(j):
                n = O_MOBA + 2 * j
                c = cf[:, n % 4:n % 4 + 2]
                p0, p1 = da_p[j % 3]
                dve.wait_ge(s_exp, n + 2)
                link(dve.reciprocal(c, ls[:, n % 4:n % 4 + 2]))
                dve.tensor_tensor(c[:, 1:2], lam[:, 5:6], c[:, 1:2], ALU.mult)
                link(dve.tensor_scalar(p0, p0, c[:, 0:1], None, ALU.mult))
                dve.scalar_tensor_tensor(out=p0, in0=p1, scalar=c[:, 1:2], in1=p0, op0=ALU.mult, op1=ALU.add)\
                   .then_inc(w_ok, 1)

            def take(st):
                dve.wait_ge(o_done, st["at"] + 1)
                dve.tensor_copy(st["dst"], bank[6 + st["at"] % 2][:, 0:P]).then_inc(o_acc, 1)
            for j in range(len(da_steps) + 3):
                if j < len(da_steps):
                    if j >= 3:
                        dve.wait_ge(t_done, O_MOBA + j - 2)
                    for m in range(2):
                        n = O_MOBA + 2 * j + m
                        dve.wait_ge(s_done, n + 1)
                        dve.tensor_tensor_reduce(out=da_p[j % 3][m], in0=bank[n % 4][:, :], in1=da_steps[j]["bias"],
                                                 scale=1.0, scalar=3e38, op0=ALU.add, op1=ALU.min,
                                                 accum_out=mn[:, n % 4:n % 4 + 1]).then_inc(s_bias, 1)
                if 1 <= j <= len(da_steps):
                    difference(j - 1)
                if j >= 3:
                    take(da_steps[j - 3])

        def act_norm(act, link, r):
            for t in range(ND):
                n = ND * r + t
                if r:
                    act.wait_ge(res_ok, n - ND + 1)
                if t >= 2:
                    act.wait_ge(sum_ok, n - 1)
                act.activation(sq[t % 2], resT[:, t, :], ACT.Square).then_inc(sq_ok, 1)
            act.wait_ge(sum_ok, ND * (r + 1))
            link(act.activation(rr[0], bank[0][:, :], ACT.Ln, scale=1.0 / D, bias=eps))
            act.activation(rr[0], rr[0], ACT.Exp, scale=-0.5).then_inc(rstd_ok, 1)

        def pe_norm(pe, r, tiles=range(ND)):
            for t in tiles:
                pe.wait_ge(sq_ok, ND * r + t + 1)
                pe.matmul(bank[0][:, :], ones[:, :], sq[t % 2], start=(t == 0), stop=(t == ND - 1)).then_inc(sum_ok, 1)

        def dve_norm(dve, link, r, scale, done):
            dve.wait_ge(rstd_ok, r + 1)
            refine_root_of(dve, link, rr[0], bank[0][:, :], 1.0 / D, sq[0])
            for t in range(ND):
                dve.scalar_tensor_tensor(out=hT[:, t, :], in0=resT[:, t, :], scalar=scale[:, t:t + 1], in1=rr[0],
                                         op0=ALU.mult, op1=ALU.mult).then_inc(done, 1)

        def act_shift(act, r, shift):
            for t in range(ND):
                act.wait_ge(hs_ok, ND * r + t + 1)
                act.activation(hT[:, t, :], hT[:, t, :], ACT.Identity, bias=shift[:, t:t + 1]).then_inc(h_ok, 1)

        def pe_out(pe, r, name, res0):
            for t in range(ND):
                if t >= 2:
                    pe.wait_ge(mixT_ok, ND * r + t - 1)
                for i in range(NT):
                    mm = pe.transpose(bank[t % 2][:, i * P:(i + 1) * P], omix[:, i, t * P:(t + 1) * P], ident[:, :])
                mm.then_inc(mixT_t, 1)
            pe.wait_ge(mixT_ok, ND * (r + 1))
            for n in range(ND):
                if n % 2 == 0:
                    arrived(pe, name, n // 2)
                if n >= 3:
                    pe.wait_ge(res_ok, res0 + n - 2)
                for k in range(ND):
                    mm = pe.matmul(bank[2 + n % 3][:, :], chunk(name, n // 2)[:, k, P * (n % 2):P * (n % 2) + P],
                                   hT[:, k, :], start=(k == 0), stop=(k == ND - 1))
                mm.then_inc(out_t, 1)
                if r == 0 and n >= 2:
                    pe_norm(pe, 1, [n - 2])
                if r == 1 and n >= 2:
                    result_rows(pe, n - 2)
                if n % 2 and (r == 1 or n < ND - 1):
                    slots_read(pe)

        def result_rows(pe, t):
            pe.wait_ge(res_ok, 2 * ND + t + 1)
            if t >= 2:
                pe.wait_ge(f_ok, t - 1)
            for i in range(NT):
                mm = pe.transpose(bank[5 + t % 2][:, P * i:P * i + P], resT[:, t, i * P:(i + 1) * P], ident[:, :])
            mm.then_inc(f_t, 1)

        def act_out(act, r):
            for t in range(ND):
                act.wait_ge(mixT_t, ND * r + t + 1)
                act.activation(hT[:, t, :], bank[t % 2][:, :], ACT.Copy).then_inc(mixT_ok, 1)

        def dve_out(dve, r, scale, res0):
            for n in range(ND):
                dve.wait_ge(out_t, ND * r + n + 1)
                if scale is None:
                    ins = dve.tensor_tensor(resT[:, n, :], bank[2 + n % 3][:, :], resT[:, n, :], ALU.add)
                else:
                    ins = dve.scalar_tensor_tensor(out=resT[:, n, :], in0=bank[2 + n % 3][:, :],
                                                   scalar=scale[:, n:n + 1], in1=resT[:, n, :], op0=ALU.mult, op1=ALU.add)
                ins.then_inc(res_ok, 1)

        OUT_PARTS = ((0, 4), (4, 6), (6, 8))

        block = ctx.enter_context(nc.Block())

        @block.sync
        def _(sp):
            def rows(ap):
                return ap.rearrange("(k p) n -> p k n", p=P)

            def load(name, part, n, m):
                if n - SLOTS >= FIRST_SLOT:
                    if last_of[n] < 0:
                        sp.wait_ge(ada_read, -last_of[n])
                    else:
                        sp.wait_ge(slot_used, last_of[n])
                dst = ring[:, slot(n), :, :]
                if name == "ada":
                    sp.dma_start(dst, rows(ada_w[0])[:, :, SW * part:SW * (part + 1)]).then_inc(landed[slot(n)], 16)
                elif name == "q_nsa":
                    for t in range(2):
                        for g in range(2):
                            c0 = HD * (2 * part + t + 4 * g)
                            sp.dma_start(dst[:, :, P * t + HD * g:P * t + HD * (g + 1)], rows(w_in[0])[:, :, c0:c0 + HD])\
                              .then_inc(landed[slot(n)] if (t, g) == (1, 1) else q_in, 16)
                elif name == "cmp_w1":
                    sp.dma_start(dst.rearrange("p k c -> p (k c)").rearrange("p (m h) -> p m h", h=P),
                                 nsa_cmp_w1[0, part].rearrange("(m q) h -> q m h", q=P)).then_inc(landed[slot(n)], 16)
                else:
                    src, c0 = {"kv_cmp": (w_in, 512), "kv_slc": (w_in, 768), "kv_win": (w_in, 1024),
                               "q_moba": (w_in, 1304), "k_moba": (w_in, 1816), "v_moba": (w_in, 2328),
                               "w_out": (w_out, 0), "w_in_2": (w_in_2, 0), "w_out_2": (w_out_2, 0)}[name]
                    c0 += SW * part
                    sp.dma_start(dst, rows(src[0])[:, :, c0:c0 + SW]).then_inc(landed[slot(n)], 16)

            for name, part, m in PLAN:
                load(name, part, PLACE[name, part], m)

            def expert(e, used, base, signal):
                w1 = exp_w1[0].rearrange("e (k p) n -> p k e n", p=P)
                w2 = exp_w2[0].rearrange("e (k p) n -> p k e n", p=P)
                for j in range(4):
                    for half in range(2):
                        s = 2 * j + half
                        sp.wait_ge(used, base + s + 1)
                        c0 = FF * half + SW * j
                        sp.dma_start(ring[:, s, :, :], w1[:, :, bass.ds(e, 1), c0:c0 + SW].rearrange("p k e n -> p k (e n)"))\
                          .then_inc(signal[s], 16)
                for q in range(4):
                    s = 8 + q
                    sp.wait_ge(used, base + s + 1)
                    dst = ringf[:, s * 2048:(s + 1) * 2048].rearrange("p (k n) -> p k n", k=2)
                    sp.dma_start(dst, w2[:, 2 * q:2 * q + 2, bass.ds(e, 1), :].rearrange("p k e n -> p k (e n)"))\
                      .then_inc(signal[s], 16)

            sp.wait_ge(ada_read, len(ADA_DVE))
            sp.wait_ge(slot_used, USED0 - 4)
            with sp.Fori(0, NEXP) as e:
                expert(e, slot_used, e * SLOTS + (USED0 - SLOTS), landed)

            sp.wait_ge(r_dv, 1)
            extra = sp.value_load(extra_i[0:1, 0:1], min_val=0, max_val=15)
            with sp.If(extra > 0):
                with sp.Fori(0, extra) as o:
                    sp.wait_ge(exp_ok, o + 1)
                    sp.sem_inc(waited_sp, 1)
                    e = sp.value_load(exp_i[0:1, 0:1], min_val=0, max_val=NEXP - 1)
                    w1 = exp_w1[0].rearrange("e (k p) n -> p k e n", p=P)
                    w2 = exp_w2[0].rearrange("e (k p) n -> p k e n", p=P)
                    for s in range(8):
                        c0 = FF * (s % 2) + SW * (s // 2)
                        sp.dma_start(ring[:, s, :, :], w1[:, :, bass.ds(e, 1), c0:c0 + SW].rearrange("p k e n -> p k (e n)"))\
                          .then_inc(over_in, 16)
                    for q in range(4):
                        dst = ringf[:, (8 + q) * 2048:(9 + q) * 2048].rearrange("p (k n) -> p k n", k=2)
                        sp.dma_start(dst, w2[:, 2 * q:2 * q + 2, bass.ds(e, 1), :].rearrange("p k e n -> p k (e n)"))\
                          .then_inc(over_in, 16)
            sp.wait_ge(over_done, 1)
            for i in range(NT):
                sp.wait_ge(y_in[i], 16)
            for name, part, m in AFTER:
                load(name, part, PLACE[name, part], m)

        @block.gpsimd
        def _(pool):
            count = [0]

            def link(ins):
                count[0] += 1
                ins.then_inc(pool_c, 1)
                pool.wait_ge(pool_c, count[0])

            pool.memset(ones[:, :], 1.0).then_inc(consts, 1)
            link(pool.memset(ident[:, :], 0.0))
            pool.affine_select(out=ident[:, :], in_=ident[:, :], compare_op=ALU.not_equal, fill=1.0, base=0,
                               pattern=[[-1, P]], channel_multiplier=1).then_inc(consts, 1)
            link(pool.memset(head_mean[:, :], 0.0))
            for a in range(2):
                pool.memset(head_mean[HD * a:HD * a + HD, HD * a:HD * a + HD], 1.0 / HD).then_inc(consts, 1)
            pool.wait_ge(consts, 4)
            pool.affine_select(out=before_tok[:, :], in_=ones[:, :], compare_op=ALU.is_gt, fill=0.0, base=0,
                               pattern=[[1, P]], channel_multiplier=-1).then_inc(consts, 1)
            pool.iota(iota_c[:, :], pattern=[[1, P]], base=0, channel_multiplier=0,
                      allow_small_or_imprecise_dtypes=True).then_inc(consts, 1)
            pool.iota(tok_id, pattern=[[P, NT]], base=0, channel_multiplier=1,
                      allow_small_or_imprecise_dtypes=True).then_inc(consts, 1)
            pool.iota(junk, pattern=[[1, 1]], base=JUNK, channel_multiplier=1,
                      allow_small_or_imprecise_dtypes=True).then_inc(consts, 1)
            pool.affine_select(out=row_ok, in_=ones[:, 0:NT], compare_op=ALU.is_ge, fill=0.0, base=-(CMP_L - 1),
                               pattern=[[P, NT]], channel_multiplier=1).then_inc(consts, 1)
            pool.memset(eps, EPS).then_inc(consts, 1)
            pool.iota(work[:, 0, :], pattern=[[-1, S]], base=S - P, channel_multiplier=1,
                      allow_small_or_imprecise_dtypes=True).then_inc(dist_ok, 1)
            for h in range(HEADS):
                pool.wait_ge(scaled_ok, h + 1)
                pool.affine_select(out=bias8[:, h, :], in_=bias8[:, h, :], compare_op=ALU.is_ge, fill=NEG,
                                   base=S - P, pattern=[[-1, S]], channel_multiplier=1).then_inc(bias_ok, 1)
            for kv in range(2):
                pool.wait_ge(xt_ok, ND)
                pool.wait_ge(z_free, kv + 1)
                for g in range(2):
                    pool.dma_start(kv_turned[kv][HD * (1 - g):HD * (2 - g), :], qkT[HD * g:HD * (g + 1), 6 + kv, :])\
                        .then_inc(turned, 16)
            pool.wait_ge(c_pe, 1)
            pool.iota(cmp_bias.rearrange("p (g i h) n -> p g i h n", g=2, i=NT),
                      pattern=[[0, 2], [2 * P, NT], [0, 4], [-2 * CMP_STRIDE, CMP_N]],
                      base=-(CMP_L - 1), channel_multiplier=2, allow_small_or_imprecise_dtypes=True).then_inc(dist_ok, 1)
            for h in range(HEADS):
                pool.wait_ge(scaled_ok, HEADS + h + 1)
                part = cmp_bias.rearrange("p (g i h) n -> p g i h n", g=2, i=NT)[:, h // 4, :, h % 4, :]
                pool.affine_select(out=part, in_=part, compare_op=ALU.is_ge, fill=NEG,
                                   base=-(CMP_L - 1), pattern=[[P, NT], [-CMP_STRIDE, CMP_N]],
                                   channel_multiplier=1).then_inc(bias_ok, 1)
            pool.wait_ge(o_acc, O_MOBA)
            pool.wait_ge(s_bias, O_MOBA)
            link(pool.memset(ybuf[:, :], 0.0))
            for i in range(NT + 1):
                pool.dma_start(y_dram[i * P:(i + 1) * P, :], ybuf[:, :]).then_inc(y_zero, 16)
            pool.wait_ge(y_zero, 16 * (NT + 1))

            def fetch(sg, n):
                pool.wait_ge(sg.idx_ok, n)
                pool.sem_inc(waited_pool, 1)
                pool.indirect_dma_start(xg[:, :], None, h2_dram, bass.IndirectOffsetOnAxis(src_i[:, 0:1], 0))\
                    .then_inc(sg.got, 16)

            def put(sg, n, rows):
                pool.wait_ge(sg.y_ok, rows + 2)
                pool.wait_ge(sg.dst, n)
                pool.sem_inc(waited_pool, 1)
                pool.indirect_dma_start(y_dram, bass.IndirectOffsetOnAxis(dst_i[:, 0:1], 0), ybuf[:, :], None,
                                        bounds_check=JUNK + CAP - 1, compute_op=ALU.add)\
                    .then_inc(sg.put, 16)
                pool.wait_ge(sg.put, n * 16)
                pool.sem_inc(sg.free, 1)

            for sg in (main, over):
                pool.sem_inc(sg.free, 1)
                pool.sem_inc(sg.y_ok, 2)
            pool.wait_ge(h2_out, 16 * NT)
            fetch(main, 1)
            with pool.Fori(0, NEXP - 1) as b:
                pool.wait_ge(main.xt, b * 2 + 2)
                fetch(main, b + 2)
                put(main, b + 1, b * 2 + 2)
            put(main, NEXP, 2 * NEXP)
            pool.wait_ge(r_dv, 1)
            extra = pool.value_load(extra_i[0:1, 0:1], min_val=0, max_val=15)
            with pool.If(extra > 0):
                with pool.Fori(0, extra) as o:
                    fetch(over, o + 1)
                    put(over, o + 1, o * 2 + 2)
            pool.wait_ge(res_ok, 2 * ND)
            pool.iota(bias4[:, 0, :], pattern=[[-1, 896]], base=384, channel_multiplier=1,
                      allow_small_or_imprecise_dtypes=True).then_inc(dist_ok, 1)
            pool.wait_ge(o_acc, O_DA)
            pool.wait_ge(s_bias, S_DA)
            pool.iota(ret_dist, pattern=[[448, 2], [1, 448]], base=-384, channel_multiplier=-1,
                      allow_small_or_imprecise_dtypes=True).then_inc(dist_ok, 1)

        @block.scalar
        def _(act):
            count = [0]

            def link(ins):
                count[0] += 1
                ins.then_inc(ac, 1)
                act.wait_ge(ac, count[0])

            act.preload_act_table_set("natural_log_exp_and_others")
            act.dma_start(vec_rows, vec_rows_in).then_inc(vec_in, 16)
            act.dma_start(pos_rows.rearrange("m (k q) -> m k q", k=2),
                          nsa_cmp_pos[0].rearrange("k (m r) d -> m k (r d)", r=2)).then_inc(vec_in, 16)
            act.dma_start(x_rows, x[0].rearrange("(i p) d -> p i d", p=P)).then_inc(x_in, 16)
            act.dma_start(cw2[:, :, :], nsa_cmp_w2[0].rearrange("k p n -> p k n")).then_inc(c_in, 16)
            act.dma_start(misc[:, :], misc_in.to_broadcast([P, MISC])).then_inc(lam_in, 16)

            act.wait_ge(vec_ok, 1)
            act.activation(vecs[:, 88:96], vecs[:, 72:80], ACT.Exp, scale=-1.0).then_inc(silu_e, 1)
            for t in range(ND):
                act.wait_ge(xt_t, t + 1)
                act.activation(resT[:, t, :], bank[t % 4][:, :], ACT.Copy).then_inc(xt_ok, 1)
            act.dma_start(gate_w[:, :, :], w_in[0].rearrange("(k p) n -> p k n", p=P)[:, :, 1280:1304]).then_inc(gate_in, 16)
            act.wait_ge(consts, 10)
            act.wait_ge(xt_ok, ND)
            act.wait_ge(scaled_ok, HEADS)
            act_norm(act, link, 0)
            act.wait_ge(mod_ok, 1)
            act_shift(act, 0, mod[:, 0:8])

            def gelu_exp():
                act.wait_ge(c_dv, C_CUBE)
                act.activation(hid_t[:, :, :], hid_t[:, :, :], ACT.Exp, scale=-2.0 * 0.7978845608028654).then_inc(c_ac, 1)

            def key_roots():
                act.preload_act_table_set("natural_log_exp_and_others")
                act.wait_ge(c_dv, C_SQ)
                link(act.activation(cs[0:CMP_N, 0, 0:2], cs[0:CMP_N, 1, 0:2], ACT.Ln, bias=eps[0:CMP_N, :], scale=1.0 / HD))
                act.activation(cs[0:CMP_N, 0, 0:2], cs[0:CMP_N, 0, 0:2], ACT.Exp, scale=-0.5).then_inc(c_ac, 1)

            def cmp_exp():
                for g in range(2):
                    act.wait_ge(c_dv, C_S + g)
                    act.activation(cmp_s[:, 16 * g:16 * g + 16, :], cmp_s[:, 16 * g:16 * g + 16, :], ACT.Exp, scale=-1.0)\
                        .then_inc(c_ac, 1)

            act_project(act, link, nsa_jobs, {4: gelu_exp, 6: key_roots, 7: cmp_exp})
            for g in range(2):
                act.wait_ge(c_pe, 6 + g)
                act.activation(cmp_pT[:, g, :], bank[5 + g][:, :], ACT.Copy).then_inc(c_ac, 1)

            act_attend(act, nsa_steps)
            act_project(act, link, moba_jobs)
            act_attend(act, moba_steps)
            act_out(act, 0)

            act.wait_ge(mixT_ok, ND)
            act.dma_start(rw[:, :, :], router_w[0].rearrange("(k p) n -> p k n", p=P)).then_inc(rt_in, 16)
            act.dma_start(b1_rows, exp_b1[0]).then_inc(b_in, 16)
            act.dma_start(b2_keep, exp_b2[0]).then_inc(b_in, 16)
            act_norm(act, link, 1)
            act.wait_ge(mod_ok, 2)
            act_shift(act, 1, mod[:, 24:32])
            for i in range(NT):
                for a in range(2):
                    act.wait_ge(h2_t, 2 * i + a + 1)
                    act.activation(h2_rows[:, i, 512 * a:512 * a + 512], bank[4 + a][:, :], ACT.Copy).then_inc(h2_ok, 1)
                act.wait_ge(h2_ok, 2 * i + 2)
                act.dma_start(h2_dram[i * P:(i + 1) * P, :], h2_rows[:, i, :]).then_inc(h2_out, 16)
            act.wait_ge(lg_ok, 1)
            for i in range(NT):
                act.activation(gates[:, i, :], lg[:, i, :], ACT.Exp, bias=m8[:, i, 7:8]).then_inc(r_ac, 1)

            def sigmoids(sg, n):
                for j in range(8):
                    act.wait_ge(sg.g, n + (j + 1))
                    act.activation(s_t[:, j % 2, :], g_t[:, j % 2, :], ACT.Sigmoid, scale=ALPHA).then_inc(sg.sig, 1)

            def rows_in(sg, n):
                for a in range(2):
                    act.wait_ge(sg.xt, n + (a + 1))
                    act.activation(xgT[:, 4 * a:4 * a + 4, :], bank[5 + a][:, :].rearrange("p (k q) -> p k q", k=4),
                                   ACT.Copy).then_inc(sg.xt_ok, 1)

            def rows_done(sg, n):
                for a in range(2):
                    act.wait_ge(sg.y, n + (a + 1))
                    act.activation(ybuf[:, 512 * a:512 * a + 512], bank[3 + a][:, :], ACT.Copy,
                                   scale=meta_c[:, 2:3]).then_inc(sg.y_ok, 1)

            rows_in(main, 0)
            with act.Fori(0, NEXP - 1) as b:
                sigmoids(main, b * 8)
                rows_in(main, b * 2 + 2)
                act.wait_ge(main.free, b + 1)
                act.wait_ge(main.dst, b + 1)
                rows_done(main, b * 2)
            sigmoids(main, 8 * (NEXP - 1))
            act.wait_ge(main.free, NEXP)
            act.wait_ge(main.dst, NEXP)
            rows_done(main, 2 * (NEXP - 1))
            act.wait_ge(main.free, NEXP + 1)
            act.wait_ge(r_dv, 1)
            extra = act.value_load(extra_i[0:1, 0:1], min_val=0, max_val=15)
            with act.If(extra > 0):
                with act.Fori(0, extra) as o:
                    rows_in(over, o * 2)
                    sigmoids(over, o * 8)
                    act.wait_ge(over.dst, o + 1)
                    rows_done(over, o * 2)
                    act.wait_ge(over.free, o + 2)
            for i in range(NT):
                act.dma_start(y_rows[i], y_dram[P * i:P * (i + 1), :]).then_inc(y_in[i], 16)

            act.preload_act_table_set("natural_log_exp_and_others")
            act_norm(act, link, 2)
            act.wait_ge(g_dv, 1)
            act.activation(lam[:, 2:4], lam[:, 0:2], ACT.Exp).then_inc(g_ac, 1)
            link(act.activation(lgam[:, 2, :], lgam[:, 1, :], ACT.Exp, scale=-1.0))
            act.activation(lgam[:, 4, :], lgam[:, 2, :], ACT.Ln, bias=ones[:, 0:1]).then_inc(g_ac, 1)
            act.wait_ge(h_ok, 3 * ND)
            act_project(act, link, da_jobs)
            act.preload_act_table_set("natural_log_exp_and_others")
            act_da(act)

            def inverse_roots(n):
                act.wait_ge(rt_f, n + 1)
                link(act.activation(ms[:, :], ms[:, :], ACT.Ln, scale=1.0 / P, bias=eps))
                act.activation(ms[:, :], ms[:, :], ACT.Exp, scale=-0.5).then_inc(rt_o, 1)
            for i in range(NT):
                inverse_roots(i)
            for h in range(4):
                act.wait_ge(g_dv, 2 + h)
                act.activation(decay[:, h, :], decay[:, h, :], ACT.Exp).then_inc(g_ac, 1)
            act_project(act, link, ret_jobs)
            act.preload_act_table_set("natural_log_exp_and_others")
            for h in range(4):
                inverse_roots(NT + h)
            act_out(act, 1)
            for n, (t0, t1) in enumerate(OUT_PARTS):
                for t in range(t0, t1):
                    act.wait_ge(f_t, t + 1)
                    act.activation(rows_out[:, :, P * t:P * (t + 1)], bank[5 + t % 2][:, :].rearrange("p (i d) -> p i d", i=NT),
                                   ACT.Copy).then_inc(f_ok, 1)
                act.wait_ge(f_ok, t1)
                act.dma_start(out[0].rearrange("(i p) d -> p i d", p=P)[:, :, P * t0:P * t1],
                              rows_out[:, :, P * t0:P * t1]).then_inc(f_out, 16)
            act.wait_ge(f_out, 16 * len(OUT_PARTS))

        @block.tensor
        def _(pe):
            pe.wait_ge(vec_in, 2 * 16)
            pe.wait_ge(consts, 2)
            pe.transpose(bank[0][:, 0:86], vec_rows, ident[0:86, 0:86])
            for kv in range(2):
                mm = pe.transpose(bank[0][:, 96 + 16 * kv:96 + 16 * (kv + 1)], pos_rows[:, P * kv:P * kv + P],
                                  ident[0:CMP_L // 2, 0:CMP_L // 2])
            mm.then_inc(vec_t, 1)
            pe.wait_ge(vec_ok, 1)
            def modulate(parts):
                for ch in parts:
                    if ch in ADA_PE:
                        arrived(pe, "ada", ch)
                        for m in (2 * ch, 2 * ch + 1):
                            for k in range(ND):
                                mm = pe.matmul(bank[5][:, m:m + 1], chunk("ada", ch)[:, k, P * (m % 2):P * (m % 2) + P],
                                               vecs[:, 80 + k:81 + k], start=(k == 0), stop=(k == ND - 1))
                        mm.then_inc(slot_used, 1)
                        mm = None
                        continue
                    pe.wait_ge(ada_done, (ADA_DVE.index(ch) + 1) * ND)
                    for m in (2 * ch, 2 * ch + 1):
                        mm = pe.matmul(bank[5][:, m:m + 1], ada_sum[ch][:, P * (m % 2):P * (m % 2) + P], ones[:, 0:1],
                                       start=True, stop=True)
                if mm is not None:
                    mm.then_inc(mod_a, 1)
            pe.wait_ge(silu_ok, 1)
            modulate(ADA_PE[:1])
            pe.wait_ge(x_in, 16)
            for t in range(ND):
                if t >= 4:
                    pe.wait_ge(xt_ok, t - 3)
                for i in range(NT):
                    mm = pe.transpose(bank[t % 4][:, i * P:(i + 1) * P], x_rows[:, i, t * P:(t + 1) * P], ident[:, :])
                mm.then_inc(xt_t, 1)
            pe.wait_ge(consts, 10)
            pe.wait_ge(xt_ok, ND)
            pe_norm(pe, 0)
            modulate([*ADA_PE[1:], *ADA_DVE[:EARLY_DVE]])
            def hidden_layer():
                pe.wait_ge(c_dv, C_LAID)
                for kv in range(2):
                    arrived(pe, "cmp_w1", kv)
                    w1 = chunk("cmp_w1", kv).rearrange("p k c -> p (k c)")
                    for m in range(CMP_L // 2):
                        mm = pe.matmul(bank[5][:, 2 * CMP_N * kv:2 * CMP_N * (kv + 1)], w1[:, P * m:P * (m + 1)],
                                       cmp_in[kv][:, m, :], start=(m == 0), stop=(m == CMP_L // 2 - 1))
                    mm.then_inc(slot_used, 1)
                pe.matmul(bank[7][:, 510:512], ident[:, :], ident[:, 0:2], start=True, stop=True).then_inc(c_pe, 1)

            def keys_values():
                pe.wait_ge(c_dv, C_HID)
                pe.wait_ge(c_in, 16)
                for g in range(2):
                    pe.matmul(bank[6][0:CMP_N, HD * g:HD * g + HD], hid[:, g, :], cw2[:, 0, :], start=True, stop=True)
                for g in range(2):
                    mm = pe.matmul(bank[6][:, P + HD * g:P + HD * g + HD], hid4[:, g, :, :].rearrange("p r n -> p (r n)"),
                                   cw2[:, 1, :], start=True, stop=True)
                mm.then_inc(c_pe, 1)

            def keys_turned():
                pe.wait_ge(c_dv, C_KN)
                pe.transpose(bank[5][:, 0:CMP_N], kc_n[:, :], ident[0:CMP_N, 0:CMP_N]).then_inc(c_pe, 1)

            def cmp_scores():
                pe.wait_ge(c_dv, C_KT)
                for g in range(2):
                    for n in range(4 * NT):
                        i, hh = n // 4, n % 4
                        mm = pe.matmul(bank[5 + g][:, CMP_N * n:CMP_N * (n + 1)],
                                       qkT[HD * g:HD * g + HD, hh, i * P:(i + 1) * P], kcT[HD * g:HD * g + HD, :],
                                       start=True, stop=True)
                    mm.then_inc(c_pe, 1)

            pe_project(pe, nsa_jobs, 0, {5: hidden_layer, 6: keys_values, 7: keys_turned, 8: cmp_scores})
            pe.wait_ge(z_free, nsa_jobs[-1]["at"] + 1)
            for g in range(2):
                pe.wait_ge(c_dv, C_P + g)
                for i in range(NT):
                    n = 4 * (NT * g + i)
                    mm = pe.transpose(bank[5 + g][:, P * i:P * i + P], cmp_s[:, n:n + 4, :].rearrange("p h n -> p (h n)"),
                                      ident[:, :])
                mm.then_inc(c_pe, 1)
            for g in range(2):
                pe.wait_ge(c_ac, 5 + g)
                for i in range(NT):
                    mm = pe.matmul(bank[CMP_BANK[i]][:, SW * g:SW * g + SW], cmp_pT[:, g, P * i:P * i + P],
                                   vc_diag[:, g, :], start=True, stop=True)
                    if g == 1:
                        mm.then_inc(c_pe, 1)

            pe_attend(pe, nsa_steps, lambda: pe.wait_ge(c_dv, C_O))
            pe.wait_ge(t_ok, O_NSA)
            pe.wait_ge(o_acc, O_NSA)
            pe_project(pe, moba_jobs)
            modulate(range(EARLY, 24))
            pe.wait_ge(z_free, moba_jobs[-1]["at"] + 1)
            pe_attend(pe, moba_steps)
            pe.wait_ge(o_acc, O_MOBA)
            pe_out(pe, 0, "w_out", 0)
            pe_norm(pe, 1, [ND - 2, ND - 1])

            pe.wait_ge(b_in, 32)
            for m in range(16):
                mm = pe.transpose(bank[2][:, NEXP * m:NEXP * (m + 1)], b1_rows[:, P * m:P * (m + 1)],
                                  ident[0:NEXP, 0:NEXP])
            mm.then_inc(r_pe, 1)
            pe.wait_ge(rt_in, 16)
            for k in range(ND):
                pe.wait_ge(h_ok, ND + k + 1)
                mm = pe.matmul(bank[6][0:NEXP, :], rw[:, k, :], hT[:, k, :], start=(k == 0), stop=(k == ND - 1))
            mm.then_inc(r_pe, 1)
            pe.wait_ge(lgT_ok, 1)
            for i in range(NT):
                mm = pe.transpose(bank[7][:, NEXP * i:NEXP * (i + 1)], lgT[:, i * P:(i + 1) * P], ident[0:NEXP, 0:NEXP])
            mm.then_inc(r_pe, 1)
            for i in range(NT):
                for a in range(2):
                    if i >= 1:
                        pe.wait_ge(h2_ok, 2 * (i - 1) + a + 1)
                    for k in range(4):
                        mm = pe.transpose(bank[4 + a][:, P * k:P * k + P], hT[:, 4 * a + k, i * P:(i + 1) * P], ident[:, :])
                    mm.then_inc(h2_t, 1)
            pe.wait_ge(sel_ok, 1)
            for i in range(NT):
                for j in range(i + 1):
                    mm = pe.matmul(bank[7][:, NEXP * i:NEXP * (i + 1)], (before_tok if j == i else ones)[:, :],
                                   sel[:, j, :], start=(j == 0), stop=(j == i))
            for j in range(NT):
                mm = pe.matmul(bank[7][:, NEXP * NT:NEXP * (NT + 1)], ones[:, :], sel[:, j, :],
                               start=(j == 0), stop=(j == NT - 1))
            mm.then_inc(r_pe, 1)
            pe.wait_ge(sel_ok, 2)
            for i in range(NT):
                mm = pe.transpose(bank[6][0:NEXP, i * P:(i + 1) * P], gates[:, i, :], ident[:, :])
            mm.then_inc(r_pe, 1)

            def indices(sg, e, n):
                pe.wait_ge(sg.hot, n)
                for i in range(NT):
                    r = route[:, i, bass.ds(e, 1), :].rearrange("p e c -> p (e c)")
                    mm = pe.matmul(bank[7][:, 0:4], onehot[:, i, :], r, start=(i == 0), stop=(i == NT - 1))
                mm.then_inc(sg.idx, 1)

            def turn_rows(sg, n):
                pe.wait_ge(sg.got, n)
                for a in range(2):
                    for k in range(4):
                        mm = pe.transpose(bank[5 + a][:, P * k:P * k + P], xg[:, P * (4 * a + k):P * (4 * a + k + 1)],
                                          ident[:, :])
                    mm.then_inc(sg.xt, 1)

            def first_layer(sg, n, wait_slot, used, middle=None):
                for j in range(8):
                    if j % 2 == 0:
                        wait_slot(j)
                        wait_slot(j + 1)
                    if j >= 2:
                        pe.wait_ge(sg.l, n + (j - 1))
                    for half in range(2):
                        w = ring[:, 2 * (j // 2) + half, :, :]
                        for k in range(ND):
                            mm = pe.matmul(bank[j % 2][:, CAP * half:CAP * half + CAP], w[:, k, P * (j % 2):P * (j % 2) + P],
                                           xgT[:, k, :], start=(k == 0), stop=(k == ND - 1))
                            if used and half == 0 and k == 0 and j % 2 == 0:
                                mm.then_inc(slot_used, 1)
                        if used and half == 0 and j % 2:
                            mm.then_inc(slot_used, 1)
                    mm.then_inc(sg.u, 1)
                    if j == 0 and middle:
                        middle()

            def second_layer(sg, n, wait_slot, used):
                for k in range(ND):
                    if k % 2 == 0:
                        wait_slot(8 + k // 2)
                    pe.wait_ge(sg.act, n + (k + 1))
                    w = ringf[:, (8 + k // 2) * 2048 + D * (k % 2):(8 + k // 2) * 2048 + D * (k % 2) + D]
                    for a in range(2):
                        mm = pe.matmul(bank[3 + a][:, :], actT[:, k, :], w[:, 512 * a:512 * a + 512],
                                       start=(k == 0), stop=(k == ND - 1))
                        if used and k % 2 == 0 and a == 0:
                            mm.then_inc(slot_used, 1)
                        if k == ND - 1:
                            mm.then_inc(sg.y, 1)

            FILLS = [fill_of(MOE0 + s) for s in range(SLOTS)]

            pe.wait_ge(gT_ok, 1)
            indices(main, 0, 1)
            turn_rows(main, 16)
            with pe.Fori(0, NEXP - 1) as b:
                def wait_slot(s):
                    pe.wait_ge(landed[s], b * 16 + 16 * FILLS[s])
                pe.wait_ge(main.xt_ok, b * 2 + 2)
                first_layer(main, b * 8, wait_slot, True, lambda: indices(main, b + 1, b + 2))
                turn_rows(main, b * 16 + 32)
                pe.wait_ge(main.y_ok, b * 2 + 2)
                second_layer(main, b * 8, wait_slot, True)

            def wait_slot(s):
                pe.wait_ge(landed[s], 16 * (NEXP - 1 + FILLS[s]))
            pe.wait_ge(main.xt_ok, 2 * NEXP)
            first_layer(main, 8 * (NEXP - 1), wait_slot, True)
            pe.wait_ge(main.y_ok, 2 * NEXP)
            second_layer(main, 8 * (NEXP - 1), wait_slot, True)
            pe.wait_ge(main.y_ok, 2 * NEXP + 2)
            slots_read(pe)
            pe.wait_ge(r_dv, 1)
            extra = pe.value_load(extra_i[0:1, 0:1], min_val=0, max_val=15)
            with pe.If(extra > 0):
                with pe.Fori(0, extra) as o:
                    pe.wait_ge(exp_ok, o + 1)
                    pe.sem_inc(waited_pe, 1)
                    e = pe.value_load(exp_i[0:1, 0:1], min_val=0, max_val=NEXP - 1)
                    indices(over, e, o + 1)
                    turn_rows(over, o * 16 + 16)
                    pe.wait_ge(over.xt_ok, o * 2 + 2)
                    pe.wait_ge(over_in, o * (16 * SLOTS) + 16 * SLOTS)
                    first_layer(over, o * 8, lambda s: None, False)
                    second_layer(over, o * 8, lambda s: None, False)
                    pe.wait_ge(over.y_ok, o * 2 + 4)
            pe.matmul(bank[2][:, 510:512], ident[:, :], ident[:, 0:2], start=True, stop=True).then_inc(over_done, 1)

            pe.wait_ge(gT_ok, 1)
            for t in range(ND):
                pe.matmul(bank[t][:, :], b2_keep[:, P * t:P * (t + 1)], gatesT, start=True, stop=False)
            for i in range(NT):
                pe.wait_ge(y_in[i], 16)
                for t in range(ND):
                    mm = pe.matmul(bank[t][:, i * P:(i + 1) * P], y_rows[i][:, P * t:P * (t + 1)], ident[:, :],
                                   start=False, stop=(i == NT - 1))
                mm.then_inc(y_used, 1)

            pe.wait_ge(res_ok, ND + 1)
            pe_norm(pe, 2)
            pe_project(pe, da_jobs, 2 * ND)
            pe.wait_ge(z_free, da_jobs[-1]["at"] + 1)
            pe_da(pe)
            pe.wait_ge(o_acc, O_DA)
            pe_project(pe, ret_jobs)
            pe.wait_ge(z_free, ret_jobs[-1]["at"] + 1)

            def ret_values(h):
                for i in range(NT):
                    for kt in range(NT):
                        if i == 0:
                            pe.wait_ge(rt_d, 4 * h + kt + 1)
                        if kt == 0 and h >= 1:
                            pe.wait_ge(rt_rd, 4 * (h - 1) + i + 1)
                        mm = pe.matmul(bank[4 + i][:, 0:P], ret_s[h % 2][:, kt, i * P:(i + 1) * P],
                                       vtok[:, kt, P * h:P * (h + 1)], start=(kt == 0), stop=(kt == NT - 1))
                    mm.then_inc(rt_pv, 1)
            for h in range(4):
                half = HD * (h % 2)
                for kt in range(NT):
                    if h >= 1:
                        pe.wait_ge(rt_d, 4 * (h - 1) + kt + 1)
                    pe.matmul(bank[kt][:, :], qkT[half:half + HD, 2 + h // 2, kt * P:(kt + 1) * P],
                              qkT[half:half + HD, h // 2, :], start=True, stop=True).then_inc(rt_s, 1)
                if h >= 1:
                    ret_values(h - 1)
            ret_values(3)
            pe.wait_ge(rt_m, 4)
            pe_out(pe, 1, "w_out_2", 2 * ND)
            for t in (ND - 2, ND - 1):
                result_rows(pe, t)

        @block.vector
        def _(dve):
            count = [0]

            def link(ins):
                count[0] += 1
                ins.then_inc(dv, 1)
                dve.wait_ge(dv, count[0])

            def bc(ap, shape):
                return ap.to_broadcast(shape)

            dve.wait_ge(vec_t, 1)
            g2 = bank[0][:, 80:86].rearrange("p (a b) -> p a b", b=2)
            gv = gain.rearrange("p (a b) -> p a b", b=2)
            dve.tensor_scalar(gv[:, :, 0], g2[:, :, 0], -HD ** -0.5, None, ALU.mult)
            dve.tensor_copy(gv[:, :, 1], g2[:, :, 1])
            dve.tensor_copy(posT[:, :, :], bank[0][:, 96:96 + CMP_L].rearrange("p (k l) -> p k l", k=2))
            dve.tensor_copy(vecs[:, 0:80], bank[0][:, 0:80]).then_inc(vec_ok, 1)
            dve.wait_ge(silu_e, 1)
            link(dve.tensor_scalar(vecs[:, 88:96], vecs[:, 88:96], 1.0, None, ALU.add))
            link(dve.reciprocal(vecs[:, 88:96], vecs[:, 88:96]))
            dve.tensor_tensor(vecs[:, 80:88], vecs[:, 72:80], vecs[:, 88:96], ALU.mult).then_inc(silu_ok, 1)
            dve.wait_ge(dist_ok, 1)
            for h in range(HEADS):
                dve.tensor_scalar(bias8[:, h, :], work[:, 0, :], 2.0 ** -(h + 1), None, ALU.mult).then_inc(scaled_ok, 1)
            dve.wait_ge(silu_ok, 1)
            for m in range(EARLY_DVE * ND):
                modulate_part(dve, m)
            dve.wait_ge(mod_a, 1)
            link(dve.tensor_tensor(mod[:, 0:16], bank[5][:, 0:16], vecs[:, 0:16], ALU.add))
            dve.scalar_tensor_tensor(out=a1, in0=mod[:, 8:16], scalar=1.0, in1=vecs[:, 48:56],
                                     op0=ALU.add, op1=ALU.mult).then_inc(mod_ok, 1)
            dve.wait_ge(mod_ok, 1)
            dve_norm(dve, link, 0, a1, hs_ok)
            def lay_out():
                dve.wait_ge(turned, 4 * 16)
                for kv in range(2):
                    for r in range(2):
                        for g in range(2):
                            lanes = slice(HD * r, HD * (r + 1))
                            z = (qkT[lanes, 6 + kv, :] if r == g else kv_turned[kv][lanes, :])\
                                .rearrange("p (n l) -> p l n", l=CMP_STRIDE)[:, r:CMP_STRIDE:2, :]
                            dst = cmp_in[kv][lanes, :, CMP_N * g:CMP_N * g + CMP_N - 1]
                            dve.tensor_copy(dst[:, 0:8, :], z[:, :, 0:CMP_N - 1])
                            dve.tensor_copy(dst[:, 8:16, :], z[:, :, 1:CMP_N])
                    for g in range(2):
                        ins = dve.tensor_copy(cmp_in[kv][:, :, CMP_N * (g + 1) - 1:CMP_N * (g + 1)],
                                              posT[:, kv, :].rearrange("p (l a) -> p l a", a=1))
                ins.then_inc(c_dv, 1)

            def gelu():
                dve.wait_ge(c_pe, 1)
                link(dve.memset(hid[:, :, :], 0.0))
                for m in range(4):
                    z = bank[5][:, CMP_N * m:CMP_N * (m + 1)]
                    ins = dve.tensor_scalar(hid[:, m, 0:31], z[:, 0:31], z[:, 31:32], None, ALU.add)
                link(ins)
                link(dve.tensor_tensor(hid_t[:, :, :], hid[:, :, :], hid[:, :, :], ALU.mult))
                link(dve.tensor_scalar(hid_t[:, :, :], hid_t[:, :, :], 0.044715, 1.0, ALU.mult, ALU.add))
                link(dve.tensor_tensor(hid_t[:, :, :], hid_t[:, :, :], hid[:, :, :], ALU.mult))
                dve.tensor_scalar(hid_t[:, :, :], hid_t[:, :, :], -50.0, None, ALU.max).then_inc(c_dv, 1)
                dve.wait_ge(c_ac, 1)
                link(dve.tensor_scalar(hid_t[:, :, :], hid_t[:, :, :], 1.0, None, ALU.add))
                link(dve.reciprocal(hid_t[:, :, :], hid_t[:, :, :]))
                link(dve.tensor_tensor(hid[:, :, :], hid[:, :, :], hid_t[:, :, :], ALU.mult))
                for r in range(4):
                    ins = dve.tensor_copy(hid4[:, :, r, :], hid[:, 2:4, :])
                ins.then_inc(c_dv, 1)

            def keys_values():
                dve.wait_ge(c_pe, 2)
                kc = bank[6][0:CMP_N, 0:P]
                link(dve.tensor_copy(kc_n[:, :], kc))
                link(dve.tensor_tensor(kc_n[:, :], kc, kc_n[:, :], ALU.mult))
                dve.tensor_reduce(cs[0:CMP_N, 1, 0:2], kc_n[:, :].rearrange("p (g d) -> p g d", g=2), X, ALU.add).then_inc(c_dv, 1)
                dve.wait_ge(c_ac, 2)
                r2, m2, t2 = (cs[0:CMP_N, a, 0:2] for a in (0, 1, 2))
                link(dve.tensor_scalar(m2, m2, 1.0 / HD, EPS, ALU.mult, ALU.add))
                refine_root(dve, link, r2, m2, t2)
                for g in range(2):
                    ins = dve.tensor_scalar(kc_n[:, HD * g:HD * g + HD], kc[:, HD * g:HD * g + HD], cs[0:CMP_N, 0, g:g + 1],
                                            None, ALU.mult)
                ins.then_inc(c_dv, 1)
                link(dve.memset(vc_diag, 0.0))
                for g in range(2):
                    for h in range(4):
                        ins = dve.tensor_copy(vc_diag[CMP_N * h:CMP_N * (h + 1), g, HD * h:HD * h + HD],
                                              bank[6][CMP_N * h:CMP_N * (h + 1), P + HD * g:P + HD * g + HD])
                ins.then_inc(c_dv, 1)
                dve.wait_ge(dist_ok, 2)
                cb = cmp_bias.rearrange("p (g i h) n -> p g i h n", g=2, i=NT)
                for h in range(HEADS):
                    dve.tensor_scalar(cb[:, h // 4, :, h % 4, :], cb[:, h // 4, :, h % 4, :], 0.5 * 2.0 ** -(h + 1), None,
                                      ALU.mult).then_inc(scaled_ok, 1)
                dve.wait_ge(c_pe, 3)
                dve.tensor_scalar(kcT[:, :], bank[5][:, 0:CMP_N], gain[:, 1:2], None, ALU.mult).then_inc(c_dv, 1)

            def cmp_softmax():
                for g in range(2):
                    part = slice(16 * g, 16 * g + 16)
                    dve.wait_ge(bias_ok, HEADS + 4 * (g + 1))
                    dve.wait_ge(c_pe, 4 + g)
                    link(dve.tensor_tensor(cmp_s[:, part, :], bank[5 + g][:, :].rearrange("p (h n) -> p h n", n=CMP_N),
                                           cmp_bias[:, part, :], ALU.add))
                    link(dve.tensor_reduce(cs[:, 1, part], cmp_s[:, part, :], X, ALU.min))
                    dve.tensor_tensor(cmp_s[:, part, :], cmp_s[:, part, :], bc(cs[:, 1, part].unsqueeze(2), [P, 16, CMP_N]),
                                      ALU.subtract).then_inc(c_dv, 1)
                for g in range(2):
                    part = slice(16 * g, 16 * g + 16)
                    dve.wait_ge(c_ac, 3 + g)
                    link(dve.tensor_reduce(cs[:, 2, part], cmp_s[:, part, :], X, ALU.add))
                    link(dve.reciprocal(cs[:, 2, part], cs[:, 2, part]))
                    c4 = cs[:, 3, part].rearrange("p (i h) -> p i h", i=NT)
                    link(dve.tensor_tensor(c4, nsa_gate[:, :, 12 * g:12 * g + 12:3],
                                           cs[:, 2, part].rearrange("p (i h) -> p i h", i=NT), ALU.mult))
                    link(dve.tensor_scalar(c4[:, 0, :], c4[:, 0, :], row_ok[:, 0:1], None, ALU.mult))
                    dve.tensor_tensor(cmp_s[:, part, :], cmp_s[:, part, :], bc(cs[:, 3, part].unsqueeze(2), [P, 16, CMP_N]),
                                      ALU.mult).then_inc(c_dv, 1)

            dve_project(dve, link, nsa_jobs, {2: lay_out, 4: gelu, 6: keys_values, 8: cmp_softmax})
            for i in range(NT):
                dve.wait_ge(c_pe, 8 + i)
                dve.tensor_copy(omix[:, i, 0:512], bank[CMP_BANK[i]][:, :]).then_inc(c_dv, 1)

            dve.wait_ge(c_dv, C_O)
            dve_attend(dve, link, nsa_steps, True)
            def some_parts(first):
                for m in range(first, min(first + 6, len(ADA_DVE) * ND)):
                    modulate_part(dve, m)
            dve_project(dve, link, moba_jobs,
                        {j["at"]: lambda n=n: some_parts(EARLY_DVE * ND + O_NSA + 6 * n) for n, j in enumerate(moba_jobs)})
            dve.wait_ge(mod_a, 2)
            link(dve.tensor_tensor(mod[:, 16:48], bank[5][:, 16:48], vecs[:, 16:48], ALU.add))
            dve.scalar_tensor_tensor(out=a2, in0=mod[:, 32:40], scalar=1.0, in1=vecs[:, 56:64],
                                     op0=ALU.add, op1=ALU.mult).then_inc(mod_ok, 1)
            dve.wait_ge(mod_ok, 2)
            dve_attend(dve, link, moba_steps)
            dve_out(dve, 0, mod[:, 16:24], 0)
            dve_norm(dve, link, 1, a2, hs_ok)

            dve.wait_ge(r_pe, 1)
            bv = bank[2][:, :].rearrange("p (m e) -> p e m", e=NEXP)
            dve.tensor_copy(b1T[:, :, 0:8], bv[:, :, 0:8])
            link(dve.tensor_scalar(b1T[:, :, 8:16], bv[:, :, 8:16], 1.0, None, ALU.add))

            dve.wait_ge(r_pe, 2)
            dve.tensor_copy(lgT, bank[6][0:NEXP, :]).then_inc(lgT_ok, 1)
            dve.wait_ge(lam_in, 16)
            dve.wait_ge(r_pe, 3)
            link(dve.tensor_tensor(lg, bank[7][:, 0:NT * NEXP].rearrange("p (i e) -> p i e", e=NEXP),
                                   bc(rb_row.unsqueeze(1), [P, NT, NEXP]), ALU.add))
            for i in range(NT):
                ins = dve.max(m8[:, i, :], lg[:, i, :])
            link(ins)
            link(dve.tensor_scalar(m8[:, :, 7:8], m8[:, :, 0:1], -1.0, None, ALU.mult))
            thr = bc(m8[:, :, TOPK - 1:TOPK], [P, NT, NEXP])
            link(dve.tensor_tensor(sel, lg, thr, ALU.is_gt))
            dve.tensor_tensor(lt, lg, thr, ALU.is_equal).then_inc(lg_ok, 1)
            dve.wait_ge(lg_ok, 1)
            link(dve.tensor_reduce(m8[:, :, 6:7], sel, X, ALU.add))
            link(dve.tensor_scalar(m8[:, :, 6:7], m8[:, :, 6:7], -1.0, float(TOPK), ALU.mult, ALU.add))
            for i in range(NT):
                ins = dve.tensor_tensor_scan(posm[:, i, :], ones[:, 0:NEXP], lt[:, i, :], 0.0, ALU.mult, ALU.add)
            link(ins)
            link(dve.tensor_tensor(posm, posm, bc(m8[:, :, 6:7], [P, NT, NEXP]), ALU.is_le))
            link(dve.tensor_tensor(posm, posm, lt, ALU.mult))
            dve.tensor_tensor(sel, sel, posm, ALU.add).then_inc(sel_ok, 1)
            dve.wait_ge(sel_ok, 1)
            dve.wait_ge(r_ac, NT)
            link(dve.tensor_tensor(gates, gates, sel, ALU.mult))
            link(dve.tensor_reduce(m8[:, :, 5:6], gates, X, ALU.add))
            link(dve.reciprocal(m8[:, :, 5:6], m8[:, :, 5:6]))
            dve.tensor_tensor(gates, gates, bc(m8[:, :, 5:6], [P, NT, NEXP]), ALU.mult).then_inc(sel_ok, 1)
            dve.wait_ge(sel_ok, 2)
            tb = bc(tok_id.unsqueeze(2), [P, NT, NEXP])
            dve.tensor_copy(route[:, :, :, 0], tb)
            dve.tensor_copy(route[:, :, :, 1], tb)
            dve.tensor_copy(route[:, :, :, 2], gates)
            link(dve.memset(route[:, :, :, 3], 1.0))
            dve.wait_ge(r_pe, 4)
            link(dve.scalar_tensor_tensor(out=posm, in0=bank[7][:, 0:NT * NEXP].rearrange("p (i e) -> p i e", e=NEXP),
                                          scalar=1.0, in1=sel, op0=ALU.add, op1=ALU.mult))
            dve.tensor_scalar(posm, posm, -1.0, None, ALU.add)
            link(dve.tensor_copy(cnt[:, 0, :], bank[7][:, NT * NEXP:(NT + 1) * NEXP]))
            link(dve.tensor_scalar(cnt[:, 1, :], cnt[:, 0, :], float(CAP), None, ALU.is_gt))
            for m in (2, 3):
                link(dve.scalar_tensor_tensor(out=cnt[:, 1, :], in0=cnt[:, 0, :], scalar=float(CAP * m), in1=cnt[:, 1, :],
                                              op0=ALU.is_gt, op1=ALU.add))
            link(dve.tensor_tensor_scan(cnt[:, 2, :], ones[:, 0:NEXP], cnt[:, 1, :], 0.0, ALU.mult, ALU.add))
            dve.tensor_scalar(neg_junk, junk, -1.0, None, ALU.mult)
            dve.memset(o_cell[:, 0:1], 0.0)
            dve.tensor_copy(extra_i[0:1, 0:1], cnt[0:1, 2, NEXP - 1:NEXP]).then_inc(r_dv, 1)
            dve.wait_ge(r_dv, 1)
            dve.wait_ge(r_pe, 5)
            dve.tensor_copy(gatesT, bank[6][0:NEXP, :]).then_inc(gT_ok, 1)
            dve.wait_ge(gT_ok, 1)

            def who(sg, e, base):
                for i in range(NT):
                    ins = dve.tensor_scalar(onehot[:, i, :], base, posm[:, i, bass.ds(e, 1)], None, ALU.is_equal)
                ins.then_inc(sg.hot, 1)

            def sources(sg, n):
                dve.wait_ge(sg.idx, n)
                link_in(dve.tensor_copy(meta[:, :], bank[7][:, 0:4]))
                dve.tensor_copy(src_i[:, :], meta[:, 0:1]).then_inc(sg.idx_ok, 1)

            steps = [0]

            def link_in(ins):
                dve.drain()
                return ins

            def targets(sg):
                dve.tensor_copy(meta_c[:, :], meta[:, :])
                dve.drain()
                dve.tensor_scalar(dst_n[:, :], meta_c[:, 3:4], neg_junk, junk, ALU.mult, ALU.add)
                dve.drain()
                dve.tensor_tensor(dst_i[:, :], dst_n[:, :], meta_c[:, 1:2], ALU.add).then_inc(sg.dst, 1)

            def pair_in(sg, n, j):
                dve.wait_ge(sg.u, n + (j + 1))
                if j >= 2:
                    dve.wait_ge(sg.act, n + (j - 1))
                dve.tensor_scalar(g_t[:, j % 2, :], bank[j % 2][:, 0:CAP], b1c[:, j:j + 1], LIMIT,
                                  ALU.add, ALU.min).then_inc(sg.g, 1)
                dve.tensor_scalar(l_t[:, j % 2, :], bank[j % 2][:, CAP:2 * CAP], b1c[:, 8 + j:9 + j], 1.0 - LIMIT,
                                  ALU.add, ALU.max).then_inc(sg.l, 1)

            def pair_out(sg, n, j):
                dve.wait_ge(sg.sig, n + (j + 1))
                dve.tensor_tensor(s_t[:, j % 2, :], s_t[:, j % 2, :], g_t[:, j % 2, :], ALU.mult)
                dve.drain()
                dve.scalar_tensor_tensor(out=actT[:, j, :], in0=l_t[:, j % 2, :], scalar=1.0 + LIMIT,
                                         in1=s_t[:, j % 2, :], op0=ALU.min, op1=ALU.mult).then_inc(sg.act, 1)

            def biases(e):
                dve.tensor_copy(b1c[:, :], b1T[:, bass.ds(e, 1), :].rearrange("p e m -> p (e m)"))
                dve.drain()

            who(main, 0, iota_c[:, :])
            sources(main, 1)
            with dve.Fori(0, NEXP - 1) as b:
                biases(b)
                who(main, b + 1, iota_c[:, :])
                for j in range(8):
                    pair_in(main, b * 8, j)
                    if j >= 1:
                        pair_out(main, b * 8, j - 1)
                    if j == 3:
                        dve.wait_ge(main.y_ok, b * 2 + 2)
                        dve.wait_ge(main.free, b + 1)
                        targets(main)
                        dve.drain()
                        dve.wait_ge(main.got, b * 16 + 16)
                        sources(main, b + 2)
                pair_out(main, b * 8, 7)
            biases(NEXP - 1)
            dve.wait_ge(main.y_ok, 2 * NEXP)
            dve.wait_ge(main.free, NEXP)
            targets(main)
            for j in range(8):
                pair_in(main, 8 * (NEXP - 1), j)
                if j >= 1:
                    pair_out(main, 8 * (NEXP - 1), j - 1)
            pair_out(main, 8 * (NEXP - 1), 7)
            dve.wait_ge(main.free, NEXP + 1)
            extra = dve.value_load(extra_i[0:1, 0:1], min_val=0, max_val=15)
            with dve.If(extra > 0):
                with dve.Fori(0, extra) as o:
                    dve.wait_ge(over.free, o + 1)
                    dve.tensor_scalar(cnt[:, 3, :], cnt[:, 2, :], o_cell[:, 0:1], None, ALU.is_le)
                    dve.drain()
                    dve.tensor_reduce(o_cell[:, 1:2], cnt[:, 3, :], X, ALU.add)
                    dve.tensor_tensor(cnt[:, 3, :], cnt[:, 3, :], cnt[:, 1, :], ALU.mult)
                    dve.drain()
                    dve.tensor_reduce(o_cell[:, 2:3], cnt[:, 3, :], X, ALU.add)
                    dve.drain()
                    dve.tensor_tensor(o_cell[:, 3:4], o_cell[:, 0:1], o_cell[:, 2:3], ALU.subtract)
                    dve.drain()
                    dve.tensor_scalar(o_cell[:, 3:4], o_cell[:, 3:4], 1.0, float(CAP), ALU.add, ALU.mult)
                    dve.drain()
                    dve.tensor_scalar(iota_b[:, :], iota_c[:, :], o_cell[:, 3:4], None, ALU.add)
                    dve.tensor_scalar(o_cell[:, 0:1], o_cell[:, 0:1], 1.0, None, ALU.add)
                    dve.tensor_copy(exp_i[0:1, 0:1], o_cell[0:1, 1:2]).then_inc(exp_ok, 1)
                    dve.wait_ge(exp_ok, o + 1)
                    dve.sem_inc(waited_dve, 1)
                    e = dve.value_load(exp_i[0:1, 0:1], min_val=0, max_val=NEXP - 1)
                    biases(e)
                    who(over, e, iota_b[:, :])
                    sources(over, o + 1)
                    dve.drain()
                    targets(over)
                    for j in range(8):
                        pair_in(over, o * 8, j)
                        if j >= 1:
                            pair_out(over, o * 8, j - 1)
                    pair_out(over, o * 8, 7)
            dve.wait_ge(y_used, NT)
            for t in range(ND):
                dve.scalar_tensor_tensor(out=resT[:, t, :], in0=bank[t][:, :], scalar=mod[:, 40 + t:41 + t],
                                         in1=resT[:, t, :], op0=ALU.mult, op1=ALU.add).then_inc(res_ok, 1)

            dve.wait_ge(lam_in, 16)
            for m in range(2):
                dve.tensor_tensor_reduce(out=lam_rows[:, 2 * m, :], in0=lam_rows[:, 2 * m, :], in1=lam_rows[:, 2 * m + 1, :],
                                         scale=1.0, scalar=0.0, op0=ALU.mult, op1=ALU.add, accum_out=lam[:, m:m + 1])
            dve.tensor_scalar(subln, subln, 1.0 - LAMBDA_INIT, None, ALU.mult)
            link(dve.tensor_copy(lgam[:, 0, :], ret_decays))
            link(dve.tensor_scalar(lgam[:, 1, :], lgam[:, 0, :], -1.0, None, ALU.mult))
            dve.tensor_tensor(lgam[:, 1, :], lgam[:, 0, :], lgam[:, 1, :], ALU.max).then_inc(g_dv, 1)
            dve.wait_ge(g_ac, 2)
            link(dve.tensor_scalar(lam[:, 4:5], lam[:, 2:3], lam[:, 3:4], LAMBDA_INIT, ALU.subtract, ALU.add))
            dve.tensor_scalar(lam[:, 5:6], lam[:, 4:5], -1.0, None, ALU.mult)
            link(dve.tensor_scalar(lgam[:, 3, :], lgam[:, 2, :], 1.0, None, ALU.add))
            dve.tensor_scalar(lgam[:, 5, :], lgam[:, 3, :], 1.0, None, ALU.is_equal)
            link(dve.tensor_scalar(lgam[:, 3, :], lgam[:, 3, :], -1.0, 1e-30, ALU.add, ALU.max))
            link(dve.reciprocal(lgam[:, 3, :], lgam[:, 3, :]))
            link(dve.tensor_tensor(lgam[:, 3, :], lgam[:, 2, :], lgam[:, 3, :], ALU.mult))
            link(dve.tensor_tensor(lgam[:, 3, :], lgam[:, 3, :], lgam[:, 4, :], ALU.mult))
            link(dve.tensor_tensor(lgam[:, 5, :], lgam[:, 5, :], lgam[:, 2, :], ALU.mult))
            link(dve.tensor_tensor(lgam[:, 3, :], lgam[:, 3, :], lgam[:, 5, :], ALU.add))
            link(dve.scalar_tensor_tensor(out=lgam[:, 7, :], in0=lgam[:, 0, :], scalar=0.0, in1=lgam[:, 3, :],
                                          op0=ALU.min, op1=ALU.subtract))
            dve_norm(dve, link, 2, vecs[:, 64:72], h_ok)
            dve.wait_ge(dist_ok, 3)
            link(dve.tensor_scalar(bias4[:, 1, :], bias4[:, 0, :], -1.0, None, ALU.mult))
            link(dve.tensor_tensor(bias4[:, 0, :], bias4[:, 0, :], bias4[:, 1, :], ALU.max))
            for h in (3, 2, 1, 0):
                ins = dve.tensor_scalar(bias4[:, h, :], bias4[:, 0, :], 4.0 ** -(h + 1), None, ALU.mult)
            link(ins)
            dve_project(dve, link, da_jobs)
            dve_da(dve, link)
            dve.wait_ge(o_acc, O_DA)
            for i in range(NT):
                o4 = omix[:, i, 0:512].rearrange("p (h d) -> p h d", h=4)
                t4 = work[:, 0, :].rearrange("p (h d) -> p h d", h=4)
                link(dve.tensor_tensor(t4, o4, o4, ALU.mult))
                dve.tensor_reduce(ms[:, :], t4, X, ALU.add).then_inc(rt_f, 1)
                dve.wait_ge(rt_o, i + 1)
                link(dve.tensor_tensor(o4, o4, bc(ms[:, :].unsqueeze(2), [P, 4, P]), ALU.mult))
                link(dve.tensor_tensor(o4, o4, bc(subln.unsqueeze(1), [P, 4, P]), ALU.mult))
                link(dve.tensor_tensor(omix[:, i, 0:512], omix[:, i, 0:512], gtok[:, i, :], ALU.mult))
            def exponents():
                dve.wait_ge(dist_ok, 4)
                for h in range(4):
                    d2 = decay[:, h, :].rearrange("p (a b) -> p a b", a=2)
                    dve.tensor_scalar(d2, ret_dist, 0.0, lgam[:, 7, h:h + 1], ALU.max, ALU.mult)
                    link(dve.tensor_scalar(ret_tmp, ret_dist, 0.0, lgam[:, 7, 4 + h:5 + h], ALU.min, ALU.mult))
                    dve.tensor_tensor(d2, d2, ret_tmp, ALU.subtract).then_inc(g_dv, 1)
                    dve.wait_ge(g_dv, 2 + h)
            dve_project(dve, link, ret_jobs, {ret_jobs[3]["at"]: exponents})

            def decayed(h):
                dve.wait_ge(g_ac, 3 + h)
                for kt in range(NT):
                    dve.wait_ge(rt_s, 4 * h + kt + 1)
                    if h >= 2:
                        dve.wait_ge(rt_pv, 4 * (h - 1))
                    dve.tensor_tensor(ret_s[h % 2][:, kt, :], bank[kt][:, :],
                                      decay[:, h, 384 - P * kt:384 - P * kt + S], ALU.mult).then_inc(rt_d, 1)

            def ret_norm(h):
                oh = omix[:, :, 512 + P * h:512 + P * (h + 1)]
                for i in range(NT):
                    dve.wait_ge(rt_pv, 4 * h + i + 1)
                    dve.tensor_copy(oh[:, i, :], bank[4 + i][:, 0:P]).then_inc(rt_rd, 1)
                dve.wait_ge(rt_rd, 4 * (h + 1))
                t4 = hT[:, 0, :].rearrange("p (i d) -> p i d", i=NT)
                link(dve.tensor_tensor(t4, oh, oh, ALU.mult))
                dve.tensor_reduce(ms[:, :], t4, X, ALU.add).then_inc(rt_f, 1)
                dve.wait_ge(rt_o, NT + h + 1)
                link(dve.tensor_tensor(oh, oh, bc(ms[:, :].unsqueeze(2), [P, NT, P]), ALU.mult))
                dve.tensor_tensor(oh, oh, gtok[:, :, P * h:P * (h + 1)], ALU.mult).then_inc(rt_m, 1)
            for h in range(5):
                if h < 4:
                    decayed(h)
                if h >= 1:
                    ret_norm(h - 1)
            dve_out(dve, 1, None, 2 * ND)


_INS = ["x", "vec_rows", "misc", "ada_w", "w_in", "nsa_cmp_pos", "nsa_cmp_w1", "nsa_cmp_w2", "w_out", "router_w",
        "exp_w1", "exp_b1", "exp_w2", "exp_b2", "w_in_2", "w_out_2"]


def packed(inputs):
    import numpy as _np

    rows = [_np.asarray(inputs[n]).reshape(-1, P) for n in ("ada_b", "ln1_g", "ln2_g", "norm_w_2", "c")]
    for n in ("nsa_q_gain", "nsa_k_gain", "moba_q_gain", "moba_k_gain", "q_norm_w_2", "k_norm_w_2"):
        gain = _np.asarray(inputs[n])
        rows.append(_np.concatenate([gain, gain], axis=1))
    flat = [_np.asarray(inputs[n]) for n in ("lambda_q1_2", "lambda_k1_2", "lambda_q2_2", "lambda_k2_2", "subln_w_2",
                                             "ret_decay_fwd_2", "ret_decay_bwd_2", "router_b")]
    return {**inputs, "vec_rows": _np.concatenate(rows, axis=0), "misc": _np.concatenate(flat, axis=1)}


def kernel(**inputs):
    import numpy as _np
    import concourse.bacc as _bacc
    from concourse.bass_utils import run_bass_kernel_spmd as _run

    nc = _bacc.Bacc("TRN2", target_bir_lowering=False, num_devices=1)
    arrays, args = {}, []
    inputs = packed(inputs)
    for name in _INS:
        a = _np.ascontiguousarray(inputs[name])
        arrays[f"in_{name}_dram"] = a
        args.append(nc.dram_tensor(f"in_{name}_dram", a.shape, mybir.dt.from_np(a.dtype), kind="ExternalInput").ap())
    args.append(nc.dram_tensor("out_0_dram", (1, S, D), F32, kind="ExternalOutput").ap())
    two_block_layer(nc, *args)
    r = _run(nc, [arrays], core_ids=[0])
    return r.results[0]["out_0_dram"]
```
